# Optimizing a Trainium2 kernel written in Bass

```python
import math
import jax, jax.numpy as jnp
from jax import lax
import numpy as np

D_MODEL = 1024
BATCH = 1
SEQ = 256
DEPTH = 2
DEC_BATCH = 1
DEC_SEQ = 32
PAST_LEN = 512

CHUNK = 64
N_A = DEPTH // 2
N_B = DEPTH - N_A
HEAD_DIM = 64
N_HEADS = D_MODEL // HEAD_DIM
DECAY_LORA = 64
AAA_LORA = 64
GATE_LORA = 128
N_GROUPS = 4
EXP_PER_GROUP = 4
N_EXPERTS = N_GROUPS * EXP_PER_GROUP
EXP_HIDDEN = 256
TOP_K_INNER = 2
Q_BLOCK = 128
FORGET_BIAS = 2.0
ALPHA = (2.0 * DEPTH) ** 0.25
BETA = (8.0 * DEPTH) ** -0.25
LN_EPS = 1e-5
GN_EPS = 64e-5
F32 = jnp.float32

kernel_name = 'yoco_rwkv7_fox_hmoe_step'

def _layer_norm(z, g, b):
    zf = z.astype(F32)
    mu = jnp.mean(zf, -1, keepdims=True)
    var = jnp.mean(jnp.square(zf - mu), -1, keepdims=True)
    return ((zf - mu) * lax.rsqrt(var + LN_EPS) * g + b).astype(z.dtype)

def _adaln(c, w, b):
    m = jax.nn.silu(c) @ w + b
    return jnp.split(m[:, None, :], 6, axis=-1)

def _rwkv7(h, shift_prev, s0, mu, w_rkv, w0, w1, w2, a0, a1, a2, g1, g2, k_k, k_a, r_k,
           lnx_g, lnx_b, w_o):
    bsz, t, d = h.shape
    xx = jnp.concatenate([shift_prev[:, None, :], h[:, :-1]], axis=1) - h
    mix = lambda i: h + xx * mu[i]
    r = mix(0) @ w_rkv[0]
    k = mix(1) @ w_rkv[1]
    v = mix(2) @ w_rkv[2]
    w_log = -jax.nn.softplus(-(w0 + jnp.tanh(mix(3) @ w1) @ w2).astype(F32)) - 0.5
    decay = jnp.exp(-jnp.exp(w_log))
    a = jax.nn.sigmoid((a0 + (mix(4) @ a1) @ a2).astype(F32))
    g = jax.nn.sigmoid(mix(5) @ g1) @ g2
    heads = lambda z: z.reshape(bsz, t, N_HEADS, HEAD_DIM).astype(F32)
    kk = heads(k * k_k)
    kk = kk * lax.rsqrt(jnp.maximum(jnp.sum(kk * kk, -1, keepdims=True), 1e-24))
    k = k.astype(F32) * (1.0 + (a - 1.0) * k_a)
    r, k, v, a, decay = heads(r), heads(k), heads(v), heads(a), heads(decay)

    def step(s, inp):
        r_t, w_t, k_t, v_t, kk_t, b_t = inp
        sa = jnp.einsum('bhvk,bhk->bhv', s, -kk_t)
        s = s * w_t[:, :, None, :] + sa[..., None] * b_t[:, :, None, :] + v_t[..., None] * k_t[:, :, None, :]
        return s, jnp.einsum('bhvk,bhk->bhv', s, r_t)

    seq = tuple(jnp.swapaxes(z, 0, 1) for z in (r, decay, k, v, kk, kk * a))
    s_t, ys = lax.scan(step, s0.astype(F32), seq)
    y = jnp.swapaxes(ys, 0, 1)
    ym = jnp.mean(y, -1, keepdims=True)
    yv = jnp.mean(jnp.square(y - ym), -1, keepdims=True)
    y = ((y - ym) * lax.rsqrt(yv + GN_EPS)).reshape(bsz, t, d) * lnx_g + lnx_b
    bonus = jnp.sum(r * k * r_k, -1, keepdims=True) * v
    y = (y + bonus.reshape(bsz, t, d)) * g
    return y.astype(h.dtype) @ w_o, h[:, -1], s_t.astype(s0.dtype)

def _hmoe(h, rg_w, rg_b, re_w, re_b, wg, wu, wd):
    bsz, t, d = h.shape
    xf = h.reshape(-1, d)
    n = xf.shape[0]
    gl = (xf @ rg_w + rg_b).astype(F32)
    gsel = jnp.argmax(gl, -1)
    gprob = jnp.max(jax.nn.softmax(gl, -1), -1, keepdims=True)
    el = (xf @ re_w + re_b).astype(F32).reshape(n, N_GROUPS, EXP_PER_GROUP)
    el_sel = el[jnp.arange(n), gsel]
    top_v, top_i = lax.top_k(el_sel, TOP_K_INNER)
    top_w = jax.nn.softmax(top_v, -1) * gprob
    eid = gsel[:, None] * EXP_PER_GROUP + top_i
    comb = jnp.sum(jax.nn.one_hot(eid, N_EXPERTS, dtype=F32) * top_w[..., None], 1)
    hid = jax.nn.silu(jnp.einsum('nd,edf->nef', xf, wg)) * jnp.einsum('nd,edf->nef', xf, wu)
    hid = hid * comb[:, :, None].astype(hid.dtype)
    return jnp.einsum('nef,efd->nd', hid, wd).reshape(bsz, t, d)

def _fox_attend(q, k, v, fq, fk, q_pos, k_pos):
    s = jnp.einsum('bqhd,bkhd->bhqk', q, k).astype(F32) * (HEAD_DIM ** -0.5)
    s = s + jnp.swapaxes(fq, 1, 2)[:, :, :, None] - jnp.swapaxes(fk, 1, 2)[:, :, None, :]
    s = jnp.where(k_pos[None, :] <= q_pos[:, None], s, -jnp.inf)
    p = jax.nn.softmax(s, axis=-1)
    return jnp.einsum('bhqk,bkhd->bqhd', p.astype(v.dtype), v)

def _fox_prompt(q, k, v, logf):
    t = q.shape[1]
    fcum = jnp.cumsum(logf, axis=1)
    pos = jnp.arange(t)
    outs = []
    for i in range(t // Q_BLOCK):
        lo, hi = i * Q_BLOCK, (i + 1) * Q_BLOCK
        outs.append(_fox_attend(q[:, lo:hi], k[:, :hi], v[:, :hi], fcum[:, lo:hi], fcum[:, :hi],
                                pos[lo:hi], pos[:hi]))
    return jnp.concatenate(outs, axis=1)

def _fox_sample(q, k_new, v_new, logf_new, ck, cv, clf):
    p_len, t = ck.shape[1], q.shape[1]
    clf = clf.astype(F32)
    f_new = jnp.cumsum(logf_new, axis=1)
    suf = jnp.flip(jnp.cumsum(jnp.flip(clf, 1), 1), 1) - clf
    fk = jnp.concatenate([-suf, f_new], axis=1)
    k = jnp.concatenate([ck.astype(k_new.dtype), k_new], axis=1)
    v = jnp.concatenate([cv.astype(v_new.dtype), v_new], axis=1)
    return _fox_attend(q, k, v, f_new, fk, p_len + jnp.arange(t), jnp.arange(p_len + t))

def _trunk(x, c, shift_in, wkv_in, cache, p):
    bsz, t, d = x.shape
    shifts, states = [], []
    k_sh = v_sh = lf_sh = None
    for l in range(DEPTH):
        sh1, sc1, gt1, sh2, sc2, gt2 = _adaln(c, p['ada_w'][l], p['ada_b'][l])
        h = x * (1 + sc1) + sh1
        if l < N_A:
            y, last, s_new = _rwkv7(h, shift_in[l], wkv_in[l], p['a_mu'][l], p['a_w_rkv'][l],
                                    p['a_w0'][l], p['a_w1'][l], p['a_w2'][l], p['a_a0'][l],
                                    p['a_a1'][l], p['a_a2'][l], p['a_g1'][l], p['a_g2'][l],
                                    p['a_k_k'][l], p['a_k_a'][l], p['a_r_k'][l],
                                    p['a_lnx_g'][l], p['a_lnx_b'][l], p['a_w_o'][l])
            shifts.append(last)
            states.append(s_new)
        else:
            if k_sh is None:
                kv = x @ p['kv_w']
                k_sh = kv[..., :d].reshape(bsz, t, N_HEADS, HEAD_DIM)
                v_sh = kv[..., d:].reshape(bsz, t, N_HEADS, HEAD_DIM)
                lf_sh = jax.nn.log_sigmoid((x @ p['f_w'] + p['f_b']).astype(F32))
            j = l - N_A
            q = (h @ p['b_wq'][j]).reshape(bsz, t, N_HEADS, HEAD_DIM)
            if cache is None:
                o = _fox_prompt(q, k_sh, v_sh, lf_sh)
            else:
                o = _fox_sample(q, k_sh, v_sh, lf_sh, cache[0], cache[1], cache[2])
            y = o.reshape(bsz, t, d) @ p['b_wo'][j]
        x = _layer_norm(ALPHA * x + gt1 * y, p['ln_g'][l, 0], p['ln_b'][l, 0])
        h = x * (1 + sc2) + sh2
        y = _hmoe(h, p['rg_w'][l], p['rg_b'][l], p['re_w'][l], p['re_b'][l],
                  p['exp_wg'][l], p['exp_wu'][l], p['exp_wd'][l])
        x = _layer_norm(ALPHA * x + gt2 * y, p['ln_g'][l, 1], p['ln_b'][l, 1])
    return x, jnp.stack(shifts), jnp.stack(states), k_sh, v_sh, lf_sh.astype(x.dtype)

def setup_inputs(seed: int = 0) -> dict:
    key = jax.random.key(seed)
    it = iter(jax.random.split(key, 64))
    d, h, n = D_MODEL, N_HEADS, HEAD_DIM

    def nrm(shape, scale):
        return scale * jax.random.normal(next(it), shape, F32)

    return {
        'x_prompt': nrm((BATCH, SEQ, d), 1.0),
        'x_sample': nrm((DEC_BATCH, DEC_SEQ, d), 1.0),
        'state_shift': nrm((N_A, DEC_BATCH, d), 1.0),
        'state_wkv': nrm((N_A, DEC_BATCH, h, n, n), 0.1),
        'cache_k': nrm((DEC_BATCH, PAST_LEN, h, n), 1.0),
        'cache_v': nrm((DEC_BATCH, PAST_LEN, h, n), BETA),
        'cache_logf': jax.nn.log_sigmoid(FORGET_BIAS + nrm((DEC_BATCH, PAST_LEN, h), 1.0)),
        'c_prompt': nrm((BATCH, d), 1.0),
        'c_sample': nrm((DEC_BATCH, d), 1.0),
        'ada_w': nrm((DEPTH, d, 6 * d), 0.5 * d ** -0.5),
        'ada_b': nrm((DEPTH, 6 * d), 0.02),
        'ln_g': 1.0 + nrm((DEPTH, 2, d), 0.02),
        'ln_b': nrm((DEPTH, 2, d), 0.02),
        'a_mu': jax.random.uniform(next(it), (N_A, 6, d), F32),
        'a_w_rkv': nrm((N_A, 3, d, d), d ** -0.5) * jnp.array([1.0, 1.0, BETA], F32)[:, None, None],
        'a_w0': jax.random.uniform(next(it), (N_A, d), F32, minval=-5.0, maxval=0.0),
        'a_w1': nrm((N_A, d, DECAY_LORA), d ** -0.5),
        'a_w2': nrm((N_A, DECAY_LORA, d), 0.5 * DECAY_LORA ** -0.5),
        'a_a0': nrm((N_A, d), 0.1),
        'a_a1': nrm((N_A, d, AAA_LORA), d ** -0.5),
        'a_a2': nrm((N_A, AAA_LORA, d), 0.5 * AAA_LORA ** -0.5),
        'a_g1': nrm((N_A, d, GATE_LORA), d ** -0.5),
        'a_g2': nrm((N_A, GATE_LORA, d), GATE_LORA ** -0.5),
        'a_k_k': 0.85 + nrm((N_A, d), 0.05),
        'a_k_a': 1.0 + nrm((N_A, d), 0.05),
        'a_r_k': nrm((N_A, h, n), 0.1),
        'a_lnx_g': 1.0 + nrm((N_A, d), 0.02),
        'a_lnx_b': nrm((N_A, d), 0.02),
        'a_w_o': nrm((N_A, d, d), BETA * d ** -0.5),
        'kv_w': nrm((d, 2 * d), d ** -0.5) * jnp.concatenate([jnp.ones((d,), F32), jnp.full((d,), BETA, F32)])[None, :],
        'f_w': nrm((d, h), d ** -0.5),
        'f_b': FORGET_BIAS + nrm((h,), 0.5),
        'b_wq': nrm((N_B, d, d), d ** -0.5),
        'b_wo': nrm((N_B, d, d), BETA * d ** -0.5),
        'rg_w': nrm((DEPTH, d, N_GROUPS), d ** -0.5),
        'rg_b': nrm((DEPTH, N_GROUPS), 0.01),
        're_w': nrm((DEPTH, d, N_EXPERTS), d ** -0.5),
        're_b': nrm((DEPTH, N_EXPERTS), 0.01),
        'exp_wg': nrm((DEPTH, N_EXPERTS, d, EXP_HIDDEN), d ** -0.5),
        'exp_wu': nrm((DEPTH, N_EXPERTS, d, EXP_HIDDEN), d ** -0.5),
        'exp_wd': nrm((DEPTH, N_EXPERTS, EXP_HIDDEN, d), BETA * EXP_HIDDEN ** -0.5),
    }

def reference(x_prompt, x_sample, state_shift, state_wkv, cache_k, cache_v, cache_logf,
              c_prompt, c_sample, ada_w, ada_b, ln_g, ln_b, a_mu, a_w_rkv, a_w0, a_w1, a_w2,
              a_a0, a_a1, a_a2, a_g1, a_g2, a_k_k, a_k_a, a_r_k, a_lnx_g, a_lnx_b, a_w_o,
              kv_w, f_w, f_b, b_wq, b_wo, rg_w, rg_b, re_w, re_b, exp_wg, exp_wu, exp_wd):
    p = dict(ada_w=ada_w, ada_b=ada_b, ln_g=ln_g, ln_b=ln_b, a_mu=a_mu, a_w_rkv=a_w_rkv,
             a_w0=a_w0, a_w1=a_w1, a_w2=a_w2, a_a0=a_a0, a_a1=a_a1, a_a2=a_a2, a_g1=a_g1,
             a_g2=a_g2, a_k_k=a_k_k, a_k_a=a_k_a, a_r_k=a_r_k, a_lnx_g=a_lnx_g,
             a_lnx_b=a_lnx_b, a_w_o=a_w_o, kv_w=kv_w, f_w=f_w, f_b=f_b, b_wq=b_wq, b_wo=b_wo,
             rg_w=rg_w, rg_b=rg_b, re_w=re_w, re_b=re_b, exp_wg=exp_wg, exp_wu=exp_wu,
             exp_wd=exp_wd)
    bp = x_prompt.shape[0]
    zero_shift = jnp.zeros((N_A, bp, D_MODEL), x_prompt.dtype)
    zero_wkv = jnp.zeros((N_A, bp, N_HEADS, HEAD_DIM, HEAD_DIM), x_prompt.dtype)
    y_prompt, p_shift, p_wkv, p_k, p_v, p_logf = _trunk(x_prompt, c_prompt, zero_shift, zero_wkv, None, p)
    y_sample, s_shift, s_wkv, s_k, s_v, s_logf = _trunk(x_sample, c_sample, state_shift, state_wkv,
                                                      (cache_k, cache_v, cache_logf), p)
    return (y_prompt, y_sample, p_shift, p_wkv, p_k, p_v, p_logf, s_shift, s_wkv, s_k, s_v, s_logf)


_drawn_inputs = setup_inputs


def setup_inputs(seed=0):
    import zlib

    import numpy as np

    out = dict(_drawn_inputs(seed))
    spreads = {}
    factors = {'cache_k': 8.0,
     'cache_v': 7.89,
     'cache_logf': 8.0,
     'a_g1': 2.749,
     'a_r_k': 6.568,
     'a_lnx_g': 27.558,
     'a_lnx_b': 30.655,
     'b_wq': 3.639,
     'rg_b': 56.282,
     're_b': 64.0}
    for name, (base, spread) in spreads.items():
        noise = np.random.default_rng([zlib.crc32(name.encode()), seed]).standard_normal(out[name].shape)
        drawn = base * np.exp(spread * noise) if base else spread * noise
        out[name] = __import__('jax').numpy.asarray(drawn.astype(out[name].dtype))
    for name, factor in factors.items():
        out[name] = (out[name] * factor).astype(out[name].dtype)
    return out
```

```python
from contextlib import ExitStack

import concourse.bass as bass
import numpy as np
from concourse import mybir

F32 = mybir.dt.float32
I32 = mybir.dt.int32
ALU = mybir.AluOpType
ACT = mybir.ActivationFunctionType
AX = mybir.AxisListType.X

P = 128
D, KT = 1024, 8
TP, TS = 256, 32
T = TP + TS
NTT = 3
TOK = (128, 128, 32)
NH, HD = 16, 64
PAST = 512
NKEY = PAST + TS
NG, EPG, NE = 4, 4, 16
FH = 256
C = 64
TROWS = 320
JMAX = 8
DEST_NONE = 1000
BIG = 1e30
AHEAD = 1
ALPHA = 4.0 ** 0.25
DECAY = float(np.exp(-0.5))
LN_EPS, GN_EPS = 1e-5, 64e-5
ACOL = KT * T
GC = 2 * T
NGRP = 4
WCOL = KT * 512
ECOL = KT * 512 + 2 * D
NSLOT = 4
ADA_SLOTS = 24

VEC = {n: i * KT for i, n in enumerate(
    ["mu0", "mu1", "mu2", "mu3", "mu4", "mu5", "w0", "a0", "k_k", "k_a", "r_k", "lnx_g", "lnx_b",
     "g00", "g01", "g10", "g11", "b00", "b01", "b10", "b11", "shift"])}
VEC_C = len(VEC) * KT
VEC_ADA = VEC_C + 2 * KT
NVEC = VEC_ADA + 96
CONST = {n: i * P for i, n in enumerate(
    ["ident", "ones", "mean", "bones", "bmean", "up", "nupi", "upi", "mD", "mDT", "m16", "m32",
     "m64", "cmask", "headsel"])}
CONST["cmaskS"] = len(CONST) * P
CO_HST = CONST["cmaskS"] + TS
CO_SMALL = CO_HST + KT * P
NCONST = CO_SMALL + 4 + 16 + 16 + 16 + 8 + 4
SELW = 4 * P + P


GROUP_LINKS = 88
ATTN_LINKS = 28


class Chain:

    def __init__(self, eng, sem):
        self.eng, self.sem, self.base, self.k, self.turn, self.per = eng, sem, 0, 0, None, 0

    def did(self, ins):
        self.k += 1
        return ins.then_inc(self.sem, 1)

    def settle(self):
        at = self.base + self.k
        self.eng.wait_ge(self.sem, at if self.turn is None else self.turn * self.per + at)

    def link(self, ins):
        self.did(ins)
        self.settle()

    def enter(self, turn, per):
        self.base, self.k, self.turn, self.per = self.base + self.k, 0, turn, per

    def leave(self, turns):
        assert self.k == self.per, (self.k, self.per)
        self.base, self.k, self.turn = self.base + turns * self.per, 0, None


SET_JOBS = [("L", "V"), ("LT", "V"), ("KQ", "V"), ("D2", "A"), ("D2T", "A"), ("RB", "V"),
            ("X2", "V"), ("X2T", "V"), ("D4", "A"), ("D4T", "A"), ("RK", "V"),
            ("X4", "V"), ("X4T", "V"), ("D8", "A"), ("D8T", "A"), ("X8", "V"), ("X8T", "V"),
            ("P16", "A"), ("X16", "V"), ("X16T", "V"), ("P32", "A"), ("X32", "V"), ("X32T", "V"),
            ("P64", "A"), ("X64T", "V"),
            ("WA", "A"), ("UA", "A"), ("YA", "A"), ("SA", "V"),
            ("WB", "A"), ("UB", "A"), ("YB", "A"), ("SB", "V")]
SET_STAGES = [["L", "LT"], ["KQ"], ["D2", "D2T"], ["RB"], ["X2", "X2T"], ["D4", "D4T"], ["RK"],
              ["X4", "X4T"], ["D8", "D8T"], ["X8", "X8T"], ["P16"], ["X16", "X16T"], ["P32"],
              ["X32", "X32T"], ["P64"], ["X64T"], ["WA"], ["UA"], ["YA", "SA"], ["WB"], ["UB"],
              ["YB", "SB"]]
SAM_JOBS = [("RAW", "V"), ("D2", "A"), ("X2", "V"), ("D4", "A"), ("X4", "V"), ("D8", "A"), ("X8", "V"),
            ("P16", "A"), ("X16T", "V"), ("W", "A"), ("U", "A"), ("YS", "V")]
SAM_AFTER = {0: "RAW", 2: "D2", 4: "X2", 5: "D4", 7: "X4", 8: "D8", 9: "X8", 11: "P16", 12: "X16T",
             14: "W", 16: "U", 18: "YS"}


class Jobs:

    def __init__(self, jobs):
        self.at = {n: i for i, (n, _) in enumerate(jobs)}
        self.who = dict(jobs)
        self.nth, self.count = {}, {"A": 0, "V": 0}
        for n, e in jobs:
            self.count[e] += 1
            self.nth[n] = self.count[e]
        self.names = [n for n, _ in jobs]


SETJ, SAMJ = Jobs(SET_JOBS), Jobs(SAM_JOBS)


def build(nc, I, O):
    ctx = ExitStack()
    with ctx:
        def sb(name, shape, dt=F32):
            return ctx.enter_context(nc.sbuf_tensor(name, shape, dt))

        def sem(name):
            return ctx.enter_context(nc.semaphore(name))

        con = sb("con", [P, NCONST])
        vec = sb("vec", [P, NVEC])
        mod = sb("mod", [P, 192])
        csil = sb("csil", [P, 2 * KT])
        csig = sb("csig", [P, 2 * KT])
        small = sb("small", [P, 8])
        ring = sb("ring", [P, 2 * WCOL])
        rw = sb("rw", [P, KT * 20])
        ENT = sb("ENT", [P, NTT * 2 * 4], I32)
        SLOT = sb("SLOT", [P, NTT * 2], I32)
        TBL = sb("TBL", [C, NE * 4], I32)
        IDX = [sb(f"IDX{b}", [C, 4], I32) for b in range(2)]
        JI = [sb(f"JI{i}", [1, 24], I32) for i in range(2)]
        rn = sb("rn", [16, T])
        shrow = sb("shrow", [P, 2 * KT])
        omka = sb("omka", [P, KT])
        ARENA = 17 * ACOL
        arena = sb("arena", [P, ARENA])
        ps = ctx.enter_context(nc.psum_tensor("ps", [P, 8, 512], F32))

        ps2 = ps[:].rearrange("p b n -> p (b n)")
        hbuf = [nc.dram_tensor(f"hbuf{i}", (T, D), F32, kind="Internal").ap() for i in range(2)]
        zbuf = [nc.dram_tensor(f"zbuf{i}", (2 * T, D), F32, kind="Internal").ap() for i in range(2)]
        tbl = [nc.dram_tensor(f"tbl{i}", (NE * TROWS, 4), I32, kind="Internal").ap() for i in range(2)]

        def cut(a, n):
            assert a + n <= ARENA, (a, n, ARENA)
            return arena[:, a:a + n]

        def act_flat(i):
            return cut(i * ACOL, ACOL)

        def acts(i):
            return act_flat(i).rearrange("p (k t) -> p k t", k=KT)

        A_X, A_H, A_KK, A_XX, A_B = 0, 1, 1, 2, 2
        A_R, A_K, A_V, A_G, A_LD, A_CUM, A_Y, A_A = 3, 4, 5, 6, 7, 8, 9, 10
        X, Hh = acts(A_X), acts(A_H)

        def co(name, rows=P, cols=P):
            return con[0:rows, CONST[name]:CONST[name] + cols]

        ident, ones = co("ident"), co("ones")
        hselT = con[0:16, CO_HST:CO_HST + KT * P].rearrange("p (k m) -> p k m", k=KT)
        cs = CO_SMALL
        c4, c16 = con[:, cs:cs + 4], con[:, cs + 4:cs + 20]
        cE, c15 = con[:, cs + 20:cs + 36], con[:, cs + 36:cs + 52]
        c8 = con[:, cs + 52:cs + 60]
        eps_ln, eps_gn = con[:, cs + 60:cs + 61], con[:, cs + 61:cs + 62]

        def v(name, k):
            return vec[:, VEC[name] + k:VEC[name] + k + 1]

        def m(layer, comp, k, stream):
            c = (layer * 48 + comp * 8 + k) * 2 + stream
            return mod[:, c:c + 1]

        wslot = [ring[:, j * WCOL:(j + 1) * WCOL].rearrange("p (k n) -> p k n", k=KT) for j in range(2)]
        STREAMS = ((0, TP), (TP, T))

        lw = cut(14 * ACOL, 2048 + 3072)
        lora1 = lw[:, 0:2048].rearrange("p (k n) -> p k n", k=KT)
        w2, a2, g2 = lw[0:64, 2048:3072], lw[0:64, 3072:4096], lw[:, 4096:5120]
        lh = act_flat(8)[:, 0:3 * T].rearrange("p (s t) -> p s t", s=3)

        at = [10 * ACOL]

        def take(n):
            at[0] += n
            return cut(at[0] - n, n)

        NAMES = ["D", "DT", "X", "XT", "E16", "E32", "E64", "KQ", "RB", "RK"]
        SU = [{n: take(512) for n in NAMES} for _ in range(2)]
        SS = {n: take(128) for n in NAMES}
        base = 10 * ACOL + 2 * 512 * len(NAMES)
        SS_D, SS_X = cut(base, 256)[0:TS], cut(base + 256, 256)[0:TS]
        rx, qx, bx, kx, vx = (take(GC) for _ in range(5))
        eg, ex1 = take(GC), take(GC)
        rest = [WCOL]

        def take2(n):
            rest[0] += n
            assert rest[0] <= 2 * WCOL
            return ring[:, rest[0] - n:rest[0]]

        Vt, Bt, Kt = (take2(512) for _ in range(3))
        VtS, BtS, KtS = (take2(256) for _ in range(3))
        WU = [take2(256) for _ in range(2)]
        WUS = take2(512)
        stA, stB, stS, stSo = (take2(128) for _ in range(4))
        tst = take2(128)

        at = [7 * ACOL]
        qs, ks, vs = (take(GC) for _ in range(3))
        ck, cv = take(1024), take(1024)
        selg = take(SELW)
        vt, vtS = take(512), take(256)
        qz = take(128)
        Pp = [take(384) for _ in range(2)]
        PT = [take(384) for _ in range(2)]
        Ps, PsT, PsT5 = take(NKEY), take(512), take(128)
        sm = take(16)
        fw = take(KT * 80)
        nF = take(T)
        nFS = take(NKEY)
        clf, lfo = take(PAST), take(T)
        lft = [take(T) for _ in range(3)]
        A_Q, A_KO, A_VO, A_O = 4, 3, 5, 6

        er = cut(6 * ACOL, NSLOT * ECOL)
        ewgu = [er[:, s * ECOL:s * ECOL + 4096].rearrange("p (k n) -> p k n", k=KT) for s in range(NSLOT)]
        ewd = [er[:, s * ECOL + 4096:(s + 1) * ECOL].rearrange("p (f n) -> p f n", f=2) for s in range(NSLOT)]
        at = [2 * ACOL]
        htok = take(3 * D).rearrange("p (i d) -> p i d", i=3)
        at = [2 * ACOL]
        zin = take(6 * D).rearrange("p (i r d) -> p i r d", i=3, r=2)
        at = [5 * ACOL]
        RT = take(16 * NTT * 16).rearrange("p (a b) -> p a b", a=16)
        JT = take(8 * JMAX * 16).rearrange("p (a b) -> p a b", a=8)
        LG = take(NTT * 20).rearrange("p (i n) -> p i n", i=NTT)
        lgf = take(T)[0:20]
        assert at[0] <= 6 * ACOL
        at = [2 * ACOL]
        xsel = [take(D) for _ in range(2)]
        xselT = [take(512).rearrange("p (k c) -> p k c", k=KT) for _ in range(2)]
        ysel = [take(D) for _ in range(2)]
        hsil, hid = [take(128) for _ in range(2)], [take(128) for _ in range(2)]
        assert at[0] <= 5 * ACOL

        ZB, SQB = (10, 5, 2, 5), (11, 2, 11, 2)

        names = """consts_in x_in small_in lora_in rw_in wready0 wready1 ada_done csil_ready
            csig_done mod_ready h_ready xx_ready mix_ready tile_done tile_free shift_out lora1_done lora1_act
            lora2_done lora2_act kk_sq norm_mm norm_root bc_mm kk_ready pre_ready prod_ready kk_raw norm_inv bonus_mm bonus_done
            scaled_exp scaled st_in t_mm t_copy sm_t_mm st_out u_ready
            set_done0 set_done1 set_v0 set_v1 set_a0 set_a1 sam_done sam_v sam_a
            gn_mean gn_cent gn_sq gn_var gn_rstd gn_ready yo_ready
            z_ready xa_ready ln_mean ln_cent ln_sq ln_var ln_rstd x_ready
            lg_mm lg_act lg_t lg_ready ht_mm ht_evac hbuf_out rt_exp_in rt_exp_out mask_ready pos_mm
            jobs_ready ent_ready tbl_fill tbl_scat tbl_in e_in0 e_in1 e_in2 e_in3 idx_ready gath0 gath1 xt_mm xt_ready gu_mm silu_done
            hid_ready dn_mm y_act y_dve z_scat0 z_scat1 o_in oidx o_gath o_xt_mm o_xt o_gu o_silu o_hid o_dn
            o_yact o_ydve o_scat z_in zsum zt_mm zt_free
            xcopy attn_small f_mm f_act f_neg f_scan nf_ready kv_out stage g_in vt_mm vt_ready qz_ready
            sc_mm sc_max sc_exp sc_norm pt_mm pt_copy pv_mm pv_copy ss_mm ss_max ss_exp ss_norm
            st2_mm st2_copy sv_mm sv_copy out_done st_free y_free0 y_free1 o_free passed dve_ch act_ch pool_ch""".split()
        s = {n: sem(n) for n in names}
        ONE_AHEAD = """set_v0 set_v1 set_a0 set_a1 sam_v sam_a set_done0 set_done1 sam_done st_free pv_copy sv_copy
            sv_mm pv_mm st2_mm pt_mm y_dve y_act y_free0 y_free1 o_dn o_free o_yact o_ydve""".split()
        block = ctx.enter_context(nc.Block())
        wready = [s["wready0"], s["wready1"]]
        set_done, set_v, set_a = ([s[f"set_{k}{p}"] for p in range(2)] for k in ("done", "v", "a"))

        def constant(eng):
            eng.sem_inc(s["passed"], 1)

        def further(eng, layer):
            n = eng.value_load(JI[layer][0:1, 16:17], min_val=0, max_val=JMAX)
            before = eng.value_load(JI[0][0:1, 16:17], min_val=0, max_val=JMAX) if layer else 0
            return n, before

        @block.sync
        def _(sp):
            sp.dma_start(vec[:], I["vecs"]).then_inc(s["consts_in"], 16)
            sp.dma_start(con[:], I["consts"]).then_inc(s["consts_in"], 16)
            sp.dma_start(small[:], I["small"]).then_inc(s["small_in"], 16)
            sp.dma_start(act_flat(A_X), I["x"]).then_inc(s["x_in"], 16)
            sp.dma_start(lw, I["lora"]).then_inc(s["lora_in"], 16)

            def weights(slot, j):
                sp.dma_start(wslot[j].rearrange("p k n -> p (k n)"),
                             I["w"][bass.ds(slot, 1)].rearrange("a p n -> p (a n)")).then_inc(wready[j], 16)

            def matrix(mi):
                for j in range(2):
                    if isinstance(mi, int) and mi == 0:
                        sp.wait_ge(s["ada_done"], ADA_SLOTS - 1 + j)
                    else:
                        sp.wait_ge(s["tile_done"], (mi - 1) * 8 + 4 * (j + 1))
                        if isinstance(mi, int) and mi == 3 and j == 1:
                            sp.wait_ge(s["prod_ready"], 1)
                            sp.wait_ge(s["st_out"], 16 * 2 * NGRP)
                    weights(mi * 2 + (ADA_SLOTS + j), j)

            for j in range(2):
                weights(j, j)
            with sp.Fori(1, ADA_SLOTS // 2) as i:
                for j in range(2):
                    sp.wait_ge(s["ada_done"], i * 2 + (j - 1))
                    weights(i * 2 + j, j)
            matrix(0)
            with sp.Fori(1, 3) as i:
                matrix(i)
            matrix(3)

            def expert_dma(slot, e, layer, wsem):
                sp.dma_start(er[:, slot * ECOL:(slot + 1) * ECOL],
                             I["experts"][bass.ds(e + layer * NE, 1)].rearrange("a p n -> p (a n)"))\
                    .then_inc(wsem, 16)

            def moe_loads(layer):
                sp.dma_start(rw[:], I["rw"][layer]).then_inc(s["rw_in"], 16)
                sp.wait_ge(s["x_ready"], 2 * layer + 1)
                for e in range(NSLOT):
                    expert_dma(e, e, layer, s[f"e_in{e}"])
                with sp.Fori(1, NE // NSLOT) as i:
                    for e in range(NSLOT):
                        sp.wait_ge(s["dn_mm"], layer * NE + (i - 1) * NSLOT + (e + 1))
                        expert_dma(e, i * NSLOT + e, layer, s[f"e_in{e}"])
                sp.wait_ge(s["jobs_ready"], layer + 1)
                sp.wait_ge(s["dn_mm"], (layer + 1) * NE)
                nj, before = further(sp, layer)
                with sp.If(nj > 0):
                    with sp.Fori(0, nj) as j:
                        sp.wait_ge(s["o_dn"], before + j + AHEAD)
                        ej = sp.value_load(JI[layer][0:1, bass.ds(j, 1)], min_val=0, max_val=NE - 1)
                        expert_dma(0, ej, layer, s["o_in"])

            moe_loads(0)
            with sp.Fori(4, 8) as i:
                matrix(i)
            moe_loads(1)
            sp.wait_ge(s["x_ready"], 4)
            sp.dma_start(O["y"], act_flat(A_X)).then_inc(s["out_done"], 16)
            sp.wait_ge(s["out_done"], 16)
            sp.wait_ge(s["shift_out"], 16)
            sp.wait_ge(s["st_out"], 16 * 2 * NGRP)
            sp.wait_ge(s["kv_out"], 48)

        @block.tensor
        def _(pe):
            mm = nc.tensor.matmul

            def tr(out, in_, n):
                return nc.tensor.transpose(out, in_, ident[0:n, 0:n])

            def project(mi, rhs_at):
                for j in range(2):
                    pe.wait_ge(wready[j], (mi + (ADA_SLOTS // 2 + 1)) * 16)
                    for o in range(4):
                        tile = 4 * j + o
                        if isinstance(mi, int) and mi == 0:
                            if tile >= 4:
                                pe.wait_ge(s["tile_free"], tile - 3)
                        else:
                            pe.wait_ge(s["tile_free"], mi * 8 + (tile - 3))
                        for k in range(KT):
                            last = mm(ps[:, tile % 4, 0:T], wslot[j][:, k, o * P:(o + 1) * P], rhs_at(k),
                                      start=k == 0, stop=k == KT - 1)
                        last.then_inc(s["tile_done"], 1)

            pe.wait_ge(s["csil_ready"], 1)
            c2 = csil[:].rearrange("p (k s) -> p k s", k=KT)
            with pe.Fori(0, ADA_SLOTS // 2) as i:
                for j in range(2):
                    pe.wait_ge(wready[j], i * 16 + 16)
                    for o in range(4):
                        for k in range(KT):
                            last = mm(ps[:, 7, bass.ds(i * 16 + (8 * j + 2 * o), 2)],
                                      wslot[j][:, k, o * P:(o + 1) * P], c2[:, k, :],
                                      start=k == 0, stop=k == KT - 1)
                    last.then_inc(s["ada_done"], 1)

            pe.wait_ge(s["mix_ready"], 1)
            project(0, lambda k: cut(11 * ACOL + k * T, T))
            with pe.Fori(1, 3) as i:
                pe.wait_ge(s["mix_ready"], i + 1)
                project(i, lambda k: arena[:, bass.ds(i * ACOL + (11 * ACOL + k * T), T)])

            pe.wait_ge(s["lora_in"], 16)
            for n, (c0, c1) in enumerate(((0, 64), (64, 128), (128, 256))):
                pe.wait_ge(s["mix_ready"], 4 + n)
                for k in range(KT):
                    last = mm(ps[0:c1 - c0, 4 + n, 0:T], lora1[:, k, c0:c1], cut((11 + n) * ACOL + k * T, T),
                              start=k == 0, stop=k == KT - 1)
                last.then_inc(s["lora1_done"], 1)
            for n, (w, rows) in enumerate(((w2, 64), (a2, 64), (g2, P))):
                pe.wait_ge(s["lora1_act"], n + 1)
                for k in range(KT):
                    c = n * KT + k
                    if c >= 3:
                        pe.wait_ge(s["lora2_act"], c - 2)
                    else:
                        pe.wait_ge(s["lora1_act"], 3)
                    mm(ps[:, 4 + c % 3, 0:T], w[0:rows, k * P:(k + 1) * P], lh[0:rows, n, :],
                       start=True, stop=True).then_inc(s["lora2_done"], 1)

            pe.wait_ge(s["kk_sq"], 1)
            pe.wait_ge(s["tile_free"], 24)
            hs = co("headsel").rearrange("p (k h) -> p k h", k=KT)
            for k in range(KT):
                last = mm(ps[0:16, 0, 0:T], hs[:, k, :], acts(A_Y)[:, k, :], start=k == 0, stop=k == KT - 1)
            last.then_inc(s["norm_mm"], 1)
            pe.wait_ge(s["norm_root"], 1)
            for k in range(KT):
                if k >= 3:
                    pe.wait_ge(s["kk_ready"], k - 2)
                mm(ps[:, 1 + k % 3, 0:T], hselT[:, k, :], rn[0:16, :], start=True, stop=True)\
                    .then_inc(s["bc_mm"], 1)

            with pe.Fori(0, NGRP) as g:
                pe.wait_ge(s["scaled"], g + 1)
                for p in range(2):
                    pe.wait_ge(set_v[p], g * SETJ.count["V"] + AHEAD)
                    pe.wait_ge(set_a[p], g * SETJ.count["A"] + AHEAD)
                pe.wait_ge(s["sam_v"], g * SAMJ.count["V"] + AHEAD)
                pe.wait_ge(s["sam_a"], g * SAMJ.count["A"] + AHEAD)

                def cols(x, t, c):
                    return x[:, t * T + c * P:t * T + (c + 1) * P]

                for n, x in enumerate((vx, bx, kx)):
                    for c in range(2):
                        for t in range(2):
                            last = tr(ps[:, n, (2 * c + t) * P:(2 * c + t + 1) * P], cols(x, t, c), P)
                    last.then_inc(s["t_mm"], 1)
                for n, x in enumerate((vx, bx, kx)):
                    for t in range(2):
                        o = (n % 2) * 256 + t * P
                        last = tr(ps[0:TS, 6 + n // 2, o:o + P], x[:, t * T + TP:(t + 1) * T], P)
                last.then_inc(s["sm_t_mm"], 1)
                pe.wait_ge(s["t_copy"], g * 2 + 2)

                def wait_set(p, name):
                    who = SETJ.who[name]
                    q, per = (set_v[p], SETJ.count["V"]) if who == "V" else (set_a[p], SETJ.count["A"])
                    pe.wait_ge(q, g * per + SETJ.nth[name] + AHEAD)

                def wait_sam(name):
                    who = SAMJ.who[name]
                    q, per = (s["sam_v"], SAMJ.count["V"]) if who == "V" else (s["sam_a"], SAMJ.count["A"])
                    pe.wait_ge(q, g * per + SAMJ.nth[name] + AHEAD)

                def set_job(p, name):
                    n = SETJ.at[name]
                    bank = 3 * p + n % 3
                    if n >= 3:
                        wait_set(p, SETJ.names[n - 3])
                    B = SU[p]
                    r0 = 64 * p
                    rows = slice(r0, r0 + 64)

                    def sl(x, u):
                        return x[:, u * P:(u + 1) * P]

                    def fx(x, t, c):
                        return x[rows, t * T + c * P:t * T + (c + 1) * P]

                    def square(lhs, rhs):
                        for u in range(4):
                            last = mm(ps[:, bank, u * P:(u + 1) * P], sl(B[lhs], u), sl(B[rhs], u),
                                      start=True, stop=True)
                        return last

                    raw = {"L": (qx, bx), "LT": (bx, qx), "KQ": (kx, qx), "RB": (bx, rx), "RK": (kx, rx)}
                    if name in raw:
                        a, b = raw[name]
                        for t in range(2):
                            for c in range(2):
                                u = 2 * t + c
                                last = mm(ps[:, bank, u * P:(u + 1) * P], fx(a, t, c), fx(b, t, c),
                                          start=True, stop=True)
                    elif name in ("D2", "D2T", "D4", "D4T", "D8", "D8T"):
                        if name == "D2":
                            wait_set(p, "LT")
                        elif not name.endswith("T"):
                            wait_set(p, {"D4": "D2T", "D8": "D4T"}[name])
                        last = square("D", "DT") if name.endswith("T") else square("DT", "D")
                    elif name in ("X2", "X4", "X8"):
                        wait_set(p, "D" + name[1] + "T")
                        wait_set(p, {"X2": "LT", "X4": "X2T", "X8": "X4T"}[name])
                        last = square("DT", "X")
                    elif name in ("X2T", "X4T", "X8T"):
                        last = square("D", "XT")
                    elif name in ("P16", "P32", "P64"):
                        wait_set(p, {"P16": "X8T", "P32": "X16T", "P64": "X32T"}[name])
                        last = square("E" + name[1:], "XT")
                    elif name in ("X16", "X32"):
                        wait_set(p, "P" + name[1:])
                        last = square("D", "X")
                    elif name in ("X16T", "X32T", "X64T"):
                        if name == "X64T":
                            wait_set(p, "P64")
                        last = square("X", "D")
                    else:
                        c = "AB".index(name[1])
                        st = (None, stA)[c]
                        W, U = WU[p][:, 0:128], WU[p][:, 128:256]

                        def fr(x, t):
                            o = (2 * c + t) * P + r0
                            return x[:, o:o + 64]

                        for t in range(2):
                            u = 2 * t + c
                            if name[0] == "W":
                                if t == 0:
                                    wait_set(p, "RK")
                                    if c:
                                        wait_set(p, "SA")
                                        wait_set(p, "YA")
                                o = ps[:, bank, t * 64:(t + 1) * 64]
                                last = mm(o, sl(B["KQ"], u), fr(Vt, t), start=True, stop=c == 0)
                                if c:
                                    last = mm(o, fx(qx, t, c), st[rows, t * 64:(t + 1) * 64],
                                              start=False, stop=True)
                            elif name[0] == "U":
                                if t == 0:
                                    wait_set(p, "W" + name[1])
                                    wait_set(p, "X64T")
                                last = mm(ps[:, bank, t * 64:(t + 1) * 64], sl(B["XT"], u),
                                          W[:, t * 64:(t + 1) * 64], start=True, stop=True)
                            elif name[0] == "Y":
                                if t == 0:
                                    wait_set(p, "U" + name[1])
                                o = ps[rows, bank, t * P:(t + 1) * P]
                                mm(o, U[:, t * 64:(t + 1) * 64], sl(B["RB"], u), start=True, stop=False)
                                last = mm(o, fr(Vt, t), sl(B["RK"], u), start=False, stop=c == 0)
                                if c:
                                    last = mm(o, st[rows, t * 64:(t + 1) * 64], fx(rx, t, c),
                                              start=False, stop=True)
                            else:
                                o = ps[rows, bank, t * 64:(t + 1) * 64]
                                mm(o, fr(Bt, t), U[:, t * 64:(t + 1) * 64], start=True, stop=False)
                                last = mm(o, fr(Kt, t), fr(Vt, t), start=False, stop=True)
                    last.then_inc(set_done[p], 1)

                def sam_job(name):
                    B = SS
                    W, U = WUS[0:TS, 0:256], WUS[0:TS, 256:512]

                    def sl(x, p, t):
                        u = 2 * p + t
                        return x[0:TS, u * TS:(u + 1) * TS]

                    def fx(x, p, t):
                        return x[64 * p:64 * p + 64, t * T + TP:(t + 1) * T]

                    def fr(x, p, t):
                        return x[0:TS, t * P + 64 * p:t * P + 64 * p + 64]

                    def st(p, t):
                        return stS[64 * p:64 * p + 64, t * 64:(t + 1) * 64]

                    def square(bank, *pairs):
                        for i, (lhs, rhs) in enumerate(pairs):
                            for p in range(2):
                                for t in range(2):
                                    o = i * 128 + (2 * p + t) * TS
                                    last = mm(ps[0:TS, bank, o:o + TS], sl(B[lhs], p, t), sl(B[rhs], p, t),
                                              start=True, stop=True)
                        return last

                    for need in {"D2": ["RAW"], "X2": ["D2"], "D4": [], "X4": ["D4", "X2"], "D8": [],
                                 "X8": ["D8", "X4"], "P16": ["X8"], "X16T": ["P16"], "W": ["X16T"],
                                 "U": ["W"], "YS": ["U"]}.get(name, []):
                        wait_sam(need)
                    if name == "W":
                        pe.wait_ge(s["st_in"], g * 16 + 16)
                    constant(pe)
                    if name == "RAW":
                        for i, (a, b) in enumerate(((qx, bx), (bx, qx), (kx, qx), (bx, rx), (kx, rx))):
                            for p in range(2):
                                for t in range(2):
                                    o = i * 64 + t * TS
                                    last = mm(ps[0:TS, 6 + p, o:o + TS], fx(a, p, t), fx(b, p, t),
                                              start=True, stop=True)
                    elif name[0] == "D":
                        last = square(6, ("DT", "D"), ("D", "DT"))
                    elif name in ("X2", "X4", "X8"):
                        last = square(7, ("DT", "X"), ("D", "XT"))
                    elif name == "P16":
                        last = square(6, ("E16", "XT"))
                    elif name == "X16T":
                        last = square(7, ("X", "D"))
                    else:
                        for p in range(2):
                            for t in range(2):
                                u = (2 * p + t) * 64
                                if name == "W":
                                    o = ps[0:TS, 6 + p, t * 64:(t + 1) * 64]
                                    mm(o, sl(B["KQ"], p, t), fr(VtS, p, t), start=True, stop=False)
                                    last = mm(o, fx(qx, p, t), st(p, t), start=False, stop=True)
                                elif name == "U":
                                    last = mm(ps[0:TS, 6, u:u + 64], sl(B["XT"], p, t), W[:, u:u + 64],
                                              start=True, stop=True)
                                else:
                                    r = slice(64 * p, 64 * p + 64)
                                    o = ps[r, 6 + p, t * TS:(t + 1) * TS]
                                    mm(o, U[:, u:u + 64], sl(B["RB"], p, t), start=True, stop=False)
                                    mm(o, fr(VtS, p, t), sl(B["RK"], p, t), start=False, stop=False)
                                    mm(o, st(p, t), fx(rx, p, t), start=False, stop=True)
                                    o = ps[r, 6 + p, 64 + t * 64:128 + t * 64]
                                    mm(o, fr(BtS, p, t), U[:, u:u + 64], start=True, stop=False)
                                    last = mm(o, fr(KtS, p, t), fr(VtS, p, t), start=False, stop=True)
                    last.then_inc(s["sam_done"], 1)

                for i, stage in enumerate(SET_STAGES):
                    for p in range(2):
                        for name in stage:
                            set_job(p, name)
                    if i in SAM_AFTER:
                        sam_job(SAM_AFTER[i])

            for p in range(2):
                pe.wait_ge(set_a[p], NGRP * SETJ.count["A"] + AHEAD)
            for k in range(KT):
                pe.wait_ge(s["prod_ready"], 1)
                if k >= 4:
                    pe.wait_ge(s["bonus_done"], k - 3)
                mm(ps[:, k % 4, 0:T], co("bones"), acts(A_A)[:, k, :], start=True, stop=True)\
                    .then_inc(s["bonus_mm"], 1)
            pe.wait_ge(s["bonus_done"], KT)
            for k in range(KT):
                if k >= 4:
                    pe.wait_ge(s["gn_cent"], k - 3)
                mm(ps[:, k % 4, 0:T], co("bmean"), acts(A_Y)[:, k, :], start=True, stop=True)\
                    .then_inc(s["gn_mean"], 1)
            pe.wait_ge(s["gn_sq"], 1)
            pe.wait_ge(s["gn_cent"], KT)
            for k in range(KT):
                if k >= 4:
                    pe.wait_ge(s["gn_rstd"], k - 3)
                mm(ps[:, k % 4, 0:T], co("bmean"), acts(A_A)[:, k, :], start=True, stop=True)\
                    .then_inc(s["gn_var"], 1)
            pe.wait_ge(s["yo_ready"], 1)
            project(3, lambda k: acts(A_CUM)[:, k, :])

            def layer_norm(n):
                pe.wait_ge(s["z_ready"], n + 1)
                for k in range(KT):
                    last = mm(ps[:, 4, 0:T], co("mean"), acts(ZB[n])[:, k, :], start=k == 0, stop=k == KT - 1)
                last.then_inc(s["ln_mean"], 1)
                pe.wait_ge(s["ln_sq"], n + 1)
                for k in range(KT):
                    last = mm(ps[:, 5, 0:T], co("mean"), acts(SQB[n])[:, k, :], start=k == 0, stop=k == KT - 1)
                last.then_inc(s["ln_var"], 1)

            def moe(layer):
                pe.wait_ge(s["h_ready"], 2 * layer + 2)
                pe.wait_ge(s["rw_in"], 16 * (layer + 1))
                r = rw[:].rearrange("p (k n) -> p k n", k=KT)
                for k in range(KT):
                    last = mm(ps[0:20, 0, 0:T], r[:, k, :], Hh[:, k, :], start=k == 0, stop=k == KT - 1)
                last.then_inc(s["lg_mm"], 1)
                pe.wait_ge(s["lg_act"], layer + 1)
                for i, n in enumerate(TOK):
                    last = tr(ps[0:n, 1, i * 20:(i + 1) * 20], lgf[:, i * P:i * P + n], 20)
                last.then_inc(s["lg_t"], 1)
                for i, n in enumerate(TOK):
                    for hf in range(2):
                        for q in range(4):
                            last = tr(ps[0:n, 2 + 2 * i + hf, q * P:(q + 1) * P],
                                      Hh[:, 4 * hf + q, i * P:i * P + n], P)
                        last.then_inc(s["ht_mm"], 1)
                pe.wait_ge(s["mask_ready"], layer + 1)
                mask = RT[:, 8, :].rearrange("p (i e) -> p i e", i=3)
                for i, n in enumerate(TOK):
                    o = ps[0:n, 0, i * 16:(i + 1) * 16]
                    for i2 in range(i):
                        mm(o, ones[:, 0:n], mask[:, i2, :], start=i2 == 0, stop=False)
                    mm(o, co("up")[0:n, 0:n], mask[0:n, i, :], start=i == 0, stop=True)
                for i, n in enumerate(TOK):
                    last = mm(ps[:, 0, 48:64], ones[0:n, :], mask[0:n, i, :], start=i == 0, stop=i == 2)
                last.then_inc(s["pos_mm"], 1)

                def expert(slot, b, wait):
                    wait("in")
                    constant(pe)
                    for q in range(KT):
                        last = tr(ps[:, b, q * C:(q + 1) * C], xsel[b][0:C, q * P:(q + 1) * P], C)
                    last.then_inc(wait.xt_mm, 1)
                    wait("xt")
                    for f in range(4):
                        for k in range(KT):
                            last = mm(ps[:, 2 + b, f * C:(f + 1) * C], ewgu[slot][:, k, f * P:(f + 1) * P],
                                      xselT[b][:, k, :], start=k == 0, stop=k == KT - 1)
                    last.then_inc(wait.gu_mm, 1)
                    wait("hid")
                    for n in range(2):
                        for f in range(2):
                            last = mm(ps[0:C, 4 + 2 * b + n, :], hid[b][:, f * C:(f + 1) * C],
                                      ewd[slot][:, f, n * 512:(n + 1) * 512], start=f == 0, stop=f == 1)
                    last.then_inc(wait.dn_mm, 1)

                pe.wait_ge(s["ht_evac"], 6 * (layer + 1))
                pe.wait_ge(s["ent_ready"], layer + 1)
                with pe.Fori(0, NE // NSLOT) as i:
                    for e in range(NSLOT):
                        b = e % 2
                        n = i * NSLOT + (e + layer * NE)

                        def wait(what):
                            if what == "in":
                                pe.wait_ge(s[f"e_in{e}"], i * 16 + (layer * 64 + 16))
                                pe.wait_ge(s[f"gath{b}"], i * 32 + (layer * 128 + e // 2 * 16 + 16))
                            elif what == "xt":
                                pe.wait_ge(s["xt_ready"], n + 1)
                            else:
                                pe.wait_ge(s["hid_ready"], n + 1)
                                pe.wait_ge(s["y_dve"], n + AHEAD)
                                pe.wait_ge(s["y_act"], n + AHEAD)
                        wait.xt_mm, wait.gu_mm, wait.dn_mm = s["xt_mm"], s["gu_mm"], s["dn_mm"]
                        expert(e, b, wait)
                pe.wait_ge(s["jobs_ready"], layer + 1)
                nj, base = further(pe, layer)
                with pe.If(nj > 0):
                    with pe.Fori(0, nj) as j:
                        n = base + j

                        def wait(what):
                            if what == "in":
                                pe.wait_ge(s["o_in"], n * 16 + 16)
                                pe.wait_ge(s["o_gath"], n * 16 + 16)
                                pe.wait_ge(s["y_dve"], (layer + 1) * NE + AHEAD)
                                pe.wait_ge(s["y_act"], (layer + 1) * NE + AHEAD)
                            elif what == "xt":
                                pe.wait_ge(s["o_xt"], n + 1)
                            else:
                                pe.wait_ge(s["o_hid"], n + 1)
                                pe.wait_ge(s["o_yact"], n + AHEAD)
                                pe.wait_ge(s["o_ydve"], n + AHEAD)
                        wait.xt_mm, wait.gu_mm, wait.dn_mm = s["o_xt_mm"], s["o_gu"], s["o_dn"]
                        expert(0, 0, wait)

                pe.wait_ge(s["zsum"], layer + 1)
                for k in range(KT):
                    c = layer * KT + k
                    if c >= 4:
                        pe.wait_ge(s["zt_free"], c - 3)
                    for i, n in enumerate(TOK):
                        last = tr(ps[:, k % 4, i * P:i * P + n], zin[0:n, i, 0, k * P:(k + 1) * P], n)
                    last.then_inc(s["zt_mm"], 1)

            layer_norm(0)
            moe(0)
            layer_norm(1)

            pe.wait_ge(s["attn_small"], 32)
            pe.wait_ge(s["x_ready"], 2)
            fwv = fw.rearrange("p (k n) -> p k n", k=KT)
            for k in range(KT):
                last = mm(ps[0:80, 7, 0:T], fwv[:, k, :], X[:, k, :], start=k == 0, stop=k == KT - 1)
            last.then_inc(s["f_mm"], 1)
            pe.wait_ge(s["xcopy"], 1)
            pe.wait_ge(s["h_ready"], 3)
            with pe.Fori(0, 3) as i:
                project(i + 4, lambda k: arena[:, bass.ds(i * ACOL + k * T, T)])
            with pe.Fori(0, NGRP) as g:
                pe.wait_ge(s["stage"], g * 2 + 2)
                pe.wait_ge(s["nf_ready"], 1)
                pe.wait_ge(s["tile_free"], 56)
                pe.wait_ge(s["pv_copy"], g * 2 + AHEAD)
                pe.wait_ge(s["sv_copy"], g + AHEAD)
                for c in range(2):
                    for t in range(2):
                        tr(ps[:, 2, (2 * c + t) * P:(2 * c + t + 1) * P], vs[:, t * T + c * P:t * T + (c + 1) * P], P)
                for t in range(2):
                    last = tr(ps[0:TS, 3, t * P:(t + 1) * P], vs[:, t * T + TP:(t + 1) * T], P)
                last.then_inc(s["vt_mm"], 1)
                pe.wait_ge(s["g_in"], g * 48 + 48)

                def scores(h):
                    t, p = h // 2, h % 2
                    r = slice(64 * p, 64 * p + 64)
                    r16 = slice(64 * p, 64 * p + 16)
                    if h >= 2:
                        pe.wait_ge(s["sc_exp"], g * 4 + (h - 1))
                    b = h % 2
                    sel = selg[r16, h * P:(h + 1) * P]
                    for qt in range(2):
                        q = qs[r, t * T + qt * P:t * T + (qt + 1) * P]
                        c0 = 128 * qt
                        w = P * (qt + 1)
                        o = ps[:, b, c0:c0 + w]
                        mm(o, sel, nF[r16, 0:w], start=True, stop=False)
                        mm(ps[:, b, c0 + w - P:c0 + w], ident, co("cmask"), start=False, stop=False,
                           skip_group_check=True)
                        last = mm(o, q, ks[r, t * T:t * T + w], start=False, stop=True)
                    last.then_inc(s["sc_mm"], 1)

                def out_head(h):
                    t, p = h // 2, h % 2
                    pe.wait_ge(s["sc_norm"], g * 4 + (h + 1))
                    if h >= 1:
                        pe.wait_ge(s["pt_copy"], g * 4 + h)
                    for j in range(3):
                        last = tr(ps[:, 2, j * P:(j + 1) * P], Pp[h % 2][:, j * P:(j + 1) * P], P)
                    last.then_inc(s["pt_mm"], 1)
                    pe.wait_ge(s["pt_copy"], g * 4 + (h + 1))
                    if h == 2:
                        pe.wait_ge(s["pv_copy"], g * 2 + 1 + AHEAD)
                    f0 = t * P + 64 * p
                    r = slice(64 * p, 64 * p + 64)
                    pt = PT[h % 2]
                    mm(ps[r, 3, 0:P], vt[:, f0:f0 + 64], pt[:, 0:P], start=True, stop=True)
                    mm(ps[r, 3, P:2 * P], vt[:, f0:f0 + 64], pt[:, P:2 * P], start=True, stop=False)
                    last = mm(ps[r, 3, P:2 * P], vt[:, 256 + f0:256 + f0 + 64], pt[:, 2 * P:3 * P],
                              start=False, stop=True)
                    last.then_inc(s["pv_mm"], 1)

                scores(0)
                pe.wait_ge(s["qz_ready"], g + 1)
                sel = selg[0:16, 4 * P:5 * P]
                for bank, a, w in ((4, 0, PAST), (5, PAST, TS)):
                    for t in range(2):
                        h = slice(64 * t, 64 * t + 64)
                        o = ps[h, bank, 0:w]
                        mm(o, sel[:, h], nFS[0:16, a:a + w], start=True, stop=False)
                        if bank == 5:
                            mm(o, ident[:, h], co("cmaskS", P, TS), start=False, stop=False)
                        rhs = ck[:, t * PAST:(t + 1) * PAST] if bank == 4 else ks[:, t * T + TP:(t + 1) * T]
                        last = mm(o, qz[:, h], rhs, start=False, stop=True)
                last.then_inc(s["ss_mm"], 1)
                scores(1)
                pe.wait_ge(s["vt_ready"], g + 1)
                for h in range(4):
                    out_head(h)
                    if h < 2:
                        scores(h + 2)
                pe.wait_ge(s["ss_norm"], g + 1)
                for j in range(4):
                    tr(ps[:, 6, j * P:(j + 1) * P], Ps[:, j * P:(j + 1) * P], P)
                last = tr(ps[0:TS, 7, 0:P], Ps[:, PAST:NKEY], P)
                last.then_inc(s["st2_mm"], 1)
                pe.wait_ge(s["st2_copy"], g + 1)
                for t in range(2):
                    for p in range(2):
                        o = ps[64 * p:64 * p + 64, 7, 128 + t * TS:128 + (t + 1) * TS]
                        q0 = t * 64 + p * TS
                        f0 = t * P + 64 * p
                        for j in range(4):
                            mm(o, cv[:, j * 256 + f0:j * 256 + f0 + 64], PsT[:, j * P + q0:j * P + q0 + TS],
                               start=j == 0, stop=False)
                        last = mm(o, vtS[0:TS, f0:f0 + 64], PsT5[0:TS, q0:q0 + TS], start=False, stop=True)
                last.then_inc(s["sv_mm"], 1)
            pe.wait_ge(s["pv_copy"], 2 * NGRP + AHEAD)
            pe.wait_ge(s["sv_copy"], NGRP + AHEAD)
            project(7, lambda k: acts(A_O)[:, k, :])
            layer_norm(2)
            moe(1)
            layer_norm(3)

        @block.vector
        def _(dve):
            V = nc.vector
            ch = Chain(dve, s["dve_ch"])
            did, settle, link = ch.did, ch.settle, ch.link

            def bc(x, n, shape):
                return x.unsqueeze(n).to_broadcast(shape)

            dve.wait_ge(s["csig_done"], 1)
            V.tensor_tensor(csil[:], vec[:, VEC_C:VEC_C + 2 * KT], csig[:], ALU.mult).then_inc(s["csil_ready"], 1)
            dve.wait_ge(s["ada_done"], ADA_SLOTS)
            link(V.tensor_tensor(mod[:].rearrange("p (a s) -> p a s", s=2),
                                 ps[:, 7, 0:192].rearrange("p (a s) -> p a s", s=2),
                                 bc(vec[:, VEC_ADA:VEC_ADA + 96], 2, [P, 96, 2]), ALU.add))
            for layer in range(2):
                for comp in (1, 4):
                    c = (layer * 48 + comp * 8) * 2
                    did(V.tensor_scalar(mod[:, c:c + 16], mod[:, c:c + 16], 1.0, None, ALU.add))
            did(V.tensor_scalar(omka[:], vec[:, VEC["k_a"]:VEC["k_a"] + KT], -1.0, 1.0, ALU.mult, ALU.add))
            settle()

            def modulate(layer, comp, signal):
                for k in range(KT):
                    for st, (a, b) in enumerate(STREAMS):
                        last = V.tensor_scalar(Hh[:, k, a:b], X[:, k, a:b], m(layer, comp + 1, k, st),
                                               m(layer, comp, k, st), ALU.mult, ALU.add)
                        did(last)
                settle()
                dve.sem_inc(signal, 1)

            dve.wait_ge(s["x_in"], 16)
            modulate(0, 0, s["h_ready"])
            XX = acts(A_XX)
            for a, b in STREAMS:
                did(V.tensor_tensor(XX[:, :, a + 1:b], Hh[:, :, a:b - 1], Hh[:, :, a + 1:b], ALU.subtract))
            did(V.tensor_scalar(XX[:, :, 0:1], Hh[:, :, 0:1], -1.0, None, ALU.mult))
            did(V.tensor_tensor(XX[:, :, TP:TP + 1], vec[:, VEC["shift"]:VEC["shift"] + KT].unsqueeze(2),
                                Hh[:, :, TP:TP + 1], ALU.subtract))
            settle()
            for n in range(6):
                if n >= 3:
                    dve.wait_ge(s["tile_done"], 8 * (n - 2))
                for k in range(KT):
                    last = V.scalar_tensor_tensor(cut((11 + n % 3) * ACOL + k * T, T), XX[:, k, :],
                                                  v(f"mu{n}", k), Hh[:, k, :], ALU.mult, ALU.add)
                last.then_inc(s["mix_ready"], 1)

            R, K, Vv, G = acts(A_R), acts(A_K), acts(A_V), acts(A_G)
            LD, CUM, Y, A, KK, B = acts(A_LD), acts(A_CUM), acts(A_Y), acts(A_A), acts(A_KK), acts(A_B)
            dve.wait_ge(s["tile_free"], 24)
            dve.wait_ge(s["shift_out"], 16)
            dve.wait_ge(s["mix_ready"], 6)
            for k in range(KT):
                did(V.tensor_scalar(KK[:, k, :], K[:, k, :], v("k_k", k), None, ALU.mult))
            settle()
            dve.sem_inc(s["kk_raw"], 1)
            dve.wait_ge(s["lora2_act"], 24)
            link(V.tensor_scalar(act_flat(A_LD), act_flat(A_LD), -DECAY, None, ALU.mult))
            for k in range(KT):
                for a, b in ((0, P), (P, TP), (TP, T)):
                    did(V.tensor_tensor_scan(CUM[:, k, a:b], ones[:, 0:b - a], LD[:, k, a:b], 0.0,
                                             ALU.mult, ALU.add))
            settle()
            link(V.tensor_tensor(act_flat(A_LD), act_flat(A_CUM), act_flat(A_LD), ALU.subtract))
            dve.wait_ge(s["norm_mm"], 1)
            link(V.tensor_scalar(rn[:], ps[0:16, 0, 0:T], 1e-24, None, ALU.max))
            V.reciprocal(rn[:], rn[:]).then_inc(s["norm_inv"], 1)
            for k in range(KT):
                dve.wait_ge(s["bc_mm"], k + 1)
                did(V.tensor_tensor(KK[:, k, :], KK[:, k, :], ps[:, 1 + k % 3, 0:T], ALU.mult))
                settle()
                dve.sem_inc(s["kk_ready"], 1)
            did(V.tensor_tensor(act_flat(A_B), act_flat(A_KK), act_flat(A_A), ALU.mult))
            for k in range(KT):
                did(V.tensor_scalar(Y[:, k, :], A[:, k, :], v("k_a", k), omka[:, k:k + 1], ALU.mult, ALU.add))
            settle()
            link(V.tensor_tensor(act_flat(A_K), act_flat(A_K), act_flat(A_Y), ALU.mult))
            dve.sem_inc(s["pre_ready"], 1)

            def four(x, n=P, rows=P):
                return x[0:rows].rearrange("p (u m) -> p u m", u=4)

            def mask4(name, rows=P, cols=P):
                return bc(co(name, rows, cols), 1, [rows, 4, cols])

            with dve.Fori(0, NGRP) as g:
                ch.enter(g, GROUP_LINKS)
                for p in range(2):
                    dve.wait_ge(set_done[p], g * len(SET_JOBS) + AHEAD)
                dve.wait_ge(s["sam_done"], g * len(SAM_JOBS) + AHEAD)
                dve.wait_ge(s["scaled_exp"], g + 1)

                def src(a):
                    return arena[:, bass.ds(g * GC + a * ACOL, GC)]

                did(V.tensor_tensor(rx, src(A_R), eg, ALU.mult))
                did(V.tensor_tensor(qx, src(A_KK), qx, ALU.mult))
                did(V.tensor_tensor(bx, src(A_B), ex1, ALU.mult))
                did(V.tensor_tensor(kx, src(A_K), ex1, ALU.mult))
                did(V.tensor_copy(vx, src(A_V)))
                settle()
                dve.sem_inc(s["scaled"], 1)

                def set_evac(p, name):
                    n = SETJ.at[name]
                    bank = 3 * p + n % 3
                    B = SU[p]
                    src = four(ps[:, bank, :])
                    dve.wait_ge(set_done[p], g * len(SET_JOBS) + n + 1 + (name in ("X16", "X32")) + AHEAD)
                    if name == "L":
                        did(V.tensor_tensor(four(B["D"]), src, mask4("mD"), ALU.mult))
                        for w in ("16", "32", "64"):
                            did(V.tensor_tensor(four(B["E" + w]), src, mask4("m" + w), ALU.mult))
                        settle()
                        link(V.tensor_tensor(four(B["X"]), four(B["D"]), mask4("ident"), ALU.add))
                    elif name == "LT":
                        link(V.tensor_tensor(four(B["DT"]), src, mask4("mDT"), ALU.mult))
                        link(V.tensor_tensor(four(B["XT"]), four(B["DT"]), mask4("ident"), ALU.add))
                    elif name in ("KQ", "RB", "RK"):
                        mask = {"KQ": "up", "RB": "nupi", "RK": "upi"}[name]
                        link(V.tensor_tensor(four(B[name]), src, mask4(mask), ALU.mult))
                    elif name in ("SA", "SB"):
                        rows = slice(64 * p, 64 * p + 64)
                        c = "AB".index(name[1])
                        out = (stA, stB)[c]
                        e = [eg[rows, t * T + c * P + P - 1:t * T + c * P + P] for t in range(2)]
                        if c == 0:
                            for t in range(2):
                                h = slice(t * 64, t * 64 + 64)
                                did(V.tensor_scalar(out[rows, h], ps[rows, bank, h], e[t], None, ALU.mult))
                            settle()
                        else:
                            for t in range(2):
                                h = slice(t * 64, t * 64 + 64)
                                did(V.tensor_scalar(tst[rows, h], stA[rows, h], e[t], None, ALU.mult))
                            settle()
                            if p == 0:
                                dve.wait_ge(s["st_free"], g + AHEAD)
                            for t in range(2):
                                h = slice(t * 64, t * 64 + 64)
                                did(V.scalar_tensor_tensor(out[rows, h], ps[rows, bank, h], e[t], tst[rows, h],
                                                           ALU.mult, ALU.add))
                            settle()
                    else:
                        x = B["XT"] if name.endswith("T") else B["X"]
                        sub = name[1:3] in ("16", "32", "64")
                        link(V.tensor_tensor(x, x, ps[:, bank, :], ALU.subtract if sub else ALU.add))
                    dve.sem_inc(set_v[p], 1)

                def sam_evac(name):
                    n = SAMJ.at[name]
                    B = SS
                    dve.wait_ge(s["sam_done"], g * len(SAM_JOBS) + n + 1 + AHEAD)

                    def masked(i, out, name):
                        for p in range(2):
                            did(V.tensor_tensor(
                                out[0:TS, 64 * p:64 * p + 64].rearrange("p (u m) -> p u m", u=2),
                                ps[0:TS, 6 + p, i * 64:i * 64 + 64].rearrange("p (u m) -> p u m", u=2),
                                bc(co(name, TS, TS), 1, [TS, 2, TS]), ALU.mult))

                    if name == "RAW":
                        for i, (out, mask) in enumerate((("D", "mD"), ("DT", "mDT"), ("KQ", "up"),
                                                         ("RB", "nupi"), ("RK", "upi"))):
                            masked(i, B[out], mask)
                        masked(0, B["E16"], "m16")
                        settle()
                        link(V.tensor_tensor(SS_X.rearrange("p (u m) -> p u m", u=8),
                                             SS_D.rearrange("p (u m) -> p u m", u=8),
                                             bc(co("ident", TS, TS), 1, [TS, 8, TS]), ALU.add))
                    elif name in ("X2", "X4", "X8"):
                        link(V.tensor_tensor(SS_X, SS_X, ps[0:TS, 7, 0:256], ALU.add))
                    elif name == "X16T":
                        link(V.tensor_tensor(B["XT"][0:TS], B["XT"][0:TS], ps[0:TS, 7, 0:128], ALU.subtract))
                    else:
                        def at(p, t):
                            rows = slice(64 * p, 64 * p + 64)
                            return rows, slice(t * 64, t * 64 + 64), eg[rows, t * T + T - 1:t * T + T]

                        for p in range(2):
                            for t in range(2):
                                rows, h, e = at(p, t)
                                did(V.tensor_scalar(tst[rows, h], stS[rows, h], e, None, ALU.mult))
                                did(V.tensor_copy(arena[rows, bass.ds(g * GC + (A_Y * ACOL + t * T + TP), TS)],
                                                  ps[rows, 6 + p, t * TS:(t + 1) * TS]))
                        settle()
                        dve.wait_ge(s["st_free"], g + AHEAD)
                        for p in range(2):
                            for t in range(2):
                                rows, h, e = at(p, t)
                                did(V.scalar_tensor_tensor(stSo[rows, h], ps[rows, 6 + p, 64 + t * 64:128 + t * 64],
                                                           e, tst[rows, h], ALU.mult, ALU.add))
                        settle()
                    dve.sem_inc(s["sam_v"], 1)

                for i, stage in enumerate(SET_STAGES):
                    for p in range(2):
                        for name in stage:
                            if SETJ.who[name] == "V":
                                set_evac(p, name)
                    if SAMJ.who.get(SAM_AFTER.get(i)) == "V":
                        sam_evac(SAM_AFTER[i])
                ch.leave(NGRP)

            for p in range(2):
                dve.wait_ge(set_done[p], NGRP * len(SET_JOBS) + AHEAD)
            dve.wait_ge(s["sam_done"], NGRP * len(SAM_JOBS) + AHEAD)
            for k in range(KT):
                did(V.scalar_tensor_tensor(A[:, k, :], K[:, k, :], v("r_k", k), R[:, k, :], ALU.mult, ALU.mult))
            settle()
            dve.sem_inc(s["prod_ready"], 1)
            for k in range(KT):
                dve.wait_ge(s["bonus_mm"], k + 1)
                did(V.tensor_tensor(K[:, k, :], Vv[:, k, :], ps[:, k % 4, 0:T], ALU.mult))
                settle()
                dve.sem_inc(s["bonus_done"], 1)
            for k in range(KT):
                dve.wait_ge(s["gn_mean"], k + 1)
                did(V.tensor_tensor(Y[:, k, :], Y[:, k, :], ps[:, k % 4, 0:T], ALU.subtract))
                settle()
                dve.sem_inc(s["gn_cent"], 1)
            for k in range(KT):
                dve.wait_ge(s["gn_rstd"], k + 1)
                did(V.tensor_tensor(Y[:, k, :], Y[:, k, :], acts(A_XX)[:, k, :], ALU.mult))
            settle()
            for k in range(KT):
                did(V.tensor_scalar(Y[:, k, :], Y[:, k, :], v("lnx_g", k), v("lnx_b", k), ALU.mult, ALU.add))
            settle()
            link(V.tensor_tensor(act_flat(A_Y), act_flat(A_Y), act_flat(A_K), ALU.add))
            link(V.tensor_tensor(act_flat(A_CUM), act_flat(A_Y), act_flat(A_G), ALU.mult))
            dve.sem_inc(s["yo_ready"], 1)

            def residual(n, layer, comp, tiles, freed, first):
                Z = acts(ZB[n])
                link(V.tensor_scalar(act_flat(ZB[n]), act_flat(A_X), ALPHA, None, ALU.mult))
                for k in range(KT):
                    dve.wait_ge(tiles, first + k + 1)
                    for st, (a, b) in enumerate(STREAMS):
                        did(V.scalar_tensor_tensor(Z[:, k, a:b], ps[:, k % 4, a:b], m(layer, comp, k, st),
                                                   Z[:, k, a:b], ALU.mult, ALU.add))
                    settle()
                    dve.sem_inc(freed, 1)
                dve.sem_inc(s["z_ready"], 1)

            def layer_norm(n):
                Z, flat = acts(ZB[n]), act_flat(ZB[n])
                dve.wait_ge(s["ln_mean"], n + 1)
                link(V.tensor_tensor(Z, Z, bc(ps[:, 4, 0:T], 1, [P, KT, T]), ALU.subtract))
                dve.sem_inc(s["ln_cent"], 1)
                dve.wait_ge(s["ln_rstd"], n + 1)
                link(V.tensor_tensor(Z, Z, bc(acts(SQB[n])[:, 0, :], 1, [P, KT, T]), ALU.mult))
                for k in range(KT):
                    did(V.tensor_scalar(X[:, k, :], Z[:, k, :], v(f"g{n // 2}{n % 2}", k),
                                        v(f"b{n // 2}{n % 2}", k), ALU.mult, ALU.add))
                settle()
                dve.sem_inc(s["x_ready"], 1)

            def moe(layer):
                L3 = LG
                did(V.memset(LG, 0.0))
                did(V.memset(RT, 0.0))
                settle()
                dve.wait_ge(s["lg_t"], layer + 1)
                did(V.tensor_copy(L3[:, 0:2, :], ps[:, 1, 0:40].rearrange("p (i n) -> p i n", i=2)))
                did(V.tensor_copy(L3[0:TS, 2, :], ps[0:TS, 1, 40:60]))
                settle()
                gl = L3[:, :, 0:NG]

                def row(i, n):
                    return RT[:, i, 0:NTT * n].rearrange("p (i n) -> p i n", i=NTT)

                def col(i, j):
                    return RT[:, i, NTT * j:NTT * (j + 1)]

                def b3(x, n):
                    return bc(x, 2, [P, NTT, n])

                def first_max(vals, n, mx, eq, out, cn, vm):
                    link(V.tensor_reduce(mx, vals, AX, ALU.max))
                    link(V.tensor_tensor(eq, vals, b3(mx, n), ALU.is_equal))
                    link(V.tensor_tensor(eq, eq, bc(cn, 1, [P, NTT, n]), ALU.mult))
                    link(V.tensor_reduce(vm, eq, AX, ALU.max))
                    link(V.tensor_tensor(out, eq, b3(vm, n), ALU.is_equal))

                gmax, gsum, gp, vm, m1, m2, dm, e2, w1, w2_ = (col(15, j) for j in range(10))
                gsel, eq4, ex = row(0, NG), row(1, NG), row(2, NG)
                em, eq, oh1, oh2, pen = row(3, NE), row(4, NE), row(5, NE), row(6, NE), row(7, NG)
                mask, posE, pr = row(8, NE), row(9, NE), row(10, NE)
                first_max(gl, NG, gmax, eq4, gsel, c4, vm)
                link(V.tensor_tensor(ex, gl, b3(gmax, NG), ALU.subtract))
                dve.sem_inc(s["rt_exp_in"], 1)
                link(V.tensor_scalar(pen, gsel, BIG, -BIG, ALU.mult, ALU.add))
                for i in range(NTT):
                    did(V.tensor_tensor(em[:, i, :].rearrange("p (a b) -> p a b", a=NG),
                                        L3[:, i, NG:20].rearrange("p (a b) -> p a b", a=NG),
                                        bc(pen[:, i, :], 2, [P, NG, EPG]), ALU.add))
                settle()
                first_max(em, NE, m1, eq, oh1, c16, vm)
                link(V.scalar_tensor_tensor(em, oh1, -2 * BIG, em, ALU.mult, ALU.add))
                first_max(em, NE, m2, eq, oh2, c16, vm)
                link(V.tensor_tensor(dm, m2, m1, ALU.subtract))
                dve.sem_inc(s["rt_exp_in"], 1)
                link(V.tensor_tensor(mask, oh1, oh2, ALU.add))
                dve.sem_inc(s["mask_ready"], 1)
                dve.wait_ge(s["rt_exp_out"], 2 * layer + 2)
                link(V.tensor_reduce(gsum, ex, AX, ALU.add))
                link(V.reciprocal(gp, gsum))
                link(V.tensor_scalar(w1, e2, 1.0, None, ALU.add))
                link(V.reciprocal(w1, w1))
                link(V.tensor_tensor(w1, w1, gp, ALU.mult))
                link(V.tensor_tensor(w2_, w1, e2, ALU.mult))
                dve.wait_ge(s["pos_mm"], layer + 1)
                for i, n in enumerate(TOK):
                    did(V.tensor_tensor(posE[0:n, i, :], ps[0:n, 0, i * 16:(i + 1) * 16], cE[0:n, :], ALU.add))
                did(V.tensor_copy(JT[0:1, 7, 0:16], ps[0:1, 0, 48:64]))
                settle()
                ent = ENT[:].rearrange("p (i r w) -> p i r w", i=3, r=2)
                if layer:
                    dve.wait_ge(s["tbl_scat"], 96)
                for r, (oh, w) in enumerate(((oh1, w1), (oh2, w2_))):
                    link(V.tensor_tensor(pr, oh, posE, ALU.mult))
                    link(V.tensor_reduce(dm, pr, AX, ALU.add))
                    did(V.tensor_copy(SLOT[:, 3 * r:3 * r + 3], dm))
                    did(V.tensor_copy(ent[:, :, r, 2].bitcast(F32), w))
                    settle()
                dve.sem_inc(s["ent_ready"], 1)
                cnt = JT[0:1, 7, 0:16]
                J = [JT[0:1, i, 0:16] for i in range(3)]
                link(V.tensor_scalar(J[0], cnt, float(C), None, ALU.is_gt))
                for n in range(2, 5):
                    link(V.scalar_tensor_tensor(J[0], cnt, float(n * C), J[0], ALU.is_gt, ALU.add))
                link(V.tensor_tensor_scan(J[1], ones[0:1, 0:16], J[0], 0.0, ALU.mult, ALU.add))
                link(V.tensor_tensor(J[2], J[1], J[0], ALU.subtract))
                sh = [1, JMAX, 16]

                def je(i):
                    return JT[0:1, i, :].rearrange("p (j e) -> p j e", j=JMAX)

                jj = bc(c8[0:1, :], 2, sh)
                link(V.tensor_tensor(je(3), bc(J[2], 1, sh), jj, ALU.is_le))
                link(V.tensor_tensor(je(4), bc(J[1], 1, sh), jj, ALU.is_gt))
                link(V.tensor_tensor(je(3), je(3), je(4), ALU.mult))
                link(V.tensor_tensor(je(4), je(3), bc(c15[0:1, :], 1, sh), ALU.mult))
                link(V.tensor_reduce(JT[0:1, 6, 0:8], je(4), AX, ALU.add))
                link(V.scalar_tensor_tensor(J[2], J[2], -float(C), cE[0:1, :], ALU.mult, ALU.add))
                link(V.scalar_tensor_tensor(je(5), jj, float(C), bc(J[2], 1, sh), ALU.mult, ALU.add))
                link(V.scalar_tensor_tensor(je(5), je(5), float(C), je(3), ALU.add, ALU.mult))
                link(V.tensor_reduce(JT[0:1, 6, 8:16], je(5), AX, ALU.add))
                did(V.tensor_copy(JI[layer][0:1, 0:16], JT[0:1, 6, 0:16]))
                did(V.tensor_copy(JI[layer][0:1, 16:17], J[1][:, 15:16]))
                settle()
                dve.sem_inc(s["jobs_ready"], 1)

                def expert(b, idx, w_xt, w_gu, w_dn, w_y, g_xt, g_hid, g_y):
                    w_xt()
                    V.tensor_copy(xselT[b].rearrange("p k c -> p (k c)"), ps[:, b, :]).then_inc(g_xt, 1)
                    w_gu()
                    V.tensor_tensor(hid[b], hsil[b], ps[:, 2 + b, 2 * C:4 * C], ALU.mult).then_inc(g_hid, 1)
                    w_dn()
                    w_y()
                    V.tensor_scalar(ysel[b][0:C, 512:D], ps[0:C, 5 + 2 * b, :], idx[:, 2:3].bitcast(F32), None,
                                    ALU.mult).then_inc(g_y, 1)

                with dve.Fori(0, NE // NSLOT) as i:
                    for e in range(NSLOT):
                        b = e % 2
                        n1 = i * NSLOT + (e + layer * NE + 1)
                        expert(b, IDX[b],
                               lambda: dve.wait_ge(s["xt_mm"], n1),
                               lambda: dve.wait_ge(s["silu_done"], n1),
                               lambda: dve.wait_ge(s["dn_mm"], n1),
                               lambda: dve.wait_ge(s[f"y_free{b}"], i * 2 + (layer * 8 + e // 2) + AHEAD),
                               s["xt_ready"], s["hid_ready"], s["y_dve"])
                nj, base = further(dve, layer)
                with dve.If(nj > 0):
                    with dve.Fori(0, nj) as j:
                        n1 = base + j + 1
                        expert(0, IDX[0],
                               lambda: dve.wait_ge(s["o_xt_mm"], n1),
                               lambda: dve.wait_ge(s["o_silu"], n1),
                               lambda: dve.wait_ge(s["o_dn"], n1 + AHEAD),
                               lambda: dve.wait_ge(s["o_free"], base + j + AHEAD),
                               s["o_xt"], s["o_hid"], s["o_ydve"])
                dve.wait_ge(s["z_in"], 48 * (layer + 1))
                did(V.tensor_tensor(zin[:, 0:2, 0, :], zin[:, 0:2, 0, :], zin[:, 0:2, 1, :], ALU.add))
                did(V.tensor_tensor(zin[0:TS, 2, 0, :], zin[0:TS, 2, 0, :], zin[0:TS, 2, 1, :], ALU.add))
                settle()
                dve.sem_inc(s["zsum"], 1)

            residual(0, 0, 2, s["tile_done"], s["tile_free"], 24)
            layer_norm(0)
            modulate(0, 3, s["h_ready"])
            moe(0)
            residual(1, 0, 5, s["zt_mm"], s["zt_free"], 0)
            layer_norm(1)
            modulate(1, 0, s["h_ready"])

            dve.wait_ge(s["f_mm"], 1)
            link(V.tensor_scalar(lft[0][0:80, :], ps[0:80, 7, 0:T], small[0:80, 0:1], None, ALU.add))
            dve.sem_inc(s["f_neg"], 1)
            dve.wait_ge(s["f_act"], 1)
            link(V.scalar_tensor_tensor(lfo[0:80, :], lft[0][0:80, :], 0.0, lft[1][0:80, :], ALU.min, ALU.subtract))
            dve.sem_inc(s["f_scan"], 1)
            for a, b in ((0, P), (P, TP), (TP, T)):
                init = lft[2][0:80, P - 1:P] if a == P else 0.0
                link(V.tensor_tensor_scan(lft[2][0:80, a:b], ones[0:80, 0:b - a], lfo[0:80, a:b], init,
                                          ALU.mult, ALU.add))
            link(V.tensor_scalar(nF[0:80, :], lft[2][0:80, :], -1.0, None, ALU.mult))
            for a in range(0, PAST, P):
                init = nFS[0:16, a - 1:a] if a else 0.0
                link(V.tensor_tensor_scan(nFS[0:16, a:a + P], ones[0:16, 0:P], clf[0:16, a:a + P], init,
                                          ALU.mult, ALU.add))
            link(V.tensor_tensor(nFS[0:16, 0:PAST], nFS[0:16, 0:PAST], clf[0:16, :], ALU.subtract))
            did(V.tensor_copy(nFS[0:16, PAST:NKEY], nF[0:16, TP:T]))
            did(V.memset(qz, 0.0))
            settle()
            dve.sem_inc(s["nf_ready"], 1)
            dve.wait_ge(s["tile_free"], 56)
            with dve.Fori(0, NGRP) as g:
                ch.enter(g, ATTN_LINKS)
                dve.wait_ge(s["sv_mm"], g + AHEAD)
                dve.wait_ge(s["pv_mm"], g * 4 + AHEAD)
                link(V.tensor_scalar(qs, arena[:, bass.ds(g * GC + A_Q * ACOL, GC)], HD ** -0.5, None, ALU.mult))
                dve.sem_inc(s["stage"], 1)
                for t in range(2):
                    for p in range(2):
                        r = slice(64 * p, 64 * p + 64)
                        did(V.tensor_copy(qz[r, (2 * t + p) * TS:(2 * t + p + 1) * TS],
                                          qs[r, t * T + TP:(t + 1) * T]))
                settle()
                dve.sem_inc(s["qz_ready"], 1)

                def top(h):
                    dve.wait_ge(s["sc_mm"], g * 4 + h + 1)
                    b = h % 2
                    for qt in range(2):
                        did(V.tensor_reduce(sm[:, 2 * b + qt:2 * b + qt + 1],
                                            ps[:, b, P * qt:P * qt + P * (qt + 1)], AX, ALU.max, negate=True))
                    settle()
                    dve.sem_inc(s["sc_max"], 1)

                def norm(h):
                    dve.wait_ge(s["sc_exp"], g * 4 + h + 1)
                    b = h % 2
                    link(V.reciprocal(sm[:, 8 + 2 * b:10 + 2 * b], sm[:, 4 + 2 * b:6 + 2 * b]))
                    for qt in range(2):
                        x = Pp[b][:, P * qt:P * qt + P * (qt + 1)]
                        did(V.tensor_scalar(x, x, sm[:, 8 + 2 * b + qt:9 + 2 * b + qt], None, ALU.mult))
                    settle()
                    dve.sem_inc(s["sc_norm"], 1)

                top(0)
                dve.wait_ge(s["ss_mm"], g + 1)
                link(V.tensor_reduce(sm[:, 12:13], ps2[:, 4 * 512:4 * 512 + NKEY], AX, ALU.max, negate=True))
                dve.sem_inc(s["ss_max"], 1)
                top(1)
                norm(0)
                dve.wait_ge(s["ss_exp"], g + 1)
                link(V.reciprocal(sm[:, 14:15], sm[:, 13:14]))
                link(V.tensor_scalar(Ps, Ps, sm[:, 14:15], None, ALU.mult))
                dve.sem_inc(s["ss_norm"], 1)
                top(2)
                norm(1)
                top(3)
                norm(2)
                norm(3)
                ch.leave(NGRP)

            residual(2, 1, 2, s["tile_done"], s["tile_free"], 56)
            layer_norm(2)
            modulate(1, 3, s["h_ready"])
            moe(1)
            residual(3, 1, 5, s["zt_mm"], s["zt_free"], KT)
            layer_norm(3)

        @block.scalar
        def _(act):
            Ac = nc.scalar.activation
            ch = Chain(act, s["act_ch"])
            did, settle, link = ch.did, ch.settle, ch.link

            act.wait_ge(s["consts_in"], 32)
            Ac(csig[:], vec[:, VEC_C:VEC_C + 2 * KT], ACT.Sigmoid).then_inc(s["csig_done"], 1)
            act.wait_ge(s["h_ready"], 1)
            link(Ac(shrow[:].rearrange("p (k s) -> p k s", s=2), Hh[:, :, TP - 1:T:TS], ACT.Copy))
            act.dma_start(O["shift"], shrow[:]).then_inc(s["shift_out"], 16)

            def empty(mi, dst):
                for k in range(KT):
                    act.wait_ge(s["tile_done"], mi * 8 + k + 1)
                    Ac(dst(k), ps[:, k % 4, 0:T], ACT.Copy).then_inc(s["tile_free"], 1)

            with act.Fori(0, 3) as i:
                empty(i, lambda k: arena[:, bass.ds(i * ACOL + (A_R * ACOL + k * T), T)])
            for n, (f, rows) in enumerate(((ACT.Tanh, 64), (ACT.Copy, 64), (ACT.Sigmoid, P))):
                act.wait_ge(s["lora1_done"], n + 1)
                Ac(lh[0:rows, n, :], ps[0:rows, 4 + n, 0:T], f).then_inc(s["lora1_act"], 1)
            for n, dst in enumerate((A_LD, A_A, A_G)):
                for k in range(KT):
                    c = n * KT + k
                    act.wait_ge(s["lora2_done"], c + 1)
                    out, in_ = acts(dst)[:, k, :], ps[:, 4 + c % 3, 0:T]
                    if n < 2:
                        ins = Ac(out, in_, ACT.Sigmoid, bias=v(("w0", "a0")[n], k))
                    else:
                        ins = Ac(out, in_, ACT.Copy)
                    ins.then_inc(s["lora2_act"], 1)
            act.wait_ge(s["kk_raw"], 1)
            Ac(act_flat(A_Y), act_flat(A_KK), ACT.Square).then_inc(s["kk_sq"], 1)
            act.wait_ge(s["norm_inv"], 1)
            Ac(rn[:], rn[:], ACT.Sqrt).then_inc(s["norm_root"], 1)

            act.wait_ge(s["pre_ready"], 1)
            with act.Fori(0, NGRP) as g:
                for p in range(2):
                    act.wait_ge(set_v[p], g * SETJ.count["V"] + AHEAD)
                    act.wait_ge(set_done[p], g * len(SET_JOBS) + AHEAD)
                act.wait_ge(s["sam_v"], g * SAMJ.count["V"] + AHEAD)
                act.wait_ge(s["sam_done"], g * len(SAM_JOBS) + AHEAD)
                cum = arena[:, bass.ds(g * GC + A_CUM * ACOL, GC)]
                Ac(eg, cum, ACT.Exp)
                Ac(ex1, cum, ACT.Exp, scale=-1.0)
                Ac(qx, arena[:, bass.ds(g * GC + A_LD * ACOL, GC)], ACT.Exp).then_inc(s["scaled_exp"], 1)
                for n, (dst, sg) in enumerate(((Vt, 1.0), (Bt, -1.0), (Kt, 1.0))):
                    act.wait_ge(s["t_mm"], g * 3 + n + 1)
                    last = Ac(dst, ps[:, n, :], ACT.Copy, scale=sg)
                last.then_inc(s["t_copy"], 1)
                act.wait_ge(s["sm_t_mm"], g + 1)
                Ac(VtS[0:TS], ps[0:TS, 6, 0:256], ACT.Copy)
                Ac(BtS[0:TS], ps[0:TS, 6, 256:512], ACT.Copy, scale=-1.0)
                Ac(KtS[0:TS], ps[0:TS, 7, 0:256], ACT.Copy).then_inc(s["t_copy"], 1)

                def set_evac(p, name):
                    n = SETJ.at[name]
                    bank = 3 * p + n % 3
                    B = SU[p]
                    both = name in ("D2", "D4", "D8")
                    act.wait_ge(set_done[p], g * len(SET_JOBS) + n + 1 + both + AHEAD)
                    rows = slice(64 * p, 64 * p + 64)
                    if name[0] in "DP":
                        dst, src = B["DT" if name.endswith("T") else "D"], ps[:, bank, :]
                    elif name[0] in "WU":
                        o = 128 * (name[0] == "U")
                        dst, src = WU[p][:, o:o + 128], ps[:, bank, 0:128]
                    else:
                        c = "AB".index(name[1])
                        for t in range(2):
                            last = Ac(arena[rows, bass.ds(g * GC + (A_Y * ACOL + t * T + c * P), P)],
                                      ps[rows, bank, t * P:(t + 1) * P], ACT.Copy)
                        last.then_inc(set_a[p], 1)
                        return
                    Ac(dst, src, ACT.Copy).then_inc(set_a[p], 1)

                def sam_evac(name):
                    act.wait_ge(s["sam_done"], g * len(SAM_JOBS) + SAMJ.at[name] + 1 + AHEAD)
                    if name[0] == "D":
                        last = Ac(SS_D, ps[0:TS, 6, 0:256], ACT.Copy)
                    elif name == "P16":
                        last = Ac(SS["D"][0:TS], ps[0:TS, 6, 0:128], ACT.Copy)
                    elif name == "W":
                        for p in range(2):
                            last = Ac(WUS[0:TS, 128 * p:128 * (p + 1)], ps[0:TS, 6 + p, 0:128], ACT.Copy)
                    else:
                        last = Ac(WUS[0:TS, 256:512], ps[0:TS, 6, 0:256], ACT.Copy)
                    last.then_inc(s["sam_a"], 1)

                for i, stage in enumerate(SET_STAGES):
                    for p in range(2):
                        for name in stage:
                            if SETJ.who[name] == "A":
                                set_evac(p, name)
                    if SAMJ.who.get(SAM_AFTER.get(i)) == "A":
                        sam_evac(SAM_AFTER[i])

            act.wait_ge(s["gn_cent"], KT)
            Ac(act_flat(A_A), act_flat(A_Y), ACT.Square).then_inc(s["gn_sq"], 1)
            for k in range(KT):
                act.wait_ge(s["gn_var"], k + 1)
                r = acts(A_XX)[:, k, :]
                link(Ac(r, ps[:, k % 4, 0:T], ACT.Ln, bias=eps_gn))
                Ac(r, r, ACT.Exp, scale=-0.5).then_inc(s["gn_rstd"], 1)

            def layer_norm(n):
                act.wait_ge(s["ln_cent"], n + 1)
                Ac(act_flat(SQB[n]), act_flat(ZB[n]), ACT.Square).then_inc(s["ln_sq"], 1)
                act.wait_ge(s["ln_var"], n + 1)
                r = acts(SQB[n])[:, 0, :]
                link(Ac(r, ps[:, 5, 0:T], ACT.Ln, bias=eps_ln))
                Ac(r, r, ACT.Exp, scale=-0.5).then_inc(s["ln_rstd"], 1)

            def moe(layer):
                act.wait_ge(s["lg_mm"], layer + 1)
                act.wait_ge(s["small_in"], 16)
                Ac(lgf, ps[0:20, 0, 0:T], ACT.Identity, bias=small[0:20, 1 + layer:2 + layer])\
                    .then_inc(s["lg_act"], 1)
                for i, n in enumerate(TOK):
                    for hf in range(2):
                        act.wait_ge(s["ht_mm"], layer * 6 + 2 * i + hf + 1)
                        Ac(htok[0:n, i, hf * 512:(hf + 1) * 512], ps[0:n, 2 + 2 * i + hf, :], ACT.Copy)\
                            .then_inc(s["ht_evac"], 1)
                act.wait_ge(s["ht_evac"], 6 * (layer + 1))
                for i, n in enumerate(TOK):
                    act.dma_start(hbuf[layer][i * P:i * P + n, :], htok[0:n, i, :]).then_inc(s["hbuf_out"], 16)
                act.wait_ge(s["rt_exp_in"], 2 * layer + 1)
                ex = RT[:, 2, 0:12]
                Ac(ex, ex, ACT.Exp).then_inc(s["rt_exp_out"], 1)
                act.wait_ge(s["rt_exp_in"], 2 * layer + 2)
                Ac(RT[:, 15, 21:24], RT[:, 15, 18:21], ACT.Exp).then_inc(s["rt_exp_out"], 1)

                def expert(b, idx, w_gu, w_dn, w_y, g_silu, g_y):
                    w_gu()
                    Ac(hsil[b], ps[:, 2 + b, 0:2 * C], ACT.Silu).then_inc(g_silu, 1)
                    w_dn()
                    w_y()
                    Ac(ysel[b][0:C, 0:512], ps[0:C, 4 + 2 * b, :], ACT.Copy, scale=idx[:, 2:3].bitcast(F32))\
                        .then_inc(g_y, 1)

                with act.Fori(0, NE // NSLOT) as i:
                    for e in range(NSLOT):
                        b = e % 2
                        n1 = i * NSLOT + (e + layer * NE + 1)
                        expert(b, IDX[b],
                               lambda: act.wait_ge(s["gu_mm"], n1),
                               lambda: act.wait_ge(s["dn_mm"], n1),
                               lambda: act.wait_ge(s[f"y_free{b}"], i * 2 + (layer * 8 + e // 2) + AHEAD),
                               s["silu_done"], s["y_act"])
                act.wait_ge(s["jobs_ready"], layer + 1)
                nj, base = further(act, layer)
                with act.If(nj > 0):
                    with act.Fori(0, nj) as j:
                        n1 = base + j + 1
                        expert(0, IDX[0],
                               lambda: act.wait_ge(s["o_gu"], n1),
                               lambda: act.wait_ge(s["o_dn"], n1 + AHEAD),
                               lambda: act.wait_ge(s["o_free"], base + j + AHEAD),
                               s["o_silu"], s["o_yact"])

            layer_norm(0)
            moe(0)
            layer_norm(1)
            act.wait_ge(s["f_neg"], 1)
            link(Ac(lft[1][0:80, :], lft[0][0:80, :], ACT.Abs))
            link(Ac(lft[1][0:80, :], lft[1][0:80, :], ACT.Exp, scale=-1.0))
            Ac(lft[1][0:80, :], lft[1][0:80, :], ACT.Ln, bias=ones[0:80, 0:1]).then_inc(s["f_act"], 1)
            with act.Fori(0, 3) as i:
                empty(i + 4, lambda k: arena[:, bass.ds(i * ACOL + (A_R * ACOL + k * T), T)])
            act.wait_ge(s["tile_free"], 56)
            act.wait_ge(s["f_scan"], 1)
            act.dma_start(O["k"], act_flat(A_KO)).then_inc(s["kv_out"], 16)
            act.dma_start(O["v"], act_flat(A_VO)).then_inc(s["kv_out"], 16)
            act.dma_start(O["logf"], lfo[0:16, :]).then_inc(s["kv_out"], 16)
            with act.Fori(0, NGRP) as g:
                act.wait_ge(s["vt_mm"], g + 1)
                Ac(vt, ps[:, 2, :], ACT.Copy)
                Ac(vtS[0:TS], ps[0:TS, 3, 0:256], ACT.Copy).then_inc(s["vt_ready"], 1)

                def exps(h):
                    b = h % 2
                    if h >= 2:
                        act.wait_ge(s["pt_mm"], g * 4 + (h - 1) + AHEAD)
                    else:
                        act.wait_ge(s["pt_mm"], g * 4 + AHEAD)
                    act.wait_ge(s["sc_max"], g * 4 + h + 1)
                    for qt in range(2):
                        a, w = P * qt, P * (qt + 1)
                        last = Ac(Pp[b][:, a:a + w], ps[:, b, a:a + w], ACT.Exp,
                                  bias=sm[:, 2 * b + qt:2 * b + qt + 1],
                                  accum_out=sm[:, 4 + 2 * b + qt:5 + 2 * b + qt])
                    last.then_inc(s["sc_exp"], 1)

                def outs(h):
                    act.wait_ge(s["pt_mm"], g * 4 + h + 1 + AHEAD)
                    if h >= 2:
                        act.wait_ge(s["pv_mm"], g * 4 + h - 1 + AHEAD)
                    Ac(PT[h % 2], ps[:, 2, 0:384], ACT.Copy).then_inc(s["pt_copy"], 1)
                    if h % 2:
                        act.wait_ge(s["pv_mm"], g * 4 + h + 1 + AHEAD)
                        Ac(arena[:, bass.ds(g * GC + (A_O * ACOL + h // 2 * T), TP)], ps[:, 3, 0:TP], ACT.Copy)\
                            .then_inc(s["pv_copy"], 1)

                exps(0)
                act.wait_ge(s["ss_max"], g + 1)
                act.wait_ge(s["st2_mm"], g + AHEAD)
                Ac(Ps, ps2[:, 4 * 512:4 * 512 + NKEY], ACT.Exp, bias=sm[:, 12:13], accum_out=sm[:, 13:14])\
                    .then_inc(s["ss_exp"], 1)
                exps(1)
                outs(0)
                exps(2)
                outs(1)
                exps(3)
                outs(2)
                outs(3)
                act.wait_ge(s["st2_mm"], g + 1 + AHEAD)
                Ac(PsT, ps[:, 6, :], ACT.Copy)
                Ac(PsT5[0:TS], ps[0:TS, 7, 0:P], ACT.Copy).then_inc(s["st2_copy"], 1)
                act.wait_ge(s["sv_mm"], g + 1 + AHEAD)
                for t in range(2):
                    last = Ac(arena[:, bass.ds(g * GC + (A_O * ACOL + t * T + TP), TS)],
                              ps[:, 7, 128 + t * TS:128 + (t + 1) * TS], ACT.Copy)
                last.then_inc(s["sv_copy"], 1)
            act.wait_ge(s["kv_out"], 48)
            layer_norm(2)
            moe(1)
            layer_norm(3)

        @block.gpsimd
        def _(pool):
            Pl = nc.gpsimd
            for n in ONE_AHEAD:
                pool.sem_inc(s[n], AHEAD)
            Pl.dma_start(ENT[:], I["ent"]).then_inc(s["tbl_fill"], 16)
            for layer in range(2):
                Pl.dma_start(tbl[layer], I["tbl0"]).then_inc(s["tbl_fill"], 16)
            pool.wait_ge(s["pre_ready"], 1)
            with pool.Fori(0, NGRP) as g:
                pool.wait_ge(s["sam_done"], g * len(SAM_JOBS) + AHEAD)
                pool.wait_ge(s["sam_v"], g * SAMJ.count["V"] + AHEAD)
                constant(pool)
                Pl.dma_start(stS, I["state"][bass.ds(g, 1)].rearrange("a p n -> p (a n)")).then_inc(s["st_in"], 16)
                for p in range(2):
                    pool.wait_ge(set_v[p], (g + 1) * SETJ.count["V"] + AHEAD)
                constant(pool)
                Pl.dma_start(O["pwkv"][bass.ds(g, 1)].rearrange("a p n -> p (a n)"), stB).then_inc(s["st_out"], 16)
                pool.wait_ge(s["sam_v"], (g + 1) * SAMJ.count["V"] + AHEAD)
                constant(pool)
                Pl.dma_start(O["swkv"][bass.ds(g, 1)].rearrange("a p n -> p (a n)"), stSo).then_inc(s["st_out"], 16)
                pool.wait_ge(s["st_out"], g * 32 + 32)
                pool.sem_inc(s["st_free"], 1)

            def moe(layer):
                pool.wait_ge(s["tbl_fill"], 48)
                pool.wait_ge(s["ent_ready"], layer + 1)
                for r in range(2):
                    for i, n in enumerate(TOK):
                        Pl.indirect_dma_start(out=tbl[layer],
                                              out_offset=bass.IndirectOffsetOnAxis(
                                                  ap=SLOT[0:n, 3 * r + i:3 * r + i + 1], axis=0),
                                              in_=ENT[0:n, (2 * i + r) * 4:(2 * i + r + 1) * 4], in_offset=None,
                                              bounds_check=NE * TROWS - 1, oob_is_err=False)\
                            .then_inc(s["tbl_scat"], 16)
                pool.wait_ge(s["tbl_scat"], 96 * (layer + 1))
                Pl.dma_start(TBL[:].rearrange("s (e w) -> s e w", e=NE),
                             tbl[layer].rearrange("(e s) w -> s e w", e=NE)[0:C]).then_inc(s["tbl_in"], 16)
                pool.wait_ge(s["tbl_in"], 16 * (layer + 1))
                pool.wait_ge(s["hbuf_out"], 48 * (layer + 1))

                def gather(b, done):
                    Pl.indirect_dma_start(out=xsel[b][0:C, :], out_offset=None, in_=hbuf[layer],
                                          in_offset=bass.IndirectOffsetOnAxis(ap=IDX[b][:, 0:1], axis=0),
                                          bounds_check=T - 1, oob_is_err=False).then_inc(done, 16)

                def scatter(b, done):
                    Pl.indirect_dma_start(out=zbuf[layer],
                                          out_offset=bass.IndirectOffsetOnAxis(ap=IDX[b][:, 1:2], axis=0),
                                          in_=ysel[b][0:C, :], in_offset=None,
                                          bounds_check=2 * T - 1, oob_is_err=False).then_inc(done, 16)

                def fetch(e_col, b, n1, count):
                    constant(pool)
                    Pl.tensor_copy(IDX[b][:], TBL[:, e_col]).then_inc(s["idx_ready"], 1)
                    pool.wait_ge(s["idx_ready"], n1)
                    constant(pool)
                    gather(b, s[f"gath{b}"])

                for e in range(2):
                    fetch(slice(4 * e, 4 * e + 4), e, layer * NE + e + 1, 0)
                with pool.Fori(0, NE // NSLOT - 1) as i:
                    for e in range(NSLOT):
                        b = e % 2
                        n1 = i * NSLOT + (e + layer * NE + 1)
                        pool.wait_ge(s["y_act"], n1 + AHEAD)
                        pool.wait_ge(s["y_dve"], n1 + AHEAD)
                        constant(pool)
                        scatter(b, s[f"z_scat{b}"])
                        pool.wait_ge(s[f"z_scat{b}"], i * 32 + (layer * 128 + e // 2 * 16 + 16))
                        pool.sem_inc(s[f"y_free{b}"], 1)
                        fetch(bass.ds(i * (4 * NSLOT) + 4 * (e + 2), 4), b, n1 + 2, 0)
                for e in range(NSLOT):
                    b = e % 2
                    n1 = layer * NE + NE - NSLOT + e + 1
                    pool.wait_ge(s["y_act"], n1 + AHEAD)
                    pool.wait_ge(s["y_dve"], n1 + AHEAD)
                    scatter(b, s[f"z_scat{b}"])
                    pool.wait_ge(s[f"z_scat{b}"], layer * 128 + 96 + e // 2 * 16 + 16)
                    pool.sem_inc(s[f"y_free{b}"], 1)
                    if e < 2:
                        c = 4 * (NE - 2 + e)
                        fetch(slice(c, c + 4), b, n1 + 2, 0)
                pool.wait_ge(s["jobs_ready"], layer + 1)
                nj, base = further(pool, layer)
                with pool.If(nj > 0):
                    with pool.Fori(0, nj) as j:
                        row = pool.value_load(JI[layer][0:1, bass.ds(j + 8, 1)], min_val=0,
                                              max_val=NE * TROWS - C)
                        Pl.dma_start(IDX[0][:], tbl[layer][bass.ds(row, C), :]).then_inc(s["oidx"], 16)
                        pool.wait_ge(s["oidx"], (base + j) * 16 + 16)
                        constant(pool)
                        gather(0, s["o_gath"])
                        pool.wait_ge(s["o_yact"], base + j + 1 + AHEAD)
                        pool.wait_ge(s["o_ydve"], base + j + 1 + AHEAD)
                        constant(pool)
                        scatter(0, s["o_scat"])
                        pool.wait_ge(s["o_scat"], (base + j) * 16 + 16)
                        pool.sem_inc(s["o_free"], 1)
                zr = zbuf[layer].rearrange("(r t) d -> t r d", r=2)
                for i, n in enumerate(TOK):
                    Pl.dma_start(zin[0:n, i, :, :], zr[i * P:i * P + n]).then_inc(s["z_in"], 16)

            moe(0)
            pool.wait_ge(s["x_ready"], 2)
            pool.wait_ge(s["h_ready"], 3)
            Pl.tensor_copy(act_flat(2), act_flat(A_X)).then_inc(s["xcopy"], 1)
            Pl.dma_start(fw, I["fw"]).then_inc(s["attn_small"], 16)
            Pl.dma_start(clf[0:16, :], I["clf"]).then_inc(s["attn_small"], 16)
            pool.wait_ge(s["tile_free"], 56)
            with pool.Fori(0, NGRP) as g:
                pool.wait_ge(s["sv_mm"], g + AHEAD)
                pool.wait_ge(s["pv_mm"], g * 4 + AHEAD)
                constant(pool)
                for dst, src in ((ck, "ck"), (cv, "cv"), (selg, "sel")):
                    Pl.dma_start(dst, I[src][bass.ds(g, 1)].rearrange("a p n -> p (a n)")).then_inc(s["g_in"], 16)
                Pl.tensor_copy(ks, arena[:, bass.ds(g * GC + A_KO * ACOL, GC)])
                Pl.tensor_copy(vs, arena[:, bass.ds(g * GC + A_VO * ACOL, GC)]).then_inc(s["stage"], 1)
            moe(1)


def kernel(x_prompt, x_sample, state_shift, state_wkv, cache_k, cache_v, cache_logf, c_prompt,
           c_sample, ada_w, ada_b, ln_g, ln_b, a_mu, a_w_rkv, a_w0, a_w1, a_w2, a_a0, a_a1, a_a2,
           a_g1, a_g2, a_k_k, a_k_a, a_r_k, a_lnx_g, a_lnx_b, a_w_o, kv_w, f_w, f_b, b_wq, b_wo,
           rg_w, rg_b, re_w, re_b, exp_wg, exp_wu, exp_wd):
    import concourse.bacc as bacc
    from concourse.bass_utils import run_bass_kernel_spmd as run

    np_ = lambda a: np.asarray(a)

    def fm(a):
        a = np_(a).reshape(-1, D)
        return a.T.reshape(KT, P, -1).transpose(1, 0, 2)

    def halves(w):
        w = np_(w)
        return w.reshape(KT, P, -1, 512).transpose(2, 1, 0, 3).reshape(-1, P, WCOL)

    A = {}
    A["x"] = fm(np.concatenate([np_(x_prompt)[0], np_(x_sample)[0]])).reshape(P, ACOL)
    rows = [np_(a_mu)[0, i] for i in range(6)] + [np_(a)[0] for a in (a_w0, a_a0, a_k_k, a_k_a)]
    rows += [np_(a_r_k)[0].reshape(D), np_(a_lnx_g)[0], np_(a_lnx_b)[0]]
    rows += [np_(a)[l, i] for a in (ln_g, ln_b) for l in range(2) for i in range(2)]
    rows += [np_(state_shift)[0, 0]]
    cols = [fm(r).reshape(P, KT) for r in rows]
    cols.append(fm(np.stack([np_(c_prompt)[0], np_(c_sample)[0]])).reshape(P, 2 * KT))
    cols.append(np_(ada_b).reshape(96, P).T)
    A["vecs"] = np.concatenate(cols, 1)
    A["w"] = np.concatenate([halves(np_(ada_w)[0]), halves(np_(ada_w)[1])]
                            + [halves(np_(a_w_rkv)[0, i]) for i in range(3)] + [halves(np_(a_w_o)[0])]
                            + [halves(np_(kv_w)[:, 0:D]), halves(np_(b_wq)[0]), halves(np_(kv_w)[:, D:]),
                               halves(np_(b_wo)[0])])
    l1 = np.concatenate([np_(a_w1)[0], np_(a_a1)[0], np_(a_g1)[0]], 1)
    pad = lambda a: np.concatenate([a, np.zeros((P - a.shape[0],) + a.shape[1:], a.dtype)])
    A["lora"] = np.concatenate([l1.reshape(KT, P, 256).transpose(1, 0, 2).reshape(P, 2048),
                                pad(np_(a_w2)[0]), pad(np_(a_a2)[0]), np_(a_g2)[0]], 1)
    gu = np.concatenate([np_(exp_wg), np_(exp_wu)], 3).reshape(2 * NE, KT, P, 512).transpose(0, 2, 1, 3)
    dn = np_(exp_wd).reshape(2 * NE, 2, P, D).transpose(0, 2, 1, 3)
    A["experts"] = np.concatenate([gu.reshape(2 * NE, P, WCOL), dn.reshape(2 * NE, P, 2 * D)], 2)
    r = np.concatenate([np_(rg_w), np_(re_w)], 2)
    A["rw"] = r.reshape(2, KT, P, 20).transpose(0, 2, 1, 3).reshape(2, P, KT * 20)
    small = np.zeros((P, 8), np.float32)
    small[0:16, 0] = small[64:80, 0] = np_(f_b)
    for l in range(2):
        small[0:20, 1 + l] = np.concatenate([np_(rg_b)[l], np_(re_b)[l]])
    A["small"] = small
    fwp = np.zeros((KT, P, 80), np.float32)
    fwp[:, :, 0:16] = fwp[:, :, 64:80] = np_(f_w).reshape(KT, P, 16)
    A["fw"] = fwp.transpose(1, 0, 2).reshape(P, KT * 80)
    A["clf"] = np_(cache_logf)[0, ::-1].T
    ckr = np_(cache_k)[0, ::-1].reshape(PAST, NGRP, 2, P)
    A["ck"] = ckr.transpose(1, 3, 2, 0).reshape(NGRP, P, 2 * PAST)
    cvr = np_(cache_v)[0, ::-1].reshape(4, P, NGRP, 256)
    A["cv"] = cvr.transpose(2, 1, 0, 3).reshape(NGRP, P, 1024)
    st = np_(state_wkv)[0, 0].reshape(NGRP, 2, 2, HD, HD)
    A["state"] = st.transpose(0, 2, 4, 1, 3).reshape(NGRP, P, 128)

    i = np.arange(P)
    row, col = i[:, None], i[None, :]
    lo = (col < row).astype(np.float32)
    same = lambda n: (row // n == col // n)
    f = lambda a: a.astype(np.float32)
    hs = np.zeros((P, KT, 16), np.float32)
    for k in range(KT):
        hs[i, k, 2 * k + i // 64] = 1
    blocks = {"ident": f(row == col), "ones": np.ones((P, P)), "mean": np.full((P, P), 1.0 / D),
              "bones": f(same(64)), "bmean": f(same(64)) / HD, "up": f(col > row), "nupi": -f(col >= row),
              "upi": f(col >= row), "mD": -lo * same(16), "mDT": -f(col > row) * same(16),
              "m16": lo * same(32) * ~same(16), "m32": lo * same(64) * ~same(32), "m64": lo * ~same(64),
              "cmask": -BIG * f(col > row), "headsel": hs.reshape(P, P),
              "cmaskS": -BIG * f(col > row % TS)}
    con = np.zeros((P, NCONST), np.float32)
    for n, c in CONST.items():
        w = TS if n == "cmaskS" else P
        con[:, c:c + w] = blocks[n][:, 0:w]
    con[0:16, CO_HST:CO_HST + KT * P] = hs.transpose(2, 1, 0).reshape(16, KT * P)
    tail = [4 - np.arange(4), 16 - np.arange(16), np.arange(16) * TROWS, np.arange(16), np.arange(8),
            [LN_EPS, GN_EPS, 0, 0]]
    con[:, CO_SMALL:] = np.concatenate(tail)
    A["consts"] = con
    sel = np.zeros((NGRP, P, SELW), np.float32)
    for g in range(NGRP):
        for h in range(4):
            sel[g, 4 * g + h, h * P:(h + 1) * P] = 1
            sel[g, 64 + 4 * g + h, h * P:(h + 1) * P] = 1
            sel[g, 4 * g + h, 4 * P + TS * h:4 * P + TS * (h + 1)] = 1
    A["sel"] = sel
    ent = np.zeros((P, NTT, 2, 4), np.int32)
    tok = np.arange(NTT)[None, :] * P + i[:, None]
    for k in range(2):
        ent[:, :, k, 0] = tok
        ent[:, :, k, 1] = tok + k * T
    A["ent"] = ent.reshape(P, NTT * 8)
    t0 = np.zeros((NE * TROWS, 4), np.int32)
    t0[:, 1] = DEST_NONE
    A["tbl0"] = t0

    nc = bacc.Bacc("TRN2", target_bir_lowering=False, num_devices=1)
    arrays, I = {}, {}
    for n, a in A.items():
        a = np.ascontiguousarray(a)
        if a.dtype == np.float64:
            a = a.astype(np.float32)
        arrays["in_" + n] = a
        I[n] = nc.dram_tensor("in_" + n, a.shape, mybir.dt.from_np(a.dtype), kind="ExternalInput").ap()
    outs = {"y": (P, ACOL), "shift": (P, 2 * KT), "pwkv": (NGRP, P, 128), "swkv": (NGRP, P, 128),
            "k": (P, ACOL), "v": (P, ACOL), "logf": (16, T)}
    O = {n: nc.dram_tensor("out_" + n, sh, F32, kind="ExternalOutput").ap() for n, sh in outs.items()}
    build(nc, I, O)
    r = run(nc, [arrays], core_ids=[0]).results[0]
    R = {n: np.asarray(r["out_" + n]) for n in outs}

    def tm(a):
        return a.reshape(P, KT, T).transpose(2, 1, 0).reshape(T, D)

    y, k, v = tm(R["y"]), tm(R["k"]), tm(R["v"])
    shift = R["shift"].reshape(P, KT, 2).transpose(2, 1, 0).reshape(2, 1, 1, D)
    wkv = lambda a: a.reshape(NGRP, 2, HD, 2, HD).transpose(0, 3, 1, 4, 2).reshape(1, 1, NH, HD, HD)
    lf = R["logf"].T
    h4 = lambda a: a.reshape(1, -1, NH, HD)
    return (y[None, 0:TP], y[None, TP:], shift[0], wkv(R["pwkv"]), h4(k[0:TP]), h4(v[0:TP]), lf[None, 0:TP],
            shift[1], wkv(R["swkv"]), h4(k[TP:]), h4(v[TP:]), lf[None, TP:])
```

```python
from contextlib import ExitStack

import concourse.bass as bass
import numpy as np
from concourse import mybir

F32 = mybir.dt.float32
I32 = mybir.dt.int32
ALU = mybir.AluOpType
ACT = mybir.ActivationFunctionType
AX = mybir.AxisListType.X

P = 128
D, KT = 1024, 8
TP, TS = 256, 32
T = TP + TS
NTT = 3
TOK = (128, 128, 32)
NH, HD = 16, 64
PAST = 512
NKEY = PAST + TS
NG, EPG, NE = 4, 4, 16
FH = 256
C = 128
TROWS = 384
JMAX = 8
NO_ROW = 1000
BIG = 1e30
AHEAD = 1
ALPHA = 4.0 ** 0.25
DECAY = float(np.exp(-0.5))
LN_EPS, GN_EPS = 1e-5, 64e-5
ACOL = KT * T
GC = 2 * T
NGRP = 4
WCOL = KT * 512
ECOL = KT * 512 + 2 * D
NSLOT = 4
ADA_SLOTS = 24
ADA_TURN = 4
ADA_TURNS = ADA_SLOTS // ADA_TURN
EARLY_TURNS = 4

VEC = {n: i * KT for i, n in enumerate(
    ["mu0", "mu1", "mu2", "mu3", "mu4", "mu5", "w0", "a0", "k_k", "k_a", "r_k", "lnx_g", "lnx_b",
     "g00", "g01", "g10", "g11", "b00", "b01", "b10", "b11", "shift"])}
VEC_C = len(VEC) * KT
VEC_ADA = VEC_C + 2 * KT
NVEC = VEC_ADA + 96
CONST = {n: i * P for i, n in enumerate(
    ["ident", "ones", "mean", "bones", "bmean", "up", "nupi", "upi", "mD", "mDT", "m16", "m32",
     "m64", "cmask", "headsel"])}
CONST["cmaskS"] = len(CONST) * P
CO_HST = CONST["cmaskS"] + TS
CO_SMALL = CO_HST + KT * P
NCONST = CO_SMALL + 4 + 16 + 16 + 16 + 8 + 4
SELW = 4 * P + P


GROUP_LINKS = 65
ATTN_LINKS = 30


class Chain:

    def __init__(self, eng, sem):
        self.eng, self.sem, self.base, self.k, self.turn, self.per = eng, sem, 0, 0, None, 0

    def did(self, ins):
        self.k += 1
        return ins.then_inc(self.sem, 1)

    def settle(self):
        at = self.base + self.k
        self.eng.wait_ge(self.sem, at if self.turn is None else self.turn * self.per + at)

    def link(self, ins):
        self.did(ins)
        self.settle()

    def until(self, mark):
        self.eng.wait_ge(self.sem, self.base + mark)

    def enter(self, turn, per):
        self.base, self.k, self.turn, self.per = self.base + self.k, 0, turn, per

    def leave(self, turns):
        assert self.k == self.per, (self.k, self.per)
        self.base, self.k, self.turn = self.base + turns * self.per, 0, None


SET_JOBS = [("L", "V"), ("D1T", "A"), ("D2", "A"), ("D2T", "A"), ("KQ", "V"), ("D4", "A"),
            ("X2", "V"), ("RB", "V"), ("D4T", "A"), ("D8", "A"), ("X4", "V"), ("RK", "V"), ("D8T", "A"),
            ("X8", "V"), ("X8T", "A"), ("P16", "A"), ("X16", "V"), ("X16T", "A"), ("P32", "A"),
            ("X32", "V"), ("X32T", "A"), ("P64", "A"), ("X64T", "V"),
            ("WA", "A"), ("UA", "A"), ("YA", "A"), ("SA", "V"),
            ("WB", "A"), ("UB", "A"), ("YB", "A"), ("SB", "V")]
SET_STAGES = [[n] for n, _ in SET_JOBS[:25]] + [["YA", "SA"], ["WB"], ["UB"], ["YB", "SB"]]
SAM_JOBS = [("RAW", "V"), ("D2", "A"), ("X2", "V"), ("D4", "A"), ("X4", "V"), ("D8", "A"), ("X8", "V"),
            ("P16", "A"), ("X16T", "V"), ("W", "A"), ("U", "A"), ("YS", "V")]
SAM_AFTER = {1: "RAW", 4: "D2", 6: "X2", 7: "D4", 9: "X4", 11: "D8", 13: "X8", 15: "P16", 17: "X16T",
             19: "W", 21: "U", 23: "YS"}


class Jobs:

    def __init__(self, jobs):
        self.at = {n: i for i, (n, _) in enumerate(jobs)}
        self.who = dict(jobs)
        self.nth, self.count = {}, {"A": 0, "V": 0}
        for n, e in jobs:
            self.count[e] += 1
            self.nth[n] = self.count[e]
        self.names = [n for n, _ in jobs]


SETJ, SAMJ = Jobs(SET_JOBS), Jobs(SAM_JOBS)


def build(nc, I, O):
    ctx = ExitStack()
    with ctx:
        def sb(name, shape, dt=F32):
            return ctx.enter_context(nc.sbuf_tensor(name, shape, dt))

        def sem(name):
            return ctx.enter_context(nc.semaphore(name))

        con = sb("con", [P, NCONST])
        vec = sb("vec", [P, NVEC])
        mod = sb("mod", [P, 192])
        csil = sb("csil", [P, 2 * KT])
        csig = sb("csig", [P, 2 * KT])
        small = sb("small", [P, 8])
        ring = sb("ring", [P, 2 * WCOL])
        rw = sb("rw", [P, KT * 20])
        ENT = sb("ENT", [P, NTT * 2 * 4], I32)
        SLOT = sb("SLOT", [P, NTT * 2], I32)
        TBL = sb("TBL", [C, NE * 4], I32)
        IDX = [sb(f"IDX{b}", [C, 4], I32) for b in range(NSLOT)]
        IDXG = [sb(f"IDXG{b}", [C, 1], I32) for b in range(NSLOT)]
        JI = [sb(f"JI{i}", [1, 24], I32) for i in range(2)]
        rn = sb("rn", [16, T])
        shrow = sb("shrow", [P, 2 * KT])
        omka = sb("omka", [P, KT])
        ARENA = 17 * ACOL
        arena = sb("arena", [P, ARENA])
        ps = ctx.enter_context(nc.psum_tensor("ps", [P, 8, 512], F32))

        ps2 = ps[:].rearrange("p b n -> p (b n)")
        hbuf = [nc.dram_tensor(f"hbuf{i}", (T, D), F32, kind="Internal").ap() for i in range(2)]
        zbuf = [nc.dram_tensor(f"zbuf{i}", (2 * T, D), F32, kind="Internal").ap() for i in range(2)]
        tbl = [nc.dram_tensor(f"tbl{i}", (NE * TROWS, 4), I32, kind="Internal").ap() for i in range(2)]

        def cut(a, n):
            assert a + n <= ARENA, (a, n, ARENA)
            return arena[:, a:a + n]

        def act_flat(i):
            return cut(i * ACOL, ACOL)

        def acts(i):
            return act_flat(i).rearrange("p (k t) -> p k t", k=KT)

        A_X, A_H, A_KK, A_XX, A_B = 0, 1, 1, 2, 2
        A_R, A_K, A_V, A_G, A_LD, A_CUM, A_Y, A_A = 3, 4, 5, 6, 7, 8, 9, 10
        X, Hh = acts(A_X), acts(A_H)

        def co(name, rows=P, cols=P):
            return con[0:rows, CONST[name]:CONST[name] + cols]

        ident, ones = co("ident"), co("ones")
        hselT = con[0:16, CO_HST:CO_HST + KT * P].rearrange("p (k m) -> p k m", k=KT)
        cs = CO_SMALL
        c4, c16 = con[:, cs:cs + 4], con[:, cs + 4:cs + 20]
        cE, c15 = con[:, cs + 20:cs + 36], con[:, cs + 36:cs + 52]
        c8 = con[:, cs + 52:cs + 60]
        eps_ln, eps_gn = con[:, cs + 60:cs + 61], con[:, cs + 61:cs + 62]

        def v(name, k):
            return vec[:, VEC[name] + k:VEC[name] + k + 1]

        def m(layer, comp, k, stream):
            c = (layer * 48 + comp * 8 + k) * 2 + stream
            return mod[:, c:c + 1]

        aslot = [cut(6 * ACOL + j * WCOL, WCOL) for j in range(2)]
        arow = cut(6 * ACOL + NSLOT * ECOL, 512)
        wslot = [ring[:, j * WCOL:(j + 1) * WCOL].rearrange("p (k n) -> p k n", k=KT) for j in range(2)]
        STREAMS = ((0, TP), (TP, T))

        lw = cut(14 * ACOL, 2048 + 3072)
        lora1 = lw[:, 0:2048].rearrange("p (k n) -> p k n", k=KT)
        w2, a2, g2 = lw[0:64, 2048:3072], lw[0:64, 3072:4096], lw[:, 4096:5120]
        lh = cut(14 * ACOL + 2048 + 3072, 3 * T).rearrange("p (s t) -> p s t", s=3)

        at = [10 * ACOL]

        def take(n):
            at[0] += n
            return cut(at[0] - n, n)

        NAMES = ["D", "DT", "X", "XT", "E16", "E32", "E64", "KQ", "RB", "RK"]
        SU = [{n: take(512) for n in NAMES} for _ in range(2)]
        SS = {n: take(128) for n in NAMES}
        base = 10 * ACOL + 2 * 512 * len(NAMES)
        SS_D, SS_X = cut(base, 256)[0:TS], cut(base + 256, 256)[0:TS]
        rx, qx, bx, kx, vx = (take(GC) for _ in range(5))
        eg, ex1 = take(GC), take(GC)
        rest = [WCOL]

        def take2(n):
            rest[0] += n
            assert rest[0] <= 2 * WCOL
            return ring[:, rest[0] - n:rest[0]]

        Vt, Bt, Kt = (take2(512) for _ in range(3))
        VtS, BtS, KtS = (take2(256) for _ in range(3))
        WU = [take2(256) for _ in range(2)]
        WUS = take2(512)
        stA, stB, stS, stSo = (take2(128) for _ in range(4))
        tst = take2(128)

        at = [7 * ACOL]
        QS, KS, VS, CK, CV, SELG, QZ = ([take(n) for _ in range(2)]
                                        for n in (GC, GC, GC, 1024, 1024, SELW, 128))
        vt, vtS = take(512), take(256)
        Pp = [take(384) for _ in range(2)]
        PT = [take(384) for _ in range(2)]
        Ps, PsT, PsT5 = take(NKEY), take(512), take(128)
        sm = take(16)
        fw = take(KT * 80)
        nF = take(T)
        nFS = take(NKEY)
        clf, lfo = take(PAST), take(T)
        lft = [take(T) for _ in range(3)]
        A_Q, A_KO, A_VO, A_O = 4, 3, 5, 6

        er = [cut(6 * ACOL + (s + NSLOT - 1) % NSLOT * ECOL, ECOL) for s in range(NSLOT)]
        ewgu = [e[:, 0:WCOL].rearrange("p (k n) -> p k n", k=KT) for e in er]
        ewd = [e[:, WCOL:ECOL].rearrange("p (f n) -> p f n", f=2) for e in er]
        at = [2 * ACOL]
        htok = take(3 * D).rearrange("p (i d) -> p i d", i=3)
        at = [2 * ACOL]
        zin = take(6 * D).rearrange("p (i r d) -> p i r d", i=3, r=2)
        at = [5 * ACOL]
        RT = take(16 * NTT * 16).rearrange("p (a b) -> p a b", a=16)
        JT = take(8 * JMAX * 16).rearrange("p (a b) -> p a b", a=8)
        LG = take(NTT * 20).rearrange("p (i n) -> p i n", i=NTT)
        lgf = take(T)[0:20]
        assert at[0] <= 6 * ACOL
        at = [2 * ACOL]
        xselT = take(KT * C)
        ysel = [take(D) for _ in range(NSLOT)]
        hsil, hid, hidT = take(FH), take(FH), take(2 * C)
        assert at[0] <= 5 * ACOL
        late = {4: [(cut(3 * ACOL, WCOL), "ada_in0", 8), (cut(12 * ACOL, WCOL), "ada_in1", 8),
                    (ring[:, 0:WCOL], "wready0", 6), (ring[:, WCOL:2 * WCOL], "wready1", 6)],
                5: [(ring[:, 0:WCOL], "wready0", 7)]
                   + [(er[e][:, 0:WCOL], f"e_in{e}", NE // NSLOT + 1) for e in range(1, NSLOT)]}

        def e_loads(e, layer):
            e = e % NSLOT
            return layer * NE // NSLOT + (1 if e and layer else 0)

        xsel = [ring[:, WCOL + n * D:WCOL + (n + 1) * D] for n in range(NSLOT)]

        ZB, SQB = (10, 5, 2, 5), (11, 2, 11, 2)

        names = """consts_in x_in small_in lora_in rw_in wready0 wready1
            ada_in0 ada_in1 ada_done ada_rows ada_t csil_ready
            csig_done mod_ready h_ready mix_ready tile_done tile_free shift_out lora1_done lora1_act
            lora2_done lora2_act kk_sq norm_mm norm_root bc_mm kk_ready ka_ready pre_ready prod_ready norm_inv bonus_mm bonus_done
            scaled_exp scaled d_ready st_in t_mm t_copy sm_t_mm st_out
            set_done0 set_done1 set_v0 set_v1 set_a0 set_a1 sam_done sam_v sam_a
            gn_mean gn_cent gn_sq gn_var gn_rstd yo_ready
            z_ready ln_mean ln_cent ln_sq ln_var ln_rstd x_ready
            lg_mm lg_act lg_t ht_mm ht_evac hbuf_out rt_exp_in rt_exp_out mask_ready pos_mm
            jobs_ready ent_ready tbl_fill tbl_scat tbl_in e_in0 e_in1 e_in2 e_in3 idx_ready gath0 gath1 gath2 gath3 xt_mm xt_ready gu_mm silu_done
            xt_act hid_ready ht2_mm ht2_ready dn_mm y_act y_dve z_scat o_in oidx o_gath o_xt_mm o_xt o_xta o_gu o_silu o_hid o_ht_mm o_ht o_dn
            o_yact o_ydve o_scat z_in zsum zt_mm zt_free
            xcopy attn_small f_mm f_act f_neg f_scan nf_ready kv_out stage g_in0 g_in1 vt_mm vt_ready qz_ready
            sc_mm sc_max sc_exp sc_norm pt_mm pt_copy pv_mm pv_copy ss_mm ss_max ss_exp ss_norm
            st2_mm st2_copy sv_mm sv_copy out_done st_free y_free o_free passed dve_ch act_ch""".split()
        s = {n: sem(n) for n in names}
        ONE_AHEAD = """ada_t set_v0 set_v1 set_a0 set_a1 sam_v sam_a set_done0 set_done1 sam_done st_free pv_copy sv_copy
            sv_mm pv_mm st2_mm pt_mm y_dve y_act o_dn o_free o_yact o_ydve""".split()
        block = ctx.enter_context(nc.Block())
        wready = [s["wready0"], s["wready1"]]
        set_done, set_v, set_a = ([s[f"set_{k}{p}"] for p in range(2)] for k in ("done", "v", "a"))

        def constant(eng):
            eng.sem_inc(s["passed"], 1)

        def further(eng, layer):
            n = eng.value_load(JI[layer][0:1, 16:17], min_val=0, max_val=JMAX)
            before = eng.value_load(JI[0][0:1, 16:17], min_val=0, max_val=JMAX) if layer else 0
            return n, before

        @block.sync
        def _(sp):
            sp.dma_start(vec[:], I["vecs"]).then_inc(s["consts_in"], 16)
            sp.dma_start(con[:], I["consts"]).then_inc(s["consts_in"], 16)
            sp.dma_start(small[:], I["small"]).then_inc(s["small_in"], 16)
            sp.dma_start(act_flat(A_X), I["x"]).then_inc(s["x_in"], 16)

            def weights(slot, j):
                sp.dma_start(wslot[j].rearrange("p k n -> p (k n)"),
                             I["w"][bass.ds(slot, 1)].rearrange("a p n -> p (a n)")).then_inc(wready[j], 16)

            def half(mi, j):
                if isinstance(mi, int) and mi == 0:
                    sp.wait_ge(s["ada_done"], 3 + j)
                else:
                    sp.wait_ge(s["tile_done"], (mi - 1) * 8 + 4 * (j + 1))
                weights(mi * 2 + (ADA_SLOTS + j), j)

            def ada_weights(slot, j):
                sp.dma_start(aslot[j], I["w"][slot]).then_inc(s[f"ada_in{j}"], 16)

            for j in range(2):
                ada_weights(j, j)
            for j in range(2):
                weights(2 + j, j)
            sp.dma_start(lw, I["lora"]).then_inc(s["lora_in"], 16)
            done = 0
            for slot in range(ADA_TURN, EARLY_TURNS * ADA_TURN):
                sp.wait_ge(s["ada_done"], slot - 3 if slot < ADA_TURN + 2 else slot - 1)
                ada_weights(slot, slot % 2)
                if slot % 4 == 1:
                    half(done // 2, done % 2)
                    done += 1
                if slot == ADA_TURN + 1:
                    half(0, 1)
                    done += 1
            for n in range(done, 6):
                half(n // 2, n % 2)
            half(3, 0)
            sp.wait_ge(s["prod_ready"], 1)
            sp.wait_ge(s["st_out"], 16 * 2 * NGRP)
            half(3, 1)

            def late_weights(turn, j):
                buf, name, _ = late[turn][j]
                sp.dma_start(buf, I["w"][turn * ADA_TURN + j]).then_inc(s[name], 16)

            late_weights(4, 1)
            sp.wait_ge(s["yo_ready"], KT)
            late_weights(4, 0)
            for j in range(2):
                sp.wait_ge(s["tile_done"], 28 + 4 * j)
                late_weights(4, 2 + j)

            def expert_dma(slot, e, layer, wsem):
                sp.dma_start(er[slot],
                             I["experts"][bass.ds(e + layer * NE, 1)].rearrange("a p n -> p (a n)"))\
                    .then_inc(wsem, 16)

            def moe_loads(layer):
                sp.dma_start(rw[:], I["rw"][layer]).then_inc(s["rw_in"], 16)
                expert_dma(0, 0, layer, s["e_in0"])
                sp.wait_ge(s["x_ready"], KT * (2 * layer + 1))
                for e in range(1, NSLOT):
                    if e == 2:
                        sp.wait_ge(s["gath0"], 64 * layer + 16)
                    expert_dma(e, e, layer, s[f"e_in{e}"])
                with sp.Fori(1, NE // NSLOT) as i:
                    for e in range(NSLOT):
                        sp.wait_ge(s["dn_mm"], layer * NE + (i - 1) * NSLOT + (e + 1))
                        expert_dma(e, i * NSLOT + e, layer, s[f"e_in{e}"])
                if layer == 0:
                    for j in range(ADA_TURN):
                        if j == 0:
                            sp.wait_ge(s["ada_done"], 4 * ADA_TURN + 3)
                        else:
                            sp.wait_ge(s["dn_mm"], NE - NSLOT + j + 1)
                        late_weights(5, j)
                sp.wait_ge(s["jobs_ready"], layer + 1)
                sp.wait_ge(s["dn_mm"], (layer + 1) * NE)
                nj, before = further(sp, layer)
                with sp.If(nj > 0):
                    with sp.Fori(0, nj) as j:
                        sp.wait_ge(s["o_dn"], before + j + AHEAD)
                        ej = sp.value_load(JI[layer][0:1, bass.ds(j, 1)], min_val=0, max_val=NE - 1)
                        expert_dma(0, ej, layer, s["o_in"])

            moe_loads(0)
            sp.wait_ge(s["ada_done"], 5 * ADA_TURN + 1)
            half(4, 0)
            sp.wait_ge(s["zsum"], 1)
            half(4, 1)
            with sp.Fori(5, 8) as i:
                for j in range(2):
                    half(i, j)
            moe_loads(1)
            sp.wait_ge(s["x_ready"], 4 * KT)
            sp.dma_start(O["y"], act_flat(A_X)).then_inc(s["out_done"], 16)
            sp.wait_ge(s["out_done"], 16)
            sp.wait_ge(s["shift_out"], 16)
            sp.wait_ge(s["st_out"], 16 * 2 * NGRP)
            sp.wait_ge(s["kv_out"], 48)

        @block.tensor
        def _(pe):
            mm = nc.tensor.matmul

            def tr(out, in_, n):
                return nc.tensor.transpose(out, in_, ident[0:n, 0:n])

            def project(mi, rhs_at, turn=0, ready=None, loads=(1, 1)):
                for j in range(2):
                    pe.wait_ge(wready[j], mi * 16 + 16 * (loads[j] + 1))
                    for o in range(4):
                        tile = 4 * j + o
                        if turn and turn + j < EARLY_TURNS:
                            ada_slot(turn + j, o)
                        if isinstance(mi, int) and mi == 0:
                            if tile >= 4:
                                pe.wait_ge(s["tile_free"], tile - 3)
                        else:
                            pe.wait_ge(s["tile_free"], mi * 8 + (tile - 3))
                        for k in range(KT):
                            if ready and tile == 0:
                                pe.wait_ge(s[ready], k + 1)
                            last = mm(ps[:, tile % 4, 0:T], wslot[j][:, k, o * P:(o + 1) * P], rhs_at(k),
                                      start=k == 0, stop=k == KT - 1)
                        last.then_inc(s["tile_done"], 1)
                        if turn and o == 1 and 1 < turn + j <= EARLY_TURNS:
                            ada_columns(turn + j - 1)

            pe.wait_ge(s["csil_ready"], 1)
            c2 = csil[:].rearrange("p (k s) -> p k s", k=KT)

            def ada_slot(turn, j):
                slot = ADA_TURN * turn + j
                if turn in late:
                    buf, name, loads = late[turn][j]
                    pe.wait_ge(s[name], 16 * loads)
                    w = buf.rearrange("p (k n) -> p k n", k=KT)
                elif turn == 0 and j >= 2:
                    pe.wait_ge(wready[j - 2], 16)
                    w = wslot[j - 2]
                else:
                    pe.wait_ge(s[f"ada_in{j % 2}"], 16 * (slot // 2 if turn else 1))
                    w = aslot[j % 2].rearrange("p (k n) -> p k n", k=KT)
                for k in range(KT):
                    last = mm(ps[32 * j:32 * j + 2, 4 + turn % 2, :], c2[:, k, :], w[:, k, :],
                              start=k == 0, stop=k == KT - 1)
                last.then_inc(s["ada_done"], 1)

            def ada_columns(turn):
                pe.wait_ge(s["ada_rows"], turn + 1)
                if turn >= 2:
                    pe.wait_ge(s["mod_ready"], (turn - 1) * ADA_TURN)
                for o in range(4):
                    last = tr(ps[:, 6 + turn % 2, o * P:(o + 1) * P], arow[:, o * P:(o + 1) * P], P)
                last.then_inc(s["ada_t"], 1)

            pe.wait_ge(s["consts_in"], 32)
            for j in range(ADA_TURN):
                ada_slot(0, j)
            ada_columns(0)

            for i in range(3):
                pe.wait_ge(s["mix_ready"], i + 1)
                project(i, lambda k: cut((11 + i) * ACOL + k * T, T), turn=2 * i + 1)

            pe.wait_ge(s["lora_in"], 16)
            for n, (c0, c1) in enumerate(((0, 64), (64, 128), (128, 256))):
                pe.wait_ge(s["mix_ready"], 4 + n)
                for k in range(KT):
                    last = mm(ps[0:c1 - c0, 4 + n, 0:T], lora1[:, k, c0:c1], cut((11 + n) * ACOL + k * T, T),
                              start=k == 0, stop=k == KT - 1)
                last.then_inc(s["lora1_done"], 1)
            for n, (w, rows) in enumerate(((w2, 64), (a2, 64), (g2, P))):
                pe.wait_ge(s["lora1_act"], n + 1)
                for k in range(KT):
                    c = n * KT + k
                    if c >= 3:
                        pe.wait_ge(s["lora2_act"], c - 2)
                    else:
                        pe.wait_ge(s["lora1_act"], 3)
                    mm(ps[:, 4 + c % 3, 0:T], w[0:rows, k * P:(k + 1) * P], lh[0:rows, n, :],
                       start=True, stop=True).then_inc(s["lora2_done"], 1)
                if n == 0:
                    pe.wait_ge(s["kk_sq"], 1)
                    pe.wait_ge(s["tile_free"], 24)
                    hs = co("headsel").rearrange("p (k h) -> p k h", k=KT)
                    for k in range(KT):
                        last = mm(ps[0:16, 0, 0:T], hs[:, k, :], acts(A_Y)[:, k, :],
                                  start=k == 0, stop=k == KT - 1)
                    last.then_inc(s["norm_mm"], 1)
            pe.wait_ge(s["norm_root"], 1)
            for k in range(KT):
                if k >= 3:
                    pe.wait_ge(s["kk_ready"], k - 2)
                mm(ps[:, 1 + k % 3, 0:T], hselT[:, k, :], rn[0:16, :], start=True, stop=True)\
                    .then_inc(s["bc_mm"], 1)

            with pe.Fori(0, NGRP) as g:
                for p in range(2):
                    pe.wait_ge(set_v[p], g * SETJ.count["V"] + AHEAD)
                    pe.wait_ge(set_a[p], g * SETJ.count["A"] + AHEAD)
                pe.wait_ge(s["sam_v"], g * SAMJ.count["V"] + AHEAD)
                pe.wait_ge(s["sam_a"], g * SAMJ.count["A"] + AHEAD)

                def cols(x, t, c):
                    return x[:, t * T + c * P:t * T + (c + 1) * P]

                for n, x in enumerate((vx, bx, kx)):
                    pe.wait_ge(s["scaled"], g * 5 + n + 1)
                    for c in range(2):
                        for t in range(2):
                            last = tr(ps[:, n, (2 * c + t) * P:(2 * c + t + 1) * P], cols(x, t, c), P)
                    last.then_inc(s["t_mm"], 1)
                for n, x in enumerate((vx, bx, kx)):
                    for t in range(2):
                        o = (n % 2) * 256 + t * P
                        last = tr(ps[0:TS, 6 + n // 2, o:o + P], x[:, t * T + TP:(t + 1) * T], P)
                last.then_inc(s["sm_t_mm"], 1)
                pe.wait_ge(s["scaled"], g * 5 + 4)
                pe.wait_ge(s["t_copy"], g * 2 + 1)

                def wait_set(p, name):
                    who = SETJ.who[name]
                    q, per = (set_v[p], SETJ.count["V"]) if who == "V" else (set_a[p], SETJ.count["A"])
                    pe.wait_ge(q, g * per + SETJ.nth[name] + AHEAD)

                def wait_sam(name):
                    who = SAMJ.who[name]
                    q, per = (s["sam_v"], SAMJ.count["V"]) if who == "V" else (s["sam_a"], SAMJ.count["A"])
                    pe.wait_ge(q, g * per + SAMJ.nth[name] + AHEAD)

                def set_job(p, name):
                    n = SETJ.at[name]
                    bank = 3 * p + n % 3
                    if n >= 3:
                        wait_set(p, SETJ.names[n - 3])
                    B = SU[p]
                    r0 = 64 * p
                    rows = slice(r0, r0 + 64)

                    def sl(x, u):
                        return x[:, u * P:(u + 1) * P]

                    def fx(x, t, c):
                        return x[rows, t * T + c * P:t * T + (c + 1) * P]

                    def square(lhs, rhs):
                        for u in range(4):
                            last = mm(ps[:, bank, u * P:(u + 1) * P], sl(B[lhs], u), sl(B[rhs], u),
                                      start=True, stop=True)
                        return last

                    raw = {"L": (qx, bx), "KQ": (kx, qx), "RB": (bx, rx), "RK": (kx, rx)}
                    if name in raw:
                        a, b = raw[name]
                        for t in range(2):
                            for c in range(2):
                                u = 2 * t + c
                                last = mm(ps[:, bank, u * P:(u + 1) * P], fx(a, t, c), fx(b, t, c),
                                          start=True, stop=True)
                    elif name[0] in "DXP":
                        after = {"D1T": [], "D2": ["D1T"], "D2T": ["D2"], "D4": ["D2T"], "X2": [],
                                 "D4T": ["D4"], "D8": ["D4T"], "X4": ["X2"], "D8T": ["D8"],
                                 "X8": ["D8T", "X4"], "X8T": ["X8"], "P16": ["X8T"], "X16": ["P16"],
                                 "X16T": ["X16"], "P32": ["X16T"], "X32": ["P32"], "X32T": ["X32"],
                                 "P64": ["X32T"], "X64T": ["P64"]}
                        if name == "D1T":
                            pe.wait_ge(s["d_ready"], g * 4 + p + 1)
                        for job in after[name]:
                            wait_set(p, job)
                        if name == "X2":
                            wait_set(p, "L")
                        if name == "X64T":
                            last = square("X", "D")
                        elif name.endswith("T"):
                            for u in range(4):
                                last = tr(ps[:, bank, u * P:(u + 1) * P], sl(B[name[0]], u), P)
                        elif name[0] == "P":
                            last = square("E" + name[1:], "XT")
                        elif name in ("X16", "X32"):
                            last = square("D", "X")
                        else:
                            last = square("DT", name[0])
                    else:
                        c = "AB".index(name[1])
                        st = (None, stA)[c]
                        W, U = WU[p][:, 0:128], WU[p][:, 128:256]

                        def fr(x, t):
                            o = (2 * c + t) * P + r0
                            return x[:, o:o + 64]

                        for t in range(2):
                            u = 2 * t + c
                            if name[0] == "W":
                                if t == 0:
                                    wait_set(p, "RK")
                                    if c:
                                        wait_set(p, "SA")
                                        wait_set(p, "YA")
                                o = ps[:, bank, t * 64:(t + 1) * 64]
                                last = mm(o, sl(B["KQ"], u), fr(Vt, t), start=True, stop=c == 0)
                                if c:
                                    last = mm(o, fx(qx, t, c), st[rows, t * 64:(t + 1) * 64],
                                              start=False, stop=True)
                            elif name[0] == "U":
                                if t == 0:
                                    wait_set(p, "W" + name[1])
                                    wait_set(p, "X64T")
                                last = mm(ps[:, bank, t * 64:(t + 1) * 64], sl(B["XT"], u),
                                          W[:, t * 64:(t + 1) * 64], start=True, stop=True)
                            elif name[0] == "Y":
                                if t == 0:
                                    wait_set(p, "U" + name[1])
                                o = ps[rows, bank, t * P:(t + 1) * P]
                                mm(o, U[:, t * 64:(t + 1) * 64], sl(B["RB"], u), start=True, stop=False)
                                last = mm(o, fr(Vt, t), sl(B["RK"], u), start=False, stop=c == 0)
                                if c:
                                    last = mm(o, st[rows, t * 64:(t + 1) * 64], fx(rx, t, c),
                                              start=False, stop=True)
                            else:
                                o = ps[rows, bank, t * 64:(t + 1) * 64]
                                mm(o, fr(Bt, t), U[:, t * 64:(t + 1) * 64], start=True, stop=False)
                                last = mm(o, fr(Kt, t), fr(Vt, t), start=False, stop=True)
                    last.then_inc(set_done[p], 1)

                def sam_job(name):
                    B = SS
                    W, U = WUS[0:TS, 0:256], WUS[0:TS, 256:512]

                    def sl(x, p, t):
                        u = 2 * p + t
                        return x[0:TS, u * TS:(u + 1) * TS]

                    def fx(x, p, t):
                        return x[64 * p:64 * p + 64, t * T + TP:(t + 1) * T]

                    def fr(x, p, t):
                        return x[0:TS, t * P + 64 * p:t * P + 64 * p + 64]

                    def st(p, t):
                        return stS[64 * p:64 * p + 64, t * 64:(t + 1) * 64]

                    def square(bank, *pairs):
                        for i, (lhs, rhs) in enumerate(pairs):
                            for p in range(2):
                                for t in range(2):
                                    o = i * 128 + (2 * p + t) * TS
                                    last = mm(ps[0:TS, bank, o:o + TS], sl(B[lhs], p, t), sl(B[rhs], p, t),
                                              start=True, stop=True)
                        return last

                    for need in {"D2": ["RAW"], "X2": ["D2"], "D4": [], "X4": ["D4", "X2"], "D8": [],
                                 "X8": ["D8", "X4"], "P16": ["X8"], "X16T": ["P16"], "W": ["X16T"],
                                 "U": ["W"], "YS": ["U"]}.get(name, []):
                        wait_sam(need)
                    if name == "W":
                        pe.wait_ge(s["st_in"], g * 16 + 16)
                    constant(pe)
                    if name == "RAW":
                        for i, (a, b) in enumerate(((qx, bx), (bx, qx), (kx, qx), (bx, rx), (kx, rx))):
                            for p in range(2):
                                for t in range(2):
                                    o = i * 64 + t * TS
                                    last = mm(ps[0:TS, 6 + p, o:o + TS], fx(a, p, t), fx(b, p, t),
                                              start=True, stop=True)
                    elif name[0] == "D":
                        last = square(6, ("DT", "D"), ("D", "DT"))
                    elif name in ("X2", "X4", "X8"):
                        last = square(7, ("DT", "X"), ("D", "XT"))
                    elif name == "P16":
                        last = square(6, ("E16", "XT"))
                    elif name == "X16T":
                        last = square(7, ("X", "D"))
                    else:
                        for p in range(2):
                            for t in range(2):
                                u = (2 * p + t) * 64
                                if name == "W":
                                    o = ps[0:TS, 6 + p, t * 64:(t + 1) * 64]
                                    mm(o, sl(B["KQ"], p, t), fr(VtS, p, t), start=True, stop=False)
                                    last = mm(o, fx(qx, p, t), st(p, t), start=False, stop=True)
                                elif name == "U":
                                    last = mm(ps[0:TS, 6, u:u + 64], sl(B["XT"], p, t), W[:, u:u + 64],
                                              start=True, stop=True)
                                else:
                                    r = slice(64 * p, 64 * p + 64)
                                    o = ps[r, 6 + p, t * TS:(t + 1) * TS]
                                    mm(o, U[:, u:u + 64], sl(B["RB"], p, t), start=True, stop=False)
                                    mm(o, fr(VtS, p, t), sl(B["RK"], p, t), start=False, stop=False)
                                    mm(o, st(p, t), fx(rx, p, t), start=False, stop=True)
                                    o = ps[r, 6 + p, 64 + t * 64:128 + t * 64]
                                    mm(o, fr(BtS, p, t), U[:, u:u + 64], start=True, stop=False)
                                    last = mm(o, fr(KtS, p, t), fr(VtS, p, t), start=False, stop=True)
                    last.then_inc(s["sam_done"], 1)

                for i, stage in enumerate(SET_STAGES):
                    for p in range(2):
                        for name in stage:
                            set_job(p, name)
                    if i == 1:
                        pe.wait_ge(s["scaled"], g * 5 + 5)
                        pe.wait_ge(s["t_copy"], g * 2 + 2)
                    if i in SAM_AFTER:
                        sam_job(SAM_AFTER[i])

            for p in range(2):
                pe.wait_ge(set_a[p], NGRP * SETJ.count["A"] + AHEAD)
            for k in range(KT):
                pe.wait_ge(s["prod_ready"], 1)
                if k >= 4:
                    pe.wait_ge(s["bonus_done"], k - 3)
                mm(ps[:, k % 4, 0:T], co("bones"), acts(A_A)[:, k, :], start=True, stop=True)\
                    .then_inc(s["bonus_mm"], 1)
            pe.wait_ge(s["bonus_done"], KT)
            for k in range(KT):
                if k >= 4:
                    pe.wait_ge(s["gn_cent"], k - 3)
                mm(ps[:, k % 4, 0:T], co("bmean"), acts(A_Y)[:, k, :], start=True, stop=True)\
                    .then_inc(s["gn_mean"], 1)
            pe.wait_ge(s["gn_sq"], 1)
            pe.wait_ge(s["gn_cent"], KT)
            for k in range(KT):
                if k >= 4:
                    pe.wait_ge(s["gn_rstd"], k - 3)
                mm(ps[:, k % 4, 0:T], co("bmean"), acts(A_A)[:, k, :], start=True, stop=True)\
                    .then_inc(s["gn_var"], 1)
            project(3, lambda k: acts(A_CUM)[:, k, :], ready="yo_ready")

            def layer_norm(n):
                for k in range(KT):
                    pe.wait_ge(s["z_ready"], KT * n + k + 1)
                    last = mm(ps[:, 4, 0:T], co("mean"), acts(ZB[n])[:, k, :], start=k == 0, stop=k == KT - 1)
                last.then_inc(s["ln_mean"], 1)
                for k in range(KT):
                    pe.wait_ge(s["ln_sq"], KT * n + k + 1)
                    last = mm(ps[:, 5, 0:T], co("mean"), acts(SQB[n])[:, k, :], start=k == 0, stop=k == KT - 1)
                last.then_inc(s["ln_var"], 1)

            def moe(layer):
                pe.wait_ge(s["rw_in"], 16 * (layer + 1))
                r = rw[:].rearrange("p (k n) -> p k n", k=KT)
                for k in range(KT):
                    pe.wait_ge(s["h_ready"], 1 + 2 * KT * layer + k + 1)
                    last = mm(ps[0:20, 0, 0:T], r[:, k, :], Hh[:, k, :], start=k == 0, stop=k == KT - 1)
                last.then_inc(s["lg_mm"], 1)
                pe.wait_ge(s["lg_act"], layer + 1)
                for i, n in enumerate(TOK):
                    last = tr(ps[0:n, 1, i * 20:(i + 1) * 20], lgf[:, i * P:i * P + n], 20)
                last.then_inc(s["lg_t"], 1)
                if layer == 0:
                    pe.wait_ge(s["ada_rows"], 5)
                for i, n in enumerate(TOK):
                    for hf in range(2):
                        for q in range(4):
                            last = tr(ps[0:n, 2 + 2 * i + hf, q * P:(q + 1) * P],
                                      Hh[:, 4 * hf + q, i * P:i * P + n], P)
                        last.then_inc(s["ht_mm"], 1)
                pe.wait_ge(s["mask_ready"], layer + 1)
                mask = RT[:, 8, :].rearrange("p (i e) -> p i e", i=3)
                for i, n in enumerate(TOK):
                    o = ps[0:n, 0, i * 16:(i + 1) * 16]
                    for i2 in range(i):
                        mm(o, ones[:, 0:n], mask[:, i2, :], start=i2 == 0, stop=False)
                    mm(o, co("up")[0:n, 0:n], mask[0:n, i, :], start=i == 0, stop=True)
                for i, n in enumerate(TOK):
                    last = mm(ps[:, 0, 48:64], ones[0:n, :], mask[0:n, i, :], start=i == 0, stop=i == 2)
                last.then_inc(s["pos_mm"], 1)
                if layer == 0:
                    pe.wait_ge(s["ht_evac"], 6)
                    ada_columns(4)

                def rows_in(x):
                    for q in range(KT):
                        last = tr(ps2[:, q * C:(q + 1) * C], x[:, q * P:(q + 1) * P], C)
                    return last

                def gate_up(slot, b):
                    for k in range(KT):
                        last = mm(ps[:, 2 + b, :], xselT[:, k * C:(k + 1) * C], ewgu[slot][:, k, :],
                                  start=k == 0, stop=k == KT - 1)
                    return last

                def turn_hidden(b):
                    for f in range(2):
                        last = tr(ps[:, 2 + b, f * C:(f + 1) * C], hid[:, f * P:(f + 1) * P], C)
                    return last

                def down(slot, b):
                    for n in range(2):
                        for f in range(2):
                            last = mm(ps[:, 4 + 2 * b + n, :], hidT[:, f * C:(f + 1) * C],
                                      ewd[slot][:, f, n * 512:(n + 1) * 512], start=f == 0, stop=f == 1)
                    return last

                def step_t(e, turn, n):
                    pe.wait_ge(s[f"gath{e % NSLOT}"], turn * 16 + (layer * 64 + 16))
                    constant(pe)
                    rows_in(xsel[e % NSLOT]).then_inc(s["xt_mm"], 1)

                def step_u(e, turn, n):
                    pe.wait_ge(s[f"e_in{e % NSLOT}"], turn * 16 + (16 * e_loads(e, layer) + 16))
                    pe.wait_ge(s["xt_ready"], n + 1)
                    pe.wait_ge(s["xt_act"], n + 1)
                    gate_up(e % NSLOT, e % 2).then_inc(s["gu_mm"], 1)

                def step_h(e, n):
                    pe.wait_ge(s["hid_ready"], n + 1)
                    constant(pe)
                    turn_hidden(e % 2).then_inc(s["ht2_mm"], 1)

                def step_d(e, turn, n):
                    pe.wait_ge(s["ht2_ready"], n + 1)
                    if not isinstance(n, int) or n > 0:
                        pe.wait_ge(s["y_dve"], n - 1 + AHEAD)
                        pe.wait_ge(s["y_act"], n - 1 + AHEAD)
                    down(e % NSLOT, e % 2).then_inc(s["dn_mm"], 1)

                pe.wait_ge(s["ht_evac"], 6 * (layer + 1))
                pe.wait_ge(s["ent_ready"], layer + 1)
                n0 = layer * NE
                step_t(0, 0, n0)
                step_u(0, 0, n0)
                step_t(1, 0, n0 + 1)
                step_h(0, n0)
                with pe.Fori(0, NE // NSLOT - 1) as i:
                    for e in range(1, 1 + NSLOT):
                        n = i * NSLOT + (e + n0)
                        step_u(e, i + e // NSLOT, n)
                        step_t(e + 1, i + (e + 1) // NSLOT, n + 1)
                        step_d(e - 1, i, n - 1)
                        step_h(e, n)
                for e in range(NE - NSLOT + 1, NE):
                    step_u(e, e // NSLOT, n0 + e)
                    if e + 1 < NE:
                        step_t(e + 1, (e + 1) // NSLOT, n0 + e + 1)
                    step_d(e - 1, (e - 1) // NSLOT, n0 + e - 1)
                    step_h(e, n0 + e)
                step_d(NE - 1, NE // NSLOT - 1, n0 + NE - 1)
                pe.wait_ge(s["jobs_ready"], layer + 1)
                nj, base = further(pe, layer)
                with pe.If(nj > 0):
                    with pe.Fori(0, nj) as j:
                        n = base + j
                        pe.wait_ge(s["o_gath"], n * 16 + 16)
                        constant(pe)
                        rows_in(xsel[0]).then_inc(s["o_xt_mm"], 1)
                        pe.wait_ge(s["o_in"], n * 16 + 16)
                        pe.wait_ge(s["o_xt"], n + 1)
                        pe.wait_ge(s["o_xta"], n + 1)
                        gate_up(0, 0).then_inc(s["o_gu"], 1)
                        pe.wait_ge(s["o_hid"], n + 1)
                        constant(pe)
                        turn_hidden(0).then_inc(s["o_ht_mm"], 1)
                        pe.wait_ge(s["o_ht"], n + 1)
                        pe.wait_ge(s["y_dve"], (layer + 1) * NE + AHEAD)
                        pe.wait_ge(s["y_act"], (layer + 1) * NE + AHEAD)
                        pe.wait_ge(s["o_yact"], n + AHEAD)
                        pe.wait_ge(s["o_ydve"], n + AHEAD)
                        down(0, 0).then_inc(s["o_dn"], 1)
                    pe.wait_ge(s["o_yact"], nj + (base + AHEAD))
                    pe.wait_ge(s["o_ydve"], nj + (base + AHEAD))

                if layer == 0:
                    pe.wait_ge(s["y_dve"], NE + AHEAD)
                    pe.wait_ge(s["y_act"], NE + AHEAD)
                    for j in range(ADA_TURN):
                        ada_slot(5, j)
                    ada_columns(5)
                pe.wait_ge(s["zsum"], layer + 1)
                for k in range(KT):
                    c = layer * KT + k
                    if c >= 4:
                        pe.wait_ge(s["zt_free"], c - 3)
                    for i, n in enumerate(TOK):
                        last = tr(ps[:, k % 4, i * P:i * P + n], zin[0:n, i, 0, k * P:(k + 1) * P], n)
                    last.then_inc(s["zt_mm"], 1)

            layer_norm(0)
            for j in range(ADA_TURN):
                ada_slot(4, j)
            moe(0)
            layer_norm(1)

            pe.wait_ge(s["attn_small"], 32)
            pe.wait_ge(s["x_ready"], 2 * KT)
            fwv = fw.rearrange("p (k n) -> p k n", k=KT)
            for k in range(KT):
                last = mm(ps[0:80, 7, 0:T], fwv[:, k, :], X[:, k, :], start=k == 0, stop=k == KT - 1)
            last.then_inc(s["f_mm"], 1)
            pe.wait_ge(s["xcopy"], 1)
            pe.wait_ge(s["h_ready"], 1 + 2 * KT)
            with pe.Fori(0, 3) as i:
                project(i + 4, lambda k: arena[:, bass.ds(i * ACOL + k * T, T)], loads=(3, 2))
            with pe.Fori(0, NGRP // 2) as pair:
                for half in range(2):
                    g = pair * 2 + half
                    qs, ks, vs, ck, cv = QS[half], KS[half], VS[half], CK[half], CV[half]
                    selg, qz = SELG[half], QZ[half]
                    pe.wait_ge(s["stage"], g + 1)
                    pe.wait_ge(s["nf_ready"], 1)
                    pe.wait_ge(s["tile_free"], 56)
                    pe.wait_ge(s["pv_copy"], g * 2 + AHEAD)
                    pe.wait_ge(s["sv_copy"], g + AHEAD)
                    for c in range(2):
                        for t in range(2):
                            tr(ps[:, 2, (2 * c + t) * P:(2 * c + t + 1) * P], vs[:, t * T + c * P:t * T + (c + 1) * P], P)
                    for t in range(2):
                        last = tr(ps[0:TS, 3, t * P:(t + 1) * P], vs[:, t * T + TP:(t + 1) * T], P)
                    last.then_inc(s["vt_mm"], 1)
                    pe.wait_ge(s[f"g_in{half}"], pair * 48 + 48)

                    def scores(h):
                        t, p = h // 2, h % 2
                        r = slice(64 * p, 64 * p + 64)
                        r16 = slice(64 * p, 64 * p + 16)
                        if h >= 2:
                            pe.wait_ge(s["sc_exp"], g * 4 + (h - 1))
                        b = h % 2
                        sel = selg[r16, h * P:(h + 1) * P]
                        for qt in range(2):
                            q = qs[r, t * T + qt * P:t * T + (qt + 1) * P]
                            c0 = 128 * qt
                            w = P * (qt + 1)
                            o = ps[:, b, c0:c0 + w]
                            mm(o, sel, nF[r16, 0:w], start=True, stop=False)
                            mm(ps[:, b, c0 + w - P:c0 + w], ident, co("cmask"), start=False, stop=False,
                               skip_group_check=True)
                            last = mm(o, q, ks[r, t * T:t * T + w], start=False, stop=True)
                        last.then_inc(s["sc_mm"], 1)

                    def turn_head(h):
                        pe.wait_ge(s["sc_norm"], g * 4 + (h + 1))
                        if h >= 1:
                            pe.wait_ge(s["pt_copy"], g * 4 + h)
                        for j in range(3):
                            last = tr(ps[:, 2, j * P:(j + 1) * P], Pp[h % 2][:, j * P:(j + 1) * P], P)
                        last.then_inc(s["pt_mm"], 1)

                    def out_head(h):
                        t, p = h // 2, h % 2
                        pe.wait_ge(s["pt_copy"], g * 4 + (h + 1))
                        if h == 2:
                            pe.wait_ge(s["pv_copy"], g * 2 + 1 + AHEAD)
                        f0 = t * P + 64 * p
                        r = slice(64 * p, 64 * p + 64)
                        pt = PT[h % 2]
                        mm(ps[r, 3, 0:P], vt[:, f0:f0 + 64], pt[:, 0:P], start=True, stop=True)
                        mm(ps[r, 3, P:2 * P], vt[:, f0:f0 + 64], pt[:, P:2 * P], start=True, stop=False)
                        last = mm(ps[r, 3, P:2 * P], vt[:, 256 + f0:256 + f0 + 64], pt[:, 2 * P:3 * P],
                                  start=False, stop=True)
                        last.then_inc(s["pv_mm"], 1)

                    scores(0)
                    pe.wait_ge(s["qz_ready"], g + 1)
                    sel = selg[0:16, 4 * P:5 * P]
                    for bank, a, w in ((4, 0, PAST), (5, PAST, TS)):
                        for t in range(2):
                            h = slice(64 * t, 64 * t + 64)
                            o = ps[h, bank, 0:w]
                            mm(o, sel[:, h], nFS[0:16, a:a + w], start=True, stop=False)
                            if bank == 5:
                                mm(o, ident[:, h], co("cmaskS", P, TS), start=False, stop=False)
                            rhs = ck[:, t * PAST:(t + 1) * PAST] if bank == 4 else ks[:, t * T + TP:(t + 1) * T]
                            last = mm(o, qz[:, h], rhs, start=False, stop=True)
                    last.then_inc(s["ss_mm"], 1)
                    scores(1)
                    pe.wait_ge(s["vt_ready"], g + 1)
                    for h in range(4):
                        turn_head(h)
                        if h < 2:
                            scores(h + 2)
                        out_head(h)
                        if h == 1:
                            pe.wait_ge(s["ss_norm"], g + 1)
                            for j in range(4):
                                tr(ps[:, 6, j * P:(j + 1) * P], Ps[:, j * P:(j + 1) * P], P)
                            last = tr(ps[0:TS, 7, 0:P], Ps[:, PAST:NKEY], P)
                            last.then_inc(s["st2_mm"], 1)
                        if h == 2:
                            pe.wait_ge(s["st2_copy"], g + 1)
                            for t in range(2):
                                for p in range(2):
                                    o = ps[64 * p:64 * p + 64, 7, 128 + t * TS:128 + (t + 1) * TS]
                                    q0 = t * 64 + p * TS
                                    f0 = t * P + 64 * p
                                    for j in range(4):
                                        mm(o, cv[:, j * 256 + f0:j * 256 + f0 + 64], PsT[:, j * P + q0:j * P + q0 + TS],
                                           start=j == 0, stop=False)
                                    last = mm(o, vtS[0:TS, f0:f0 + 64], PsT5[0:TS, q0:q0 + TS], start=False, stop=True)
                            last.then_inc(s["sv_mm"], 1)
            pe.wait_ge(s["pv_copy"], 2 * NGRP + AHEAD)
            pe.wait_ge(s["sv_copy"], NGRP + AHEAD)
            project(7, lambda k: acts(A_O)[:, k, :], loads=(3, 2))
            layer_norm(2)
            moe(1)
            layer_norm(3)

        @block.vector
        def _(dve):
            V = nc.vector
            ch = Chain(dve, s["dve_ch"])
            did, settle, link = ch.did, ch.settle, ch.link

            def bc(x, n, shape):
                return x.unsqueeze(n).to_broadcast(shape)

            dve.wait_ge(s["csig_done"], 1)
            V.tensor_tensor(csil[:], vec[:, VEC_C:VEC_C + 2 * KT], csig[:], ALU.mult).then_inc(s["csil_ready"], 1)
            V.memset(arow, 0.0).then_inc(s["csil_ready"], 1)

            def parts(turn):
                dve.wait_ge(s["ada_t"], turn + 1 + AHEAD)
                for j in range(ADA_TURN):
                    c = 16 * turn + 4 * j
                    V.tensor_tensor(
                        mod[:, 2 * c:2 * c + 8].rearrange("p (o s) -> p o s", s=2),
                        ps[:, 6 + turn % 2, :].rearrange("p (o m) -> p o m", m=P)[:, :, 32 * j:32 * j + 2],
                        bc(vec[:, VEC_ADA + c:VEC_ADA + c + 4], 2, [P, 4, 2]), ALU.add)\
                        .then_inc(s["mod_ready"], 1)

            def one_more(*which):
                for layer, comp in which:
                    c = (layer * 48 + comp * 8) * 2
                    did(V.tensor_scalar(mod[:, c:c + 16], mod[:, c:c + 16], 1.0, None, ALU.add))
                settle()

            parts(0)
            dve.wait_ge(s["mod_ready"], ADA_TURN)
            one_more((0, 1))
            did(V.tensor_scalar(omka[:], vec[:, VEC["k_a"]:VEC["k_a"] + KT], -1.0, 1.0, ALU.mult, ALU.add))
            settle()

            def modulate(layer, comp, signal):
                for k in range(KT):
                    for st, (a, b) in enumerate(STREAMS):
                        last = V.tensor_scalar(Hh[:, k, a:b], X[:, k, a:b], m(layer, comp + 1, k, st),
                                               m(layer, comp, k, st), ALU.mult, ALU.add)
                        did(last)
                settle()
                dve.sem_inc(signal, 1)

            dve.wait_ge(s["x_in"], 16)
            modulate(0, 0, s["h_ready"])
            XX = acts(A_XX)
            for a, b in STREAMS:
                did(V.tensor_tensor(XX[:, :, a + 1:b], Hh[:, :, a:b - 1], Hh[:, :, a + 1:b], ALU.subtract))
            did(V.tensor_scalar(XX[:, :, 0:1], Hh[:, :, 0:1], -1.0, None, ALU.mult))
            did(V.tensor_tensor(XX[:, :, TP:TP + 1], vec[:, VEC["shift"]:VEC["shift"] + KT].unsqueeze(2),
                                Hh[:, :, TP:TP + 1], ALU.subtract))
            settle()
            for n in range(6):
                if n >= 3:
                    if 2 * n - 5 < EARLY_TURNS:
                        parts(2 * n - 5)
                    dve.wait_ge(s["tile_done"], 8 * (n - 2))
                for k in range(KT):
                    last = V.scalar_tensor_tensor(cut((11 + n % 3) * ACOL + k * T, T), XX[:, k, :],
                                                  v(f"mu{n}", k), Hh[:, k, :], ALU.mult, ALU.add)
                last.then_inc(s["mix_ready"], 1)
                if n == 3:
                    parts(2)
            dve.wait_ge(s["mod_ready"], EARLY_TURNS * ADA_TURN)
            one_more((0, 4), (1, 1))

            R, K, Vv, G = acts(A_R), acts(A_K), acts(A_V), acts(A_G)
            LD, CUM, Y, A, KK, B = acts(A_LD), acts(A_CUM), acts(A_Y), acts(A_A), acts(A_KK), acts(A_B)
            dve.wait_ge(s["tile_free"], 24)
            dve.wait_ge(s["shift_out"], 16)
            dve.wait_ge(s["mix_ready"], 6)
            for k in range(KT):
                did(V.tensor_scalar(KK[:, k, :], K[:, k, :], v("k_k", k), None, ALU.mult))
            settle()
            V.tensor_tensor(act_flat(A_Y), act_flat(A_KK), act_flat(A_KK), ALU.mult).then_inc(s["kk_sq"], 1)
            dve.wait_ge(s["norm_mm"], 1)
            link(V.tensor_scalar(rn[:], ps[0:16, 0, 0:T], 1e-24, None, ALU.max))
            V.reciprocal(rn[:], rn[:]).then_inc(s["norm_inv"], 1)
            dve.wait_ge(s["lora2_act"], 8)
            for k in range(KT):
                for a, b in ((0, P), (P, TP), (TP, T)):
                    did(V.tensor_tensor_scan(CUM[:, k, a:b], ones[:, 0:b - a], LD[:, k, a:b], 0.0,
                                             ALU.mult, ALU.add))
            settle()
            link(V.tensor_tensor(act_flat(A_LD), act_flat(A_CUM), act_flat(A_LD), ALU.subtract))
            dve.wait_ge(s["ka_ready"], 1)
            link(V.tensor_tensor(act_flat(A_K), act_flat(A_K), act_flat(A_Y), ALU.mult))
            for k in range(KT):
                dve.wait_ge(s["bc_mm"], k + 1)
                did(V.tensor_tensor(KK[:, k, :], KK[:, k, :], ps[:, 1 + k % 3, 0:T], ALU.mult))
                settle()
                dve.sem_inc(s["kk_ready"], 1)
                did(V.tensor_tensor(B[:, k, :], KK[:, k, :], A[:, k, :], ALU.mult))
            settle()
            dve.sem_inc(s["pre_ready"], 1)

            def four(x, n=P, rows=P):
                return x[0:rows].rearrange("p (u m) -> p u m", u=4)

            def mask4(name, rows=P, cols=P):
                return bc(co(name, rows, cols), 1, [rows, 4, cols])

            with dve.Fori(0, NGRP) as g:
                ch.enter(g, GROUP_LINKS)
                for p in range(2):
                    dve.wait_ge(set_done[p], g * len(SET_JOBS) + AHEAD)
                dve.wait_ge(s["sam_done"], g * len(SAM_JOBS) + AHEAD)

                def src(a):
                    return arena[:, bass.ds(g * GC + a * ACOL, GC)]

                V.tensor_copy(vx, src(A_V)).then_inc(s["scaled"], 1)
                dve.wait_ge(s["scaled_exp"], g * 3 + 1)
                V.tensor_tensor(bx, src(A_B), ex1, ALU.mult).then_inc(s["scaled"], 1)
                V.tensor_tensor(kx, src(A_K), ex1, ALU.mult).then_inc(s["scaled"], 1)
                dve.wait_ge(s["scaled_exp"], g * 3 + 2)
                V.tensor_tensor(qx, src(A_KK), qx, ALU.mult).then_inc(s["scaled"], 1)
                dve.wait_ge(s["scaled_exp"], g * 3 + 3)
                V.tensor_tensor(rx, src(A_R), eg, ALU.mult).then_inc(s["scaled"], 1)

                def set_evac(p, name):
                    n = SETJ.at[name]
                    bank = 3 * p + n % 3
                    B = SU[p]
                    src = four(ps[:, bank, :])
                    if name != "L":
                        dve.wait_ge(set_done[p], g * len(SET_JOBS) + n + 1 + AHEAD)
                    if name == "L":
                        for w in ("16", "32", "64"):
                            did(V.tensor_tensor(four(B["E" + w]), src, mask4("m" + w), ALU.mult))
                        settle()
                    elif name in ("KQ", "RB", "RK"):
                        mask = {"KQ": "up", "RB": "nupi", "RK": "upi"}[name]
                        link(V.tensor_tensor(four(B[name]), src, mask4(mask), ALU.mult))
                    elif name in ("SA", "SB"):
                        rows = slice(64 * p, 64 * p + 64)
                        c = "AB".index(name[1])
                        out = (stA, stB)[c]
                        e = [eg[rows, t * T + c * P + P - 1:t * T + c * P + P] for t in range(2)]
                        if c == 0:
                            for t in range(2):
                                h = slice(t * 64, t * 64 + 64)
                                did(V.tensor_scalar(out[rows, h], ps[rows, bank, h], e[t], None, ALU.mult))
                            settle()
                        else:
                            for t in range(2):
                                h = slice(t * 64, t * 64 + 64)
                                did(V.tensor_scalar(tst[rows, h], stA[rows, h], e[t], None, ALU.mult))
                            settle()
                            if p == 0:
                                dve.wait_ge(s["st_free"], g + AHEAD)
                            for t in range(2):
                                h = slice(t * 64, t * 64 + 64)
                                did(V.scalar_tensor_tensor(out[rows, h], ps[rows, bank, h], e[t], tst[rows, h],
                                                           ALU.mult, ALU.add))
                            settle()
                    else:
                        x = B["XT"] if name.endswith("T") else B["X"]
                        sub = name[1:3] in ("16", "32", "64")
                        link(V.tensor_tensor(x, x, ps[:, bank, :], ALU.subtract if sub else ALU.add))
                    dve.sem_inc(set_v[p], 1)

                def sam_evac(name):
                    n = SAMJ.at[name]
                    B = SS
                    dve.wait_ge(s["sam_done"], g * len(SAM_JOBS) + n + 1 + AHEAD)

                    def masked(i, out, name):
                        for p in range(2):
                            did(V.tensor_tensor(
                                out[0:TS, 64 * p:64 * p + 64].rearrange("p (u m) -> p u m", u=2),
                                ps[0:TS, 6 + p, i * 64:i * 64 + 64].rearrange("p (u m) -> p u m", u=2),
                                bc(co(name, TS, TS), 1, [TS, 2, TS]), ALU.mult))

                    if name == "RAW":
                        for i, (out, mask) in enumerate((("D", "mD"), ("DT", "mDT"), ("KQ", "up"),
                                                         ("RB", "nupi"), ("RK", "upi"))):
                            masked(i, B[out], mask)
                        masked(0, B["E16"], "m16")
                        settle()
                        link(V.tensor_tensor(SS_X.rearrange("p (u m) -> p u m", u=8),
                                             SS_D.rearrange("p (u m) -> p u m", u=8),
                                             bc(co("ident", TS, TS), 1, [TS, 8, TS]), ALU.add))
                    elif name in ("X2", "X4", "X8"):
                        link(V.tensor_tensor(SS_X, SS_X, ps[0:TS, 7, 0:256], ALU.add))
                    elif name == "X16T":
                        link(V.tensor_tensor(B["XT"][0:TS], B["XT"][0:TS], ps[0:TS, 7, 0:128], ALU.subtract))
                    else:
                        def at(p, t):
                            rows = slice(64 * p, 64 * p + 64)
                            return rows, slice(t * 64, t * 64 + 64), eg[rows, t * T + T - 1:t * T + T]

                        for p in range(2):
                            for t in range(2):
                                rows, h, e = at(p, t)
                                did(V.tensor_scalar(tst[rows, h], stS[rows, h], e, None, ALU.mult))
                                did(V.tensor_copy(arena[rows, bass.ds(g * GC + (A_Y * ACOL + t * T + TP), TS)],
                                                  ps[rows, 6 + p, t * TS:(t + 1) * TS]))
                        settle()
                        dve.wait_ge(s["st_free"], g + AHEAD)
                        for p in range(2):
                            for t in range(2):
                                rows, h, e = at(p, t)
                                did(V.scalar_tensor_tensor(stSo[rows, h], ps[rows, 6 + p, 64 + t * 64:128 + t * 64],
                                                           e, tst[rows, h], ALU.mult, ALU.add))
                        settle()
                    dve.sem_inc(s["sam_v"], 1)

                for p in range(2):
                    dve.wait_ge(set_done[p], g * len(SET_JOBS) + 1 + AHEAD)
                    V.tensor_tensor(four(SU[p]["D"]), four(ps[:, 3 * p, :]), mask4("mD"), ALU.mult)\
                        .then_inc(s["d_ready"], 1)
                dve.wait_ge(s["d_ready"], g * 4 + 2)
                for p in range(2):
                    V.tensor_tensor(four(SU[p]["X"]), four(SU[p]["D"]), mask4("ident"), ALU.add)\
                        .then_inc(s["d_ready"], 1)
                for i, stage in enumerate(SET_STAGES):
                    for p in range(2):
                        for name in stage:
                            if SETJ.who[name] == "V":
                                set_evac(p, name)
                    if SAMJ.who.get(SAM_AFTER.get(i)) == "V":
                        sam_evac(SAM_AFTER[i])
                ch.leave(NGRP)

            for p in range(2):
                dve.wait_ge(set_done[p], NGRP * len(SET_JOBS) + AHEAD)
            dve.wait_ge(s["sam_done"], NGRP * len(SAM_JOBS) + AHEAD)
            for k in range(KT):
                did(V.scalar_tensor_tensor(A[:, k, :], K[:, k, :], v("r_k", k), R[:, k, :], ALU.mult, ALU.mult))
            settle()
            dve.sem_inc(s["prod_ready"], 1)
            for k in range(KT):
                dve.wait_ge(s["bonus_mm"], k + 1)
                did(V.tensor_tensor(K[:, k, :], Vv[:, k, :], ps[:, k % 4, 0:T], ALU.mult))
                settle()
                dve.sem_inc(s["bonus_done"], 1)
                did(V.tensor_scalar(K[:, k, :], K[:, k, :], v("lnx_b", k), None, ALU.add))
            for k in range(KT):
                dve.wait_ge(s["gn_mean"], k + 1)
                did(V.tensor_tensor(Y[:, k, :], Y[:, k, :], ps[:, k % 4, 0:T], ALU.subtract))
                settle()
                dve.sem_inc(s["gn_cent"], 1)
            mark = {}
            for i in range(KT + 2):
                for step, k in enumerate((i, i - 1, i - 2)):
                    if not 0 <= k < KT:
                        continue
                    if step == 0:
                        dve.wait_ge(s["gn_rstd"], KT + k + 1)
                        did(V.tensor_tensor(Y[:, k, :], Y[:, k, :], acts(A_XX)[:, k, :], ALU.mult))
                    elif step == 1:
                        ch.until(mark[0, k])
                        did(V.scalar_tensor_tensor(Y[:, k, :], Y[:, k, :], v("lnx_g", k), K[:, k, :],
                                                   ALU.mult, ALU.add))
                    else:
                        ch.until(mark[1, k])
                        V.tensor_tensor(CUM[:, k, :], Y[:, k, :], G[:, k, :], ALU.mult).then_inc(s["yo_ready"], 1)
                    mark[step, k] = ch.k

            def scaled_x(n):
                link(V.tensor_scalar(act_flat(ZB[n]), act_flat(A_X), ALPHA, None, ALU.mult))

            def residual(n, layer, comp, tiles, freed, first):
                Z = acts(ZB[n])
                if not n % 2:
                    scaled_x(n)
                for k in range(KT):
                    dve.wait_ge(tiles, first + k + 1)
                    for st, (a, b) in enumerate(STREAMS):
                        did(V.scalar_tensor_tensor(Z[:, k, a:b], ps[:, k % 4, a:b], m(layer, comp, k, st),
                                                   Z[:, k, a:b], ALU.mult, ALU.add))
                    settle()
                    dve.sem_inc(freed, 1)
                    dve.sem_inc(s["z_ready"], 1)

            def layer_norm(n):
                Z = acts(ZB[n])
                dve.wait_ge(s["ln_mean"], n + 1)
                for k in range(KT):
                    V.tensor_tensor(Z[:, k, :], Z[:, k, :], ps[:, 4, 0:T], ALU.subtract)\
                        .then_inc(s["ln_cent"], 1)
                dve.wait_ge(s["ln_cent"], KT * (n + 1))
                dve.wait_ge(s["ln_rstd"], n + 1)
                rstd, mark = acts(SQB[n])[:, 0, :], []
                for k in range(KT + 1):
                    if k < KT:
                        did(V.tensor_tensor(Z[:, k, :], Z[:, k, :], rstd, ALU.mult))
                        mark.append(ch.k)
                    if k:
                        ch.until(mark[k - 1])
                        V.tensor_scalar(X[:, k - 1, :], Z[:, k - 1, :], v(f"g{n // 2}{n % 2}", k - 1),
                                        v(f"b{n // 2}{n % 2}", k - 1), ALU.mult, ALU.add)\
                            .then_inc(s["x_ready"], 1)
                dve.wait_ge(s["x_ready"], KT * (n + 1))

            def moe(layer):
                L3 = LG
                did(V.memset(LG, 0.0))
                did(V.memset(RT, 0.0))
                settle()
                dve.wait_ge(s["lg_t"], layer + 1)
                did(V.tensor_copy(L3[:, 0:2, :], ps[:, 1, 0:40].rearrange("p (i n) -> p i n", i=2)))
                did(V.tensor_copy(L3[0:TS, 2, :], ps[0:TS, 1, 40:60]))
                settle()
                gl = L3[:, :, 0:NG]

                def row(i, n):
                    return RT[:, i, 0:NTT * n].rearrange("p (i n) -> p i n", i=NTT)

                def col(i, j):
                    return RT[:, i, NTT * j:NTT * (j + 1)]

                def b3(x, n):
                    return bc(x, 2, [P, NTT, n])

                def first_max(vals, n, mx, eq, out, cn, vm):
                    link(V.tensor_reduce(mx, vals, AX, ALU.max))
                    link(V.tensor_tensor(eq, vals, b3(mx, n), ALU.is_equal))
                    link(V.tensor_tensor(eq, eq, bc(cn, 1, [P, NTT, n]), ALU.mult))
                    link(V.tensor_reduce(vm, eq, AX, ALU.max))
                    link(V.tensor_tensor(out, eq, b3(vm, n), ALU.is_equal))

                gmax, gsum, gp, vm, m1, m2, dm, e2, w1, w2_ = (col(15, j) for j in range(10))
                gsel, eq4, ex = row(0, NG), row(1, NG), row(2, NG)
                em, eq, oh1, oh2, pen = row(3, NE), row(4, NE), row(5, NE), row(6, NE), row(7, NG)
                mask, posE, pr = row(8, NE), row(9, NE), row(10, NE)
                first_max(gl, NG, gmax, eq4, gsel, c4, vm)
                link(V.tensor_tensor(ex, gl, b3(gmax, NG), ALU.subtract))
                dve.sem_inc(s["rt_exp_in"], 1)
                link(V.tensor_scalar(pen, gsel, BIG, -BIG, ALU.mult, ALU.add))
                for i in range(NTT):
                    did(V.tensor_tensor(em[:, i, :].rearrange("p (a b) -> p a b", a=NG),
                                        L3[:, i, NG:20].rearrange("p (a b) -> p a b", a=NG),
                                        bc(pen[:, i, :], 2, [P, NG, EPG]), ALU.add))
                settle()
                first_max(em, NE, m1, eq, oh1, c16, vm)
                link(V.scalar_tensor_tensor(em, oh1, -2 * BIG, em, ALU.mult, ALU.add))
                first_max(em, NE, m2, eq, oh2, c16, vm)
                link(V.tensor_tensor(dm, m2, m1, ALU.subtract))
                dve.sem_inc(s["rt_exp_in"], 1)
                link(V.tensor_tensor(mask, oh1, oh2, ALU.add))
                dve.sem_inc(s["mask_ready"], 1)
                dve.wait_ge(s["rt_exp_out"], 2 * layer + 2)
                link(V.tensor_reduce(gsum, ex, AX, ALU.add))
                link(V.reciprocal(gp, gsum))
                link(V.tensor_scalar(w1, e2, 1.0, None, ALU.add))
                link(V.reciprocal(w1, w1))
                link(V.tensor_tensor(w1, w1, gp, ALU.mult))
                link(V.tensor_tensor(w2_, w1, e2, ALU.mult))
                dve.wait_ge(s["pos_mm"], layer + 1)
                for i, n in enumerate(TOK):
                    did(V.tensor_tensor(posE[0:n, i, :], ps[0:n, 0, i * 16:(i + 1) * 16], cE[0:n, :], ALU.add))
                did(V.tensor_copy(JT[0:1, 7, 0:16], ps[0:1, 0, 48:64]))
                settle()
                ent = ENT[:].rearrange("p (i r w) -> p i r w", i=3, r=2)
                if layer:
                    dve.wait_ge(s["tbl_scat"], 96)
                for r, (oh, w) in enumerate(((oh1, w1), (oh2, w2_))):
                    link(V.tensor_tensor(pr, oh, posE, ALU.mult))
                    link(V.tensor_reduce(dm, pr, AX, ALU.add))
                    did(V.tensor_copy(SLOT[:, 3 * r:3 * r + 3], dm))
                    did(V.tensor_copy(ent[:, :, r, 2].bitcast(F32), w))
                    settle()
                dve.sem_inc(s["ent_ready"], 1)
                cnt = JT[0:1, 7, 0:16]
                J = [JT[0:1, i, 0:16] for i in range(3)]
                link(V.tensor_scalar(J[0], cnt, float(C), None, ALU.is_gt))
                for n in range(2, 5):
                    link(V.scalar_tensor_tensor(J[0], cnt, float(n * C), J[0], ALU.is_gt, ALU.add))
                link(V.tensor_tensor_scan(J[1], ones[0:1, 0:16], J[0], 0.0, ALU.mult, ALU.add))
                link(V.tensor_tensor(J[2], J[1], J[0], ALU.subtract))
                sh = [1, JMAX, 16]

                def je(i):
                    return JT[0:1, i, :].rearrange("p (j e) -> p j e", j=JMAX)

                jj = bc(c8[0:1, :], 2, sh)
                link(V.tensor_tensor(je(3), bc(J[2], 1, sh), jj, ALU.is_le))
                link(V.tensor_tensor(je(4), bc(J[1], 1, sh), jj, ALU.is_gt))
                link(V.tensor_tensor(je(3), je(3), je(4), ALU.mult))
                link(V.tensor_tensor(je(4), je(3), bc(c15[0:1, :], 1, sh), ALU.mult))
                link(V.tensor_reduce(JT[0:1, 6, 0:8], je(4), AX, ALU.add))
                link(V.scalar_tensor_tensor(J[2], J[2], -float(C), cE[0:1, :], ALU.mult, ALU.add))
                link(V.scalar_tensor_tensor(je(5), jj, float(C), bc(J[2], 1, sh), ALU.mult, ALU.add))
                link(V.scalar_tensor_tensor(je(5), je(5), float(C), je(3), ALU.add, ALU.mult))
                link(V.tensor_reduce(JT[0:1, 6, 8:16], je(5), AX, ALU.add))
                did(V.tensor_copy(JI[layer][0:1, 0:16], JT[0:1, 6, 0:16]))
                did(V.tensor_copy(JI[layer][0:1, 16:17], J[1][:, 15:16]))
                settle()
                dve.sem_inc(s["jobs_ready"], 1)

                def rows():
                    return V.tensor_copy(xselT[:, 0:4 * C], ps[:, 0, :])

                def hidden(b):
                    return V.tensor_tensor(hid, hsil, ps[:, 2 + b, FH:2 * FH], ALU.mult)

                def hidden_turned(b):
                    return V.tensor_copy(hidT, ps[:, 2 + b, 0:2 * C])

                def weighted(b, e):
                    return V.tensor_scalar(ysel[e][:, 512:D], ps[:, 5 + 2 * b, :],
                                           IDX[e][:, 2:3].bitcast(F32), None, ALU.mult)

                if layer == 0:
                    parts(4)

                def step_t(e, n):
                    dve.wait_ge(s["xt_mm"], n + 1)
                    rows().then_inc(s["xt_ready"], 1)

                def step_u(e, n):
                    dve.wait_ge(s["silu_done"], n + 1)
                    hidden(e % 2).then_inc(s["hid_ready"], 1)

                def step_h(e, n):
                    dve.wait_ge(s["ht2_mm"], n + 1)
                    hidden_turned(e % 2).then_inc(s["ht2_ready"], 1)

                def step_d(e, n):
                    dve.wait_ge(s["dn_mm"], n + 1)
                    dve.wait_ge(s["y_free"], n + 1)
                    weighted(e % 2, e % NSLOT).then_inc(s["y_dve"], 1)

                n0 = layer * NE
                step_t(0, n0)
                step_u(0, n0)
                step_t(1, n0 + 1)
                step_h(0, n0)
                with dve.Fori(0, NE // NSLOT - 1) as i:
                    for e in range(1, 1 + NSLOT):
                        n = i * NSLOT + (e + n0)
                        step_u(e, n)
                        step_t(e + 1, n + 1)
                        step_d(e - 1, n - 1)
                        step_h(e, n)
                for e in range(NE - NSLOT + 1, NE):
                    step_u(e, n0 + e)
                    if e + 1 < NE:
                        step_t(e + 1, n0 + e + 1)
                    step_d(e - 1, n0 + e - 1)
                    step_h(e, n0 + e)
                step_d(NE - 1, n0 + NE - 1)
                nj, base = further(dve, layer)
                with dve.If(nj > 0):
                    with dve.Fori(0, nj) as j:
                        n1 = base + j + 1
                        dve.wait_ge(s["o_xt_mm"], n1)
                        rows().then_inc(s["o_xt"], 1)
                        dve.wait_ge(s["o_silu"], n1)
                        hidden(0).then_inc(s["o_hid"], 1)
                        dve.wait_ge(s["o_ht_mm"], n1)
                        hidden_turned(0).then_inc(s["o_ht"], 1)
                        dve.wait_ge(s["o_dn"], n1 + AHEAD)
                        dve.wait_ge(s["o_free"], base + j + AHEAD)
                        weighted(0, 0).then_inc(s["o_ydve"], 1)
                scaled_x(2 * layer + 1)
                dve.wait_ge(s["z_in"], 48 * (layer + 1))
                did(V.tensor_tensor(zin[:, 0:2, 0, :], zin[:, 0:2, 0, :], zin[:, 0:2, 1, :], ALU.add))
                did(V.tensor_tensor(zin[0:TS, 2, 0, :], zin[0:TS, 2, 0, :], zin[0:TS, 2, 1, :], ALU.add))
                settle()
                dve.sem_inc(s["zsum"], 1)

            did(V.memset(arow, 0.0))
            settle()
            residual(0, 0, 2, s["tile_done"], s["tile_free"], 24)
            layer_norm(0)
            moe(0)
            residual(1, 0, 5, s["zt_mm"], s["zt_free"], 0)
            parts(5)
            dve.wait_ge(s["mod_ready"], ADA_SLOTS)
            one_more((1, 4))
            layer_norm(1)

            V.tensor_copy(act_flat(2), act_flat(A_X)).then_inc(s["xcopy"], 1)
            dve.wait_ge(s["f_mm"], 1)
            link(V.tensor_scalar(lft[0][0:80, :], ps[0:80, 7, 0:T], small[0:80, 0:1], None, ALU.add))
            dve.sem_inc(s["f_neg"], 1)
            dve.wait_ge(s["f_act"], 1)
            link(V.scalar_tensor_tensor(lfo[0:80, :], lft[0][0:80, :], 0.0, lft[1][0:80, :], ALU.min, ALU.subtract))
            dve.sem_inc(s["f_scan"], 1)
            for a, b in ((0, P), (P, TP), (TP, T)):
                init = lft[2][0:80, P - 1:P] if a == P else 0.0
                link(V.tensor_tensor_scan(lft[2][0:80, a:b], ones[0:80, 0:b - a], lfo[0:80, a:b], init,
                                          ALU.mult, ALU.add))
            link(V.tensor_scalar(nF[0:80, :], lft[2][0:80, :], -1.0, None, ALU.mult))
            for a in range(0, PAST, P):
                init = nFS[0:16, a - 1:a] if a else 0.0
                link(V.tensor_tensor_scan(nFS[0:16, a:a + P], ones[0:16, 0:P], clf[0:16, a:a + P], init,
                                          ALU.mult, ALU.add))
            link(V.tensor_tensor(nFS[0:16, 0:PAST], nFS[0:16, 0:PAST], clf[0:16, :], ALU.subtract))
            did(V.tensor_copy(nFS[0:16, PAST:NKEY], nF[0:16, TP:T]))
            for qz in QZ:
                did(V.memset(qz, 0.0))
            settle()
            dve.sem_inc(s["nf_ready"], 1)
            dve.wait_ge(s["tile_free"], 56)
            with dve.Fori(0, NGRP // 2) as pair:
                ch.enter(pair, 2 * ATTN_LINKS)
                for half in range(2):
                    g = pair * 2 + half
                    qs, ks, vs, qz = QS[half], KS[half], VS[half], QZ[half]
                    did(V.tensor_scalar(qs, arena[:, bass.ds(g * GC + A_Q * ACOL, GC)], HD ** -0.5, None, ALU.mult))
                    did(V.tensor_copy(ks, arena[:, bass.ds(g * GC + A_KO * ACOL, GC)]))
                    did(V.tensor_copy(vs, arena[:, bass.ds(g * GC + A_VO * ACOL, GC)]))
                    settle()
                    dve.sem_inc(s["stage"], 1)
                    for t in range(2):
                        for p in range(2):
                            r = slice(64 * p, 64 * p + 64)
                            did(V.tensor_copy(qz[r, (2 * t + p) * TS:(2 * t + p + 1) * TS],
                                              qs[r, t * T + TP:(t + 1) * T]))
                    settle()
                    dve.sem_inc(s["qz_ready"], 1)

                    def top(h):
                        dve.wait_ge(s["sc_mm"], g * 4 + h + 1)
                        b = h % 2
                        for qt in range(2):
                            did(V.tensor_reduce(sm[:, 2 * b + qt:2 * b + qt + 1],
                                                ps[:, b, P * qt:P * qt + P * (qt + 1)], AX, ALU.max, negate=True))
                        settle()
                        dve.sem_inc(s["sc_max"], 1)

                    def norm(h):
                        dve.wait_ge(s["sc_exp"], g * 4 + h + 1)
                        b = h % 2
                        link(V.reciprocal(sm[:, 8 + 2 * b:10 + 2 * b], sm[:, 4 + 2 * b:6 + 2 * b]))
                        for qt in range(2):
                            x = Pp[b][:, P * qt:P * qt + P * (qt + 1)]
                            did(V.tensor_scalar(x, x, sm[:, 8 + 2 * b + qt:9 + 2 * b + qt], None, ALU.mult))
                        settle()
                        dve.sem_inc(s["sc_norm"], 1)

                    top(0)
                    dve.wait_ge(s["ss_mm"], g + 1)
                    link(V.tensor_reduce(sm[:, 12:13], ps2[:, 4 * 512:4 * 512 + NKEY], AX, ALU.max, negate=True))
                    dve.sem_inc(s["ss_max"], 1)
                    top(1)
                    norm(0)
                    norm(1)
                    dve.wait_ge(s["ss_exp"], g + 1)
                    link(V.reciprocal(sm[:, 14:15], sm[:, 13:14]))
                    link(V.tensor_scalar(Ps, Ps, sm[:, 14:15], None, ALU.mult))
                    dve.sem_inc(s["ss_norm"], 1)
                    top(2)
                    norm(2)
                    top(3)
                    norm(3)
                ch.leave(NGRP // 2)

            residual(2, 1, 2, s["tile_done"], s["tile_free"], 56)
            layer_norm(2)
            moe(1)
            residual(3, 1, 5, s["zt_mm"], s["zt_free"], KT)
            layer_norm(3)

        @block.scalar
        def _(act):
            Ac = nc.scalar.activation
            ch = Chain(act, s["act_ch"])
            did, settle, link = ch.did, ch.settle, ch.link

            act.wait_ge(s["consts_in"], 32)
            Ac(csig[:], vec[:, VEC_C:VEC_C + 2 * KT], ACT.Sigmoid).then_inc(s["csig_done"], 1)
            act.wait_ge(s["csil_ready"], 2)

            def rows_of(turn):
                if turn:
                    act.wait_ge(s["ada_t"], turn + AHEAD)
                act.wait_ge(s["ada_done"], (turn + 1) * ADA_TURN)
                for j in range(ADA_TURN):
                    last = Ac(arow[32 * j:32 * j + 2], ps[32 * j:32 * j + 2, 4 + turn % 2, :], ACT.Copy)
                last.then_inc(s["ada_rows"], 1)

            rows_of(0)
            act.wait_ge(s["h_ready"], 1)
            link(Ac(shrow[:].rearrange("p (k s) -> p k s", s=2), Hh[:, :, TP - 1:T:TS], ACT.Copy))
            act.dma_start(O["shift"], shrow[:]).then_inc(s["shift_out"], 16)

            def empty(mi, dst, turn=0):
                for k in range(KT):
                    act.wait_ge(s["tile_done"], mi * 8 + k + 1)
                    Ac(dst(k), ps[:, k % 4, 0:T], ACT.Copy).then_inc(s["tile_free"], 1)
                    if turn and k % 4 == 3 and turn + k // 4 < EARLY_TURNS:
                        rows_of(turn + k // 4)

            for i in range(3):
                empty(i, lambda k: acts(A_R + i)[:, k, :], turn=2 * i + 1)
            for n, (f, rows) in enumerate(((ACT.Tanh, 64), (ACT.Copy, 64), (ACT.Sigmoid, P))):
                act.wait_ge(s["lora1_done"], n + 1)
                Ac(lh[0:rows, n, :], ps[0:rows, 4 + n, 0:T], f).then_inc(s["lora1_act"], 1)
            for n, dst in enumerate((A_LD, A_A, A_G)):
                for k in range(KT):
                    c = n * KT + k
                    act.wait_ge(s["lora2_done"], c + 1)
                    out, in_ = acts(dst)[:, k, :], ps[:, 4 + c % 3, 0:T]
                    if n < 2:
                        ins = Ac(out, in_, ACT.Sigmoid, bias=v(("w0", "a0")[n], k))
                    else:
                        ins = Ac(out, in_, ACT.Copy)
                    ins.then_inc(s["lora2_act"], 1)
                if n == 1:
                    act.wait_ge(s["norm_inv"], 1)
                    Ac(rn[:], rn[:], ACT.Sqrt).then_inc(s["norm_root"], 1)
                    act.wait_ge(s["lora2_act"], 16)
                    for k in range(KT):
                        last = Ac(acts(A_Y)[:, k, :], acts(A_A)[:, k, :], ACT.Identity, scale=v("k_a", k),
                                  bias=omka[:, k:k + 1])
                    last.then_inc(s["ka_ready"], 1)

            act.wait_ge(s["pre_ready"], 1)
            with act.Fori(0, NGRP) as g:
                for p in range(2):
                    act.wait_ge(set_v[p], g * SETJ.count["V"] + AHEAD)
                    act.wait_ge(set_done[p], g * len(SET_JOBS) + AHEAD)
                act.wait_ge(s["sam_v"], g * SAMJ.count["V"] + AHEAD)
                act.wait_ge(s["sam_done"], g * len(SAM_JOBS) + AHEAD)
                cum = arena[:, bass.ds(g * GC + A_CUM * ACOL, GC)]
                Ac(ex1, cum, ACT.Exp, scale=DECAY).then_inc(s["scaled_exp"], 1)
                Ac(qx, arena[:, bass.ds(g * GC + A_LD * ACOL, GC)], ACT.Exp, scale=-DECAY).then_inc(s["scaled_exp"], 1)
                Ac(eg, cum, ACT.Exp, scale=-DECAY).then_inc(s["scaled_exp"], 1)
                for n, (dst, sg) in enumerate(((Vt, 1.0), (Bt, -1.0), (Kt, 1.0))):
                    act.wait_ge(s["t_mm"], g * 3 + n + 1)
                    last = Ac(dst, ps[:, n, :], ACT.Copy, scale=sg)
                last.then_inc(s["t_copy"], 1)
                act.wait_ge(s["sm_t_mm"], g + 1)
                Ac(VtS[0:TS], ps[0:TS, 6, 0:256], ACT.Copy)
                Ac(BtS[0:TS], ps[0:TS, 6, 256:512], ACT.Copy, scale=-1.0)
                Ac(KtS[0:TS], ps[0:TS, 7, 0:256], ACT.Copy).then_inc(s["t_copy"], 1)

                def set_evac(p, name):
                    n = SETJ.at[name]
                    bank = 3 * p + n % 3
                    B = SU[p]
                    act.wait_ge(set_done[p], g * len(SET_JOBS) + n + 1 + AHEAD)
                    rows = slice(64 * p, 64 * p + 64)
                    if name == "D2":
                        act.wait_ge(s["d_ready"], g * 4 + p + 3)
                    if name[0] in "DP":
                        dst, src = B["DT" if name.endswith("T") else "D"], ps[:, bank, :]
                    elif name[0] == "X":
                        dst, src = B["XT"], ps[:, bank, :]
                    elif name[0] in "WU":
                        o = 128 * (name[0] == "U")
                        dst, src = WU[p][:, o:o + 128], ps[:, bank, 0:128]
                    else:
                        c = "AB".index(name[1])
                        for t in range(2):
                            last = Ac(arena[rows, bass.ds(g * GC + (A_Y * ACOL + t * T + c * P), P)],
                                      ps[rows, bank, t * P:(t + 1) * P], ACT.Copy)
                        last.then_inc(set_a[p], 1)
                        return
                    Ac(dst, src, ACT.Copy).then_inc(set_a[p], 1)

                def sam_evac(name):
                    act.wait_ge(s["sam_done"], g * len(SAM_JOBS) + SAMJ.at[name] + 1 + AHEAD)
                    if name[0] == "D":
                        last = Ac(SS_D, ps[0:TS, 6, 0:256], ACT.Copy)
                    elif name == "P16":
                        last = Ac(SS["D"][0:TS], ps[0:TS, 6, 0:128], ACT.Copy)
                    elif name == "W":
                        for p in range(2):
                            last = Ac(WUS[0:TS, 128 * p:128 * (p + 1)], ps[0:TS, 6 + p, 0:128], ACT.Copy)
                    else:
                        last = Ac(WUS[0:TS, 256:512], ps[0:TS, 6, 0:256], ACT.Copy)
                    last.then_inc(s["sam_a"], 1)

                for i, stage in enumerate(SET_STAGES):
                    for p in range(2):
                        for name in stage:
                            if SETJ.who[name] == "A":
                                set_evac(p, name)
                    if SAMJ.who.get(SAM_AFTER.get(i)) == "A":
                        sam_evac(SAM_AFTER[i])

            act.wait_ge(s["gn_cent"], KT)
            Ac(act_flat(A_A), act_flat(A_Y), ACT.Square).then_inc(s["gn_sq"], 1)
            for k in range(KT):
                act.wait_ge(s["gn_var"], k + 1)
                r = acts(A_XX)[:, k, :]
                Ac(r, ps[:, k % 4, 0:T], ACT.Ln, bias=eps_gn).then_inc(s["gn_rstd"], 1)
            act.wait_ge(s["gn_rstd"], KT)
            for k in range(KT):
                r = acts(A_XX)[:, k, :]
                Ac(r, r, ACT.Exp, scale=-0.5).then_inc(s["gn_rstd"], 1)

            def layer_norm(n):
                for k in range(KT):
                    act.wait_ge(s["ln_cent"], KT * n + k + 1)
                    Ac(acts(SQB[n])[:, k, :], acts(ZB[n])[:, k, :], ACT.Square).then_inc(s["ln_sq"], 1)
                act.wait_ge(s["ln_var"], n + 1)
                r = acts(SQB[n])[:, 0, :]
                link(Ac(r, ps[:, 5, 0:T], ACT.Ln, bias=eps_ln))
                Ac(r, r, ACT.Exp, scale=-0.5).then_inc(s["ln_rstd"], 1)

            def modulate(n, layer, comp):
                for k in range(KT):
                    act.wait_ge(s["x_ready"], KT * n + k + 1)
                    for st, (a, b) in enumerate(STREAMS):
                        last = Ac(Hh[:, k, a:b], X[:, k, a:b], ACT.Identity, scale=m(layer, comp + 1, k, st),
                                  bias=m(layer, comp, k, st))
                    last.then_inc(s["h_ready"], 1)

            def moe(layer):
                act.wait_ge(s["lg_mm"], layer + 1)
                act.wait_ge(s["small_in"], 16)
                Ac(lgf, ps[0:20, 0, 0:T], ACT.Identity, bias=small[0:20, 1 + layer:2 + layer])\
                    .then_inc(s["lg_act"], 1)
                for i, n in enumerate(TOK):
                    for hf in range(2):
                        act.wait_ge(s["ht_mm"], layer * 6 + 2 * i + hf + 1)
                        Ac(htok[0:n, i, hf * 512:(hf + 1) * 512], ps[0:n, 2 + 2 * i + hf, :], ACT.Copy)\
                            .then_inc(s["ht_evac"], 1)
                act.wait_ge(s["ht_evac"], 6 * (layer + 1))
                for i, n in enumerate(TOK):
                    act.dma_start(hbuf[layer][i * P:i * P + n, :], htok[0:n, i, :]).then_inc(s["hbuf_out"], 16)
                act.wait_ge(s["rt_exp_in"], 2 * layer + 1)
                ex = RT[:, 2, 0:12]
                Ac(ex, ex, ACT.Exp).then_inc(s["rt_exp_out"], 1)
                act.wait_ge(s["rt_exp_in"], 2 * layer + 2)
                Ac(RT[:, 15, 21:24], RT[:, 15, 18:21], ACT.Exp).then_inc(s["rt_exp_out"], 1)

                def rows():
                    return Ac(xselT[:, 4 * C:8 * C], ps[:, 1, :], ACT.Copy)

                def silu(b):
                    return Ac(hsil, ps[:, 2 + b, 0:FH], ACT.Silu)

                def weighted(b, e):
                    return Ac(ysel[e][:, 0:512], ps[:, 4 + 2 * b, :], ACT.Copy,
                              scale=IDX[e][:, 2:3].bitcast(F32))

                def step_t(e, n):
                    act.wait_ge(s["xt_mm"], n + 1)
                    rows().then_inc(s["xt_act"], 1)

                def step_u(e, n):
                    act.wait_ge(s["gu_mm"], n + 1)
                    silu(e % 2).then_inc(s["silu_done"], 1)

                def step_d(e, n):
                    act.wait_ge(s["dn_mm"], n + 1)
                    act.wait_ge(s["y_free"], n + 1)
                    weighted(e % 2, e % NSLOT).then_inc(s["y_act"], 1)

                n0 = layer * NE
                step_t(0, n0)
                step_u(0, n0)
                step_t(1, n0 + 1)
                with act.Fori(0, NE // NSLOT - 1) as i:
                    for e in range(1, 1 + NSLOT):
                        n = i * NSLOT + (e + n0)
                        step_u(e, n)
                        step_t(e + 1, n + 1)
                        step_d(e - 1, n - 1)
                for e in range(NE - NSLOT + 1, NE):
                    step_u(e, n0 + e)
                    if e + 1 < NE:
                        step_t(e + 1, n0 + e + 1)
                    step_d(e - 1, n0 + e - 1)
                step_d(NE - 1, n0 + NE - 1)
                act.wait_ge(s["jobs_ready"], layer + 1)
                nj, base = further(act, layer)
                with act.If(nj > 0):
                    with act.Fori(0, nj) as j:
                        n1 = base + j + 1
                        act.wait_ge(s["o_xt_mm"], n1)
                        rows().then_inc(s["o_xta"], 1)
                        act.wait_ge(s["o_gu"], n1)
                        silu(0).then_inc(s["o_silu"], 1)
                        act.wait_ge(s["o_dn"], n1 + AHEAD)
                        act.wait_ge(s["o_free"], base + j + AHEAD)
                        weighted(0, 0).then_inc(s["o_yact"], 1)
                if layer == 0:
                    rows_of(5)

            layer_norm(0)
            modulate(0, 0, 3)
            rows_of(4)
            moe(0)
            layer_norm(1)
            modulate(1, 1, 0)
            act.wait_ge(s["f_neg"], 1)
            link(Ac(lft[1][0:80, :], lft[0][0:80, :], ACT.Abs))
            link(Ac(lft[1][0:80, :], lft[1][0:80, :], ACT.Exp, scale=-1.0))
            Ac(lft[1][0:80, :], lft[1][0:80, :], ACT.Ln, bias=ones[0:80, 0:1]).then_inc(s["f_act"], 1)
            with act.Fori(0, 3) as i:
                empty(i + 4, lambda k: arena[:, bass.ds(i * ACOL + (A_R * ACOL + k * T), T)])
            act.wait_ge(s["tile_free"], 56)
            act.wait_ge(s["f_scan"], 1)
            act.dma_start(O["k"], act_flat(A_KO)).then_inc(s["kv_out"], 16)
            act.dma_start(O["v"], act_flat(A_VO)).then_inc(s["kv_out"], 16)
            act.dma_start(O["logf"], lfo[0:16, :]).then_inc(s["kv_out"], 16)
            with act.Fori(0, NGRP // 2) as pair:
                for half in range(2):
                    g = pair * 2 + half
                    act.wait_ge(s["vt_mm"], g + 1)
                    Ac(vt, ps[:, 2, :], ACT.Copy)
                    Ac(vtS[0:TS], ps[0:TS, 3, 0:256], ACT.Copy).then_inc(s["vt_ready"], 1)

                    def exps(h):
                        b = h % 2
                        if h >= 2:
                            act.wait_ge(s["pt_mm"], g * 4 + (h - 1) + AHEAD)
                        else:
                            act.wait_ge(s["pt_mm"], g * 4 + AHEAD)
                        act.wait_ge(s["sc_max"], g * 4 + h + 1)
                        for qt in range(2):
                            a, w = P * qt, P * (qt + 1)
                            last = Ac(Pp[b][:, a:a + w], ps[:, b, a:a + w], ACT.Exp,
                                      bias=sm[:, 2 * b + qt:2 * b + qt + 1],
                                      accum_out=sm[:, 4 + 2 * b + qt:5 + 2 * b + qt])
                        last.then_inc(s["sc_exp"], 1)

                    def outs(h):
                        act.wait_ge(s["pt_mm"], g * 4 + h + 1 + AHEAD)
                        if h >= 2:
                            act.wait_ge(s["pv_mm"], g * 4 + h - 1 + AHEAD)
                        Ac(PT[h % 2], ps[:, 2, 0:384], ACT.Copy).then_inc(s["pt_copy"], 1)
                        if h % 2:
                            act.wait_ge(s["pv_mm"], g * 4 + h + 1 + AHEAD)
                            Ac(arena[:, bass.ds(g * GC + (A_O * ACOL + h // 2 * T), TP)], ps[:, 3, 0:TP], ACT.Copy)\
                                .then_inc(s["pv_copy"], 1)

                    exps(0)
                    act.wait_ge(s["ss_max"], g + 1)
                    act.wait_ge(s["st2_mm"], g + AHEAD)
                    Ac(Ps, ps2[:, 4 * 512:4 * 512 + NKEY], ACT.Exp, bias=sm[:, 12:13], accum_out=sm[:, 13:14])\
                        .then_inc(s["ss_exp"], 1)
                    exps(1)
                    outs(0)
                    exps(2)
                    outs(1)
                    exps(3)
                    act.wait_ge(s["st2_mm"], g + 1 + AHEAD)
                    Ac(PsT, ps[:, 6, :], ACT.Copy)
                    Ac(PsT5[0:TS], ps[0:TS, 7, 0:P], ACT.Copy).then_inc(s["st2_copy"], 1)
                    outs(2)
                    outs(3)
                    act.wait_ge(s["sv_mm"], g + 1 + AHEAD)
                    for t in range(2):
                        last = Ac(arena[:, bass.ds(g * GC + (A_O * ACOL + t * T + TP), TS)],
                                  ps[:, 7, 128 + t * TS:128 + (t + 1) * TS], ACT.Copy)
                    last.then_inc(s["sv_copy"], 1)
            act.wait_ge(s["kv_out"], 48)
            layer_norm(2)
            modulate(2, 1, 3)
            moe(1)
            layer_norm(3)

        @block.gpsimd
        def _(pool):
            Pl = nc.gpsimd
            for n in ONE_AHEAD:
                pool.sem_inc(s[n], AHEAD)
            Pl.dma_start(ENT[:], I["ent"]).then_inc(s["tbl_fill"], 16)
            for layer in range(2):
                Pl.dma_start(tbl[layer], I["tbl0"]).then_inc(s["tbl_fill"], 16)
            pool.wait_ge(s["pre_ready"], 1)
            with pool.Fori(0, NGRP) as g:
                pool.wait_ge(s["sam_done"], g * len(SAM_JOBS) + AHEAD)
                pool.wait_ge(s["sam_v"], g * SAMJ.count["V"] + AHEAD)
                constant(pool)
                Pl.dma_start(stS, I["state"][bass.ds(g, 1)].rearrange("a p n -> p (a n)")).then_inc(s["st_in"], 16)
                for p in range(2):
                    pool.wait_ge(set_v[p], (g + 1) * SETJ.count["V"] + AHEAD)
                constant(pool)
                Pl.dma_start(O["pwkv"][bass.ds(g, 1)].rearrange("a p n -> p (a n)"), stB).then_inc(s["st_out"], 16)
                pool.wait_ge(s["sam_v"], (g + 1) * SAMJ.count["V"] + AHEAD)
                constant(pool)
                Pl.dma_start(O["swkv"][bass.ds(g, 1)].rearrange("a p n -> p (a n)"), stSo).then_inc(s["st_out"], 16)
                pool.wait_ge(s["st_out"], g * 32 + 32)
                pool.sem_inc(s["st_free"], 1)

            def moe(layer):
                pool.wait_ge(s["tbl_fill"], 48)
                pool.wait_ge(s["ent_ready"], layer + 1)
                for r in range(2):
                    for i, n in enumerate(TOK):
                        Pl.indirect_dma_start(out=tbl[layer],
                                              out_offset=bass.IndirectOffsetOnAxis(
                                                  ap=SLOT[0:n, 3 * r + i:3 * r + i + 1], axis=0),
                                              in_=ENT[0:n, (2 * i + r) * 4:(2 * i + r + 1) * 4], in_offset=None,
                                              bounds_check=NE * TROWS - 1, oob_is_err=False)\
                            .then_inc(s["tbl_scat"], 16)
                pool.wait_ge(s["tbl_scat"], 96 * (layer + 1))
                Pl.dma_start(TBL[:].rearrange("s (e w) -> s e w", e=NE),
                             tbl[layer].rearrange("(e s) w -> s e w", e=NE)[0:C]).then_inc(s["tbl_in"], 16)
                pool.wait_ge(s["tbl_in"], 16 * (layer + 1))
                pool.wait_ge(s["hbuf_out"], 48 * (layer + 1))
                if layer == 0:
                    pool.wait_ge(s["ada_done"], 5 * ADA_TURN)

                def gather(b, idx, done):
                    Pl.indirect_dma_start(out=xsel[b], out_offset=None, in_=hbuf[layer],
                                          in_offset=bass.IndirectOffsetOnAxis(ap=idx[:, 0:1], axis=0),
                                          bounds_check=T - 1, oob_is_err=False).then_inc(done, 16)

                def scatter(b, done):
                    Pl.indirect_dma_start(out=zbuf[layer],
                                          out_offset=bass.IndirectOffsetOnAxis(ap=IDX[b][:, 1:2], axis=0),
                                          in_=ysel[b], in_offset=None,
                                          bounds_check=2 * T - 1, oob_is_err=False).then_inc(done, 16)

                def entries(col, e):
                    constant(pool)
                    Pl.tensor_copy(IDX[e % NSLOT][:], TBL[:, col]).then_inc(s["y_free"], 1)

                def fetch(col, e, n):
                    b = e % NSLOT
                    constant(pool)
                    Pl.tensor_copy(IDXG[b][:], TBL[:, col]).then_inc(s["idx_ready"], 1)
                    pool.wait_ge(s["idx_ready"], n + 1)
                    constant(pool)
                    gather(b, IDXG[b], s[f"gath{b}"])

                def refetch(col, e, n):
                    pool.wait_ge(s["xt_mm"], n - NSLOT + 1)
                    fetch(col, e, n)

                def send(e, n):
                    pool.wait_ge(s["y_act"], n + 1 + AHEAD)
                    pool.wait_ge(s["y_dve"], n + 1 + AHEAD)
                    if e:
                        pool.wait_ge(s["z_scat"], n * 16)
                    constant(pool)
                    scatter(e % NSLOT, s["z_scat"])

                n0 = layer * NE
                for e in range(NSLOT):
                    fetch(slice(4 * e, 4 * e + 1), e, n0 + e)
                for e in range(NSLOT):
                    entries(slice(4 * e, 4 * e + 4), e)
                for e in range(NSLOT, NSLOT + 2):
                    refetch(slice(4 * e, 4 * e + 1), e, n0 + e)
                send(0, n0)
                with pool.Fori(0, NE // NSLOT - 2) as i:
                    for e in range(1, 1 + NSLOT):
                        n = i * NSLOT + (e + n0)
                        refetch(bass.ds(i * (4 * NSLOT) + 4 * (e + 5), 1), e + 5, n + 5)
                        send(e, n)
                        entries(bass.ds(i * (4 * NSLOT) + 4 * (e + 3), 4), e + 3)
                for e in range(NE - 2 * NSLOT + 1, NE):
                    if e + 5 < NE:
                        refetch(slice(4 * (e + 5), 4 * (e + 5) + 1), e + 5, n0 + e + 5)
                    send(e, n0 + e)
                    if e + 3 < NE:
                        entries(slice(4 * (e + 3), 4 * (e + 3) + 4), e + 3)
                pool.wait_ge(s["z_scat"], 16 * (n0 + NE))
                pool.wait_ge(s["jobs_ready"], layer + 1)
                nj, base = further(pool, layer)
                with pool.If(nj > 0):
                    with pool.Fori(0, nj) as j:
                        row = pool.value_load(JI[layer][0:1, bass.ds(j + 8, 1)], min_val=0,
                                              max_val=NE * TROWS - C)
                        Pl.dma_start(IDX[0][:], tbl[layer][bass.ds(row, C), :]).then_inc(s["oidx"], 16)
                        pool.wait_ge(s["oidx"], (base + j) * 16 + 16)
                        constant(pool)
                        gather(0, IDX[0], s["o_gath"])
                        pool.wait_ge(s["o_yact"], base + j + 1 + AHEAD)
                        pool.wait_ge(s["o_ydve"], base + j + 1 + AHEAD)
                        constant(pool)
                        scatter(0, s["o_scat"])
                        pool.wait_ge(s["o_scat"], (base + j) * 16 + 16)
                        pool.sem_inc(s["o_free"], 1)
                zr = zbuf[layer].rearrange("(r t) d -> t r d", r=2)
                for i, n in enumerate(TOK):
                    Pl.dma_start(zin[0:n, i, :, :], zr[i * P:i * P + n]).then_inc(s["z_in"], 16)

            moe(0)
            pool.wait_ge(s["x_ready"], 2 * KT)
            Pl.dma_start(fw, I["fw"]).then_inc(s["attn_small"], 16)
            Pl.dma_start(clf[0:16, :], I["clf"]).then_inc(s["attn_small"], 16)
            for g in range(NGRP):
                if g >= 2:
                    pool.wait_ge(s["sv_mm"], g - 1 + AHEAD)
                    pool.wait_ge(s["pv_mm"], (g - 1) * 4 + AHEAD)
                for dst, src in ((CK, "ck"), (CV, "cv"), (SELG, "sel")):
                    Pl.dma_start(dst[g % 2], I[src][g]).then_inc(s[f"g_in{g % 2}"], 16)
            moe(1)


def kernel(x_prompt, x_sample, state_shift, state_wkv, cache_k, cache_v, cache_logf, c_prompt,
           c_sample, ada_w, ada_b, ln_g, ln_b, a_mu, a_w_rkv, a_w0, a_w1, a_w2, a_a0, a_a1, a_a2,
           a_g1, a_g2, a_k_k, a_k_a, a_r_k, a_lnx_g, a_lnx_b, a_w_o, kv_w, f_w, f_b, b_wq, b_wo,
           rg_w, rg_b, re_w, re_b, exp_wg, exp_wu, exp_wd):
    import concourse.bacc as bacc
    from concourse.bass_utils import run_bass_kernel_spmd as run

    np_ = lambda a: np.asarray(a)

    def fm(a):
        a = np_(a).reshape(-1, D)
        return a.T.reshape(KT, P, -1).transpose(1, 0, 2)

    def halves(w):
        w = np_(w)
        return w.reshape(KT, P, -1, 512).transpose(2, 1, 0, 3).reshape(-1, P, WCOL)

    A = {}
    A["x"] = fm(np.concatenate([np_(x_prompt)[0], np_(x_sample)[0]])).reshape(P, ACOL)
    rows = [np_(a_mu)[0, i] for i in range(6)] + [np_(a)[0] for a in (a_w0, a_a0, a_k_k, a_k_a)]
    rows += [np_(a_r_k)[0].reshape(D), np_(a_lnx_g)[0], np_(a_lnx_b)[0]]
    rows += [np_(a)[l, i] for a in (ln_g, ln_b) for l in range(2) for i in range(2)]
    rows += [np_(state_shift)[0, 0]]
    cols = [fm(r).reshape(P, KT) for r in rows]
    cols.append(fm(np.stack([np_(c_prompt)[0], np_(c_sample)[0]])).reshape(P, 2 * KT))
    cols.append(np_(ada_b).reshape(96, P).T)
    A["vecs"] = np.concatenate(cols, 1)
    A["w"] = np.concatenate([halves(np_(ada_w)[0]), halves(np_(ada_w)[1])]
                            + [halves(np_(a_w_rkv)[0, i]) for i in range(3)] + [halves(np_(a_w_o)[0])]
                            + [halves(np_(kv_w)[:, 0:D]), halves(np_(b_wq)[0]), halves(np_(kv_w)[:, D:]),
                               halves(np_(b_wo)[0])])
    l1 = np.concatenate([np_(a_w1)[0], np_(a_a1)[0], np_(a_g1)[0]], 1)
    pad = lambda a: np.concatenate([a, np.zeros((P - a.shape[0],) + a.shape[1:], a.dtype)])
    A["lora"] = np.concatenate([l1.reshape(KT, P, 256).transpose(1, 0, 2).reshape(P, 2048),
                                pad(np_(a_w2)[0]), pad(np_(a_a2)[0]), np_(a_g2)[0]], 1)
    gu = np.concatenate([np_(exp_wg), np_(exp_wu)], 3).reshape(2 * NE, KT, P, 512).transpose(0, 2, 1, 3)
    dn = np_(exp_wd).reshape(2 * NE, 2, P, D).transpose(0, 2, 1, 3)
    A["experts"] = np.concatenate([gu.reshape(2 * NE, P, WCOL), dn.reshape(2 * NE, P, 2 * D)], 2)
    r = np.concatenate([np_(rg_w), np_(re_w)], 2)
    A["rw"] = r.reshape(2, KT, P, 20).transpose(0, 2, 1, 3).reshape(2, P, KT * 20)
    small = np.zeros((P, 8), np.float32)
    small[0:16, 0] = small[64:80, 0] = np_(f_b)
    for l in range(2):
        small[0:20, 1 + l] = np.concatenate([np_(rg_b)[l], np_(re_b)[l]])
    A["small"] = small
    fwp = np.zeros((KT, P, 80), np.float32)
    fwp[:, :, 0:16] = fwp[:, :, 64:80] = np_(f_w).reshape(KT, P, 16)
    A["fw"] = fwp.transpose(1, 0, 2).reshape(P, KT * 80)
    A["clf"] = np_(cache_logf)[0, ::-1].T
    ckr = np_(cache_k)[0, ::-1].reshape(PAST, NGRP, 2, P)
    A["ck"] = ckr.transpose(1, 3, 2, 0).reshape(NGRP, P, 2 * PAST)
    cvr = np_(cache_v)[0, ::-1].reshape(4, P, NGRP, 256)
    A["cv"] = cvr.transpose(2, 1, 0, 3).reshape(NGRP, P, 1024)
    st = np_(state_wkv)[0, 0].reshape(NGRP, 2, 2, HD, HD)
    A["state"] = st.transpose(0, 2, 4, 1, 3).reshape(NGRP, P, 128)

    i = np.arange(P)
    row, col = i[:, None], i[None, :]
    lo = (col < row).astype(np.float32)
    same = lambda n: (row // n == col // n)
    f = lambda a: a.astype(np.float32)
    hs = np.zeros((P, KT, 16), np.float32)
    for k in range(KT):
        hs[i, k, 2 * k + i // 64] = 1
    blocks = {"ident": f(row == col), "ones": np.ones((P, P)), "mean": np.full((P, P), 1.0 / D),
              "bones": f(same(64)), "bmean": f(same(64)) / HD, "up": f(col > row), "nupi": -f(col >= row),
              "upi": f(col >= row), "mD": -lo * same(16), "mDT": -f(col > row) * same(16),
              "m16": lo * same(32) * ~same(16), "m32": lo * same(64) * ~same(32), "m64": lo * ~same(64),
              "cmask": -BIG * f(col > row), "headsel": hs.reshape(P, P),
              "cmaskS": -BIG * f(col > row % TS)}
    con = np.zeros((P, NCONST), np.float32)
    for n, c in CONST.items():
        w = TS if n == "cmaskS" else P
        con[:, c:c + w] = blocks[n][:, 0:w]
    con[0:16, CO_HST:CO_HST + KT * P] = hs.transpose(2, 1, 0).reshape(16, KT * P)
    tail = [4 - np.arange(4), 16 - np.arange(16), np.arange(16) * TROWS, np.arange(16), np.arange(8),
            [LN_EPS, GN_EPS, 0, 0]]
    con[:, CO_SMALL:] = np.concatenate(tail)
    A["consts"] = con
    sel = np.zeros((NGRP, P, SELW), np.float32)
    for g in range(NGRP):
        for h in range(4):
            sel[g, 4 * g + h, h * P:(h + 1) * P] = 1
            sel[g, 64 + 4 * g + h, h * P:(h + 1) * P] = 1
            sel[g, 4 * g + h, 4 * P + TS * h:4 * P + TS * (h + 1)] = 1
    A["sel"] = sel
    ent = np.zeros((P, NTT, 2, 4), np.int32)
    tok = np.arange(NTT)[None, :] * P + i[:, None]
    for k in range(2):
        ent[:, :, k, 0] = tok
        ent[:, :, k, 1] = tok + k * T
    A["ent"] = ent.reshape(P, NTT * 8)
    t0 = np.zeros((NE * TROWS, 4), np.int32)
    t0[:, 0:2] = NO_ROW
    A["tbl0"] = t0

    nc = bacc.Bacc("TRN2", target_bir_lowering=False, num_devices=1)
    arrays, I = {}, {}
    for n, a in A.items():
        a = np.ascontiguousarray(a)
        if a.dtype == np.float64:
            a = a.astype(np.float32)
        arrays["in_" + n] = a
        I[n] = nc.dram_tensor("in_" + n, a.shape, mybir.dt.from_np(a.dtype), kind="ExternalInput").ap()
    outs = {"y": (P, ACOL), "shift": (P, 2 * KT), "pwkv": (NGRP, P, 128), "swkv": (NGRP, P, 128),
            "k": (P, ACOL), "v": (P, ACOL), "logf": (16, T)}
    O = {n: nc.dram_tensor("out_" + n, sh, F32, kind="ExternalOutput").ap() for n, sh in outs.items()}
    build(nc, I, O)
    r = run(nc, [arrays], core_ids=[0]).results[0]
    R = {n: np.asarray(r["out_" + n]) for n in outs}

    def tm(a):
        return a.reshape(P, KT, T).transpose(2, 1, 0).reshape(T, D)

    y, k, v = tm(R["y"]), tm(R["k"]), tm(R["v"])
    shift = R["shift"].reshape(P, KT, 2).transpose(2, 1, 0).reshape(2, 1, 1, D)
    wkv = lambda a: a.reshape(NGRP, 2, HD, 2, HD).transpose(0, 3, 1, 4, 2).reshape(1, 1, NH, HD, HD)
    lf = R["logf"].T
    h4 = lambda a: a.reshape(1, -1, NH, HD)
    return (y[None, 0:TP], y[None, TP:], shift[0], wkv(R["pwkv"]), h4(k[0:TP]), h4(v[0:TP]), lf[None, 0:TP],
            shift[1], wkv(R["swkv"]), h4(k[TP:]), h4(v[TP:]), lf[None, TP:])
```
